# Optimizing a Trainium2 kernel written in Bass

```python
import math
import jax
import jax.numpy as jnp
from jax import lax
import numpy as np

D_MODEL = 1024
BATCH = 1
SEQ = 256
DEPTH = 2

CTX_LEN = 256
GRID_W = 64
HEAD_DIM = 64
D_MIX = D_MODEL
SSD_WIDTH = 3 * D_MIX // 8
SSD_HEADS = SSD_WIDTH // HEAD_DIM
SSD_GROUPS = 2
SSD_STATE = 64
SSD_CHUNK = 128
HYENA_WIDTH = D_MIX // 4
HYENA_ORDER = 2
HYENA_BANDS = 16
HYENA_POS_DIM = 1 + 2 * HYENA_BANDS
HYENA_FILTER_HIDDEN = 64
MLSTM_WIDTH = D_MIX - SSD_WIDTH - HYENA_WIDTH
MLSTM_HEADS = MLSTM_WIDTH // HEAD_DIM
MLSTM_CHUNK = 128
SHORT_CONV = 3
N_GROUPS = 4
EXPERTS_PER_GROUP = 8
N_EXPERTS = N_GROUPS * EXPERTS_PER_GROUP
TOP_K_IN_GROUP = 2
EXPERT_HIDDEN = 256
N_MOD = 6
EPS = 1e-6
SSD_CONV_CH = SSD_WIDTH + 2 * SSD_GROUPS * SSD_STATE
IN_SIZES = (SSD_WIDTH, SSD_CONV_CH, 2 * SSD_HEADS, (HYENA_ORDER + 1) * HYENA_WIDTH,
            2 * MLSTM_WIDTH, MLSTM_WIDTH, MLSTM_WIDTH, 4 * MLSTM_HEADS)
IN_COLS = sum(IN_SIZES)

kernel_name = 'hybrid_ssd_hyena_mlstm_hmoe_dit'

def split_sizes(u, sizes):
    cuts, s = [], 0
    for n in sizes[:-1]:
        s += n
        cuts.append(s)
    return jnp.split(u, cuts, axis=-1)

def rmsnorm(x, w):
    xf = x.astype(jnp.float32)
    y = xf * lax.rsqrt(jnp.mean(xf * xf, axis=-1, keepdims=True) + EPS)
    return (y * w.astype(jnp.float32)).astype(x.dtype)

def modulated_norm(x, w, shift, scale):
    return rmsnorm(x, w) * (1 + scale[:, None, :]) + shift[:, None, :]

def short_conv(x, w, b):
    L = x.shape[1]
    pad = w.shape[0] // 2
    xp = jnp.pad(x, ((0, 0), (pad, pad), (0, 0)))
    return sum(xp[:, k:k + L] * w[k] for k in range(w.shape[0])) + b

def flip(t):
    return t[:, ::-1]

def to_col_major(u):
    b, L, ch = u.shape
    rows = L // GRID_W
    return u.reshape(b, rows, GRID_W, ch).transpose(0, 2, 1, 3).reshape(b, L, ch)

def to_row_major(u):
    b, L, ch = u.shape
    rows = L // GRID_W
    return u.reshape(b, GRID_W, rows, ch).transpose(0, 2, 1, 3).reshape(b, L, ch)

def zero_states(b):
    f32 = jnp.float32
    ssd0 = jnp.zeros((b, SSD_HEADS, HEAD_DIM, SSD_STATE), f32)
    ml0 = (jnp.zeros((b, MLSTM_HEADS, HEAD_DIM, HEAD_DIM), f32),
           jnp.zeros((b, MLSTM_HEADS, HEAD_DIM), f32),
           jnp.zeros((b, MLSTM_HEADS), f32))
    return (ssd0, ssd0), (ml0, ml0)

def ssd_scan(xh, dt, a, bh, ch, init, want_y):
    b, L, h, pd = xh.shape
    n = bh.shape[-1]
    q = SSD_CHUNK
    nc = L // q
    cum = jnp.cumsum((dt * a).reshape(b, nc, q, h).transpose(0, 1, 3, 2), axis=-1)
    xdt = (xh * dt[..., None]).reshape(b, nc, q, h, pd)
    bc = bh.reshape(b, nc, q, h, n)
    cc = ch.reshape(b, nc, q, h, n)
    to_end = jnp.exp(cum[..., -1:] - cum)
    chunk_states = jnp.einsum('bcqhn,bchq,bcqhp->bchpn', bc, to_end, xdt)
    chunk_decay = jnp.exp(cum[..., -1])

    def step(state, inp):
        s_c, d_c = inp
        return state * d_c[..., None, None] + s_c, state

    final, entering = lax.scan(step, init, (jnp.moveaxis(chunk_states, 1, 0), jnp.moveaxis(chunk_decay, 1, 0)))
    if not want_y:
        return None, final
    entering = jnp.moveaxis(entering, 0, 1)
    causal = jnp.tril(jnp.ones((q, q), dtype=bool))
    seg = jnp.exp(jnp.where(causal, cum[..., :, None] - cum[..., None, :], -jnp.inf))
    scores = jnp.einsum('bclhn,bcshn->bchls', cc, bc) * seg
    y = jnp.einsum('bchls,bcshp->bclhp', scores, xdt)
    y = y + jnp.einsum('bclhn,bchpn->bclhp', cc, entering) * jnp.exp(cum).transpose(0, 1, 3, 2)[..., None]
    return y.reshape(b, L, h, pd), final

def ssd_mixer(z, xbc, dt_raw, p, init, want_y):
    b, L, _ = z.shape
    f32 = jnp.float32
    xbc = jax.nn.silu(short_conv(xbc, p['ssd_conv_w'], p['ssd_conv_b']))
    xs, bs, cs = split_sizes(xbc, (SSD_WIDTH, SSD_GROUPS * SSD_STATE, SSD_GROUPS * SSD_STATE))
    rep = SSD_HEADS // SSD_GROUPS
    xh = xs.reshape(b, L, SSD_HEADS, HEAD_DIM).astype(f32)
    bh = jnp.repeat(bs.reshape(b, L, SSD_GROUPS, SSD_STATE), rep, axis=2).astype(f32)
    chh = jnp.repeat(cs.reshape(b, L, SSD_GROUPS, SSD_STATE), rep, axis=2).astype(f32)
    dt = jax.nn.softplus(dt_raw.reshape(b, L, 2, SSD_HEADS).astype(f32) + p['ssd_dt_bias'])
    a = -jnp.exp(p['ssd_a_log'].astype(f32))
    y_f, s_f = ssd_scan(xh, dt[:, :, 0], a[0], bh, chh, init[0], want_y)
    y_b, s_b = ssd_scan(flip(xh), flip(dt[:, :, 1]), a[1], flip(bh), flip(chh), init[1], want_y)
    if not want_y:
        return None, (s_f, s_b)
    y = y_f + flip(y_b) + xh * p['ssd_d'][:, None]
    y = y.reshape(b, L, SSD_WIDTH).astype(z.dtype)
    return rmsnorm(y * jax.nn.silu(z), p['ssd_norm_w']), (s_f, s_b)

def mlstm_scan(q, k, v, i_pre, f_pre, init, want_y):
    b, L, h, d = q.shape
    qn = MLSTM_CHUNK
    nc = L // qn
    chunk = lambda t: t.reshape(b, nc, qn, h, d).transpose(0, 1, 3, 2, 4)
    gate = lambda t: t.reshape(b, nc, qn, h).transpose(0, 1, 3, 2)
    qc, kc, vc = chunk(q), chunk(k) * (d ** -0.5), chunk(v)
    ig = gate(i_pre)
    cum_f = jnp.cumsum(gate(jax.nn.log_sigmoid(f_pre)), axis=-1)
    tot_f = cum_f[..., -1]
    w_end = tot_f[..., None] - cum_f + ig
    m_loc = jnp.max(w_end, axis=-1)
    e_end = jnp.exp(w_end - m_loc[..., None])
    c_loc = jnp.einsum('bchq,bchqv,bchqk->bchvk', e_end, vc, kc)
    n_loc = jnp.einsum('bchq,bchqk->bchk', e_end, kc)

    def step(carry, inp):
        c_prev, n_prev, m_prev = carry
        c_l, n_l, m_l, g_l = inp
        m_new = jnp.maximum(g_l + m_prev, m_l)
        a_prev = jnp.exp(g_l + m_prev - m_new)
        a_loc = jnp.exp(m_l - m_new)
        new = (a_prev[..., None, None] * c_prev + a_loc[..., None, None] * c_l,
               a_prev[..., None] * n_prev + a_loc[..., None] * n_l,
               m_new)
        return new, (c_prev, n_prev, m_prev)

    mv = lambda t: jnp.moveaxis(t, 1, 0)
    final, (c_in, n_in, m_in) = lax.scan(step, init, (mv(c_loc), mv(n_loc), mv(m_loc), mv(tot_f)))
    if not want_y:
        return None, final
    c_in, n_in, m_in = mv(c_in), mv(n_in), mv(m_in)
    causal = jnp.tril(jnp.ones((qn, qn), dtype=bool))
    log_w = jnp.where(causal, cum_f[..., :, None] - cum_f[..., None, :] + ig[..., None, :], -jnp.inf)
    inter = cum_f + m_in[..., None]
    m_t = jnp.maximum(inter, jnp.max(log_w, axis=-1))
    s = jnp.einsum('bchld,bchsd->bchls', qc, kc) * jnp.exp(log_w - m_t[..., None])
    a_inter = jnp.exp(inter - m_t)
    num = jnp.einsum('bchls,bchsv->bchlv', s, vc) + a_inter[..., None] * jnp.einsum('bchld,bchvd->bchlv', qc, c_in)
    den = jnp.sum(s, axis=-1) + a_inter * jnp.einsum('bchld,bchd->bchl', qc, n_in)
    hid = num / jnp.maximum(jnp.abs(den), jnp.exp(-m_t))[..., None]
    return hid.transpose(0, 1, 3, 2, 4).reshape(b, L, h, d), final

def head_layernorm(h, w):
    mu = jnp.mean(h, axis=-1, keepdims=True)
    hc = h - mu
    return hc * lax.rsqrt(jnp.mean(hc * hc, axis=-1, keepdims=True) + EPS) * w

def mlstm_mixer(qk, v, o, g, p, init, want_y):
    b, L, _ = v.shape
    f32 = jnp.float32
    qk = jax.nn.silu(short_conv(qk, p['ml_conv_w'], p['ml_conv_b']))
    q, k = jnp.split(qk, 2, axis=-1)
    heads = lambda t: t.reshape(b, L, MLSTM_HEADS, HEAD_DIM).astype(f32)
    q, k, vh = heads(q), heads(k), heads(v)
    gates = g.reshape(b, L, 2, 2, MLSTM_HEADS).astype(f32) + p['ml_gate_b']
    h_f, s_f = mlstm_scan(q, k, vh, gates[:, :, 0, 0], gates[:, :, 0, 1], init[0], want_y)
    h_b, s_b = mlstm_scan(flip(q), flip(k), flip(vh), flip(gates[:, :, 1, 0]), flip(gates[:, :, 1, 1]), init[1], want_y)
    if not want_y:
        return None, (s_f, s_b)
    h = head_layernorm(h_f + flip(h_b), p['ml_norm_w'].reshape(MLSTM_HEADS, HEAD_DIM))
    out = jax.nn.sigmoid(o.astype(f32)) * h.reshape(b, L, MLSTM_WIDTH)
    return out.astype(v.dtype), (s_f, s_b)

def hyena_filters(L, p):
    t = jnp.arange(L, dtype=jnp.float32)
    t_unit = t / float(max(L - 1, 1))
    bands = jnp.linspace(1e-4, HYENA_BANDS - 1, HYENA_BANDS, dtype=jnp.float32)
    ang = (2 * math.pi / L) * t[:, None] * bands[None, :]
    feats = jnp.concatenate([t_unit[:, None], jnp.cos(ang), -jnp.sin(ang)], axis=-1)
    freq = p['hy_freq']
    hdn = jnp.sin(freq * (feats @ p['hy_pos_w1'] + p['hy_pos_b1']))
    hdn = jnp.sin(freq * (hdn @ p['hy_pos_w2'] + p['hy_pos_b2']))
    filt = (hdn @ p['hy_pos_w3']).reshape(L, 2, HYENA_ORDER, HYENA_WIDTH)
    window = jnp.exp(-t_unit[:, None, None, None] * jnp.abs(p['hy_decay']))
    return (filt * window).astype(jnp.float32)

def bidir_long_conv(z, h_fwd, h_bwd):
    L, ch = h_fwd.shape
    two_sided = jnp.concatenate([h_fwd, jnp.zeros((1, ch), h_fwd.dtype), h_bwd[1:][::-1]], axis=0)
    two_sided = two_sided / jnp.sum(jnp.abs(two_sided), axis=0, keepdims=True)
    zf = jnp.fft.rfft(z.astype(jnp.float32), n=2 * L, axis=1)
    hf = jnp.fft.rfft(two_sided, n=2 * L, axis=0)
    return jnp.fft.irfft(zf * hf[None], n=2 * L, axis=1)[:, :L]

def hyena_mixer(u, p):
    uc = short_conv(u, p['hy_conv_w'], p['hy_conv_b'])
    v, *gates = jnp.split(uc.astype(jnp.float32), HYENA_ORDER + 1, axis=-1)
    filt = hyena_filters(u.shape[1], p)
    z = v
    for order, gate in enumerate(gates):
        z = gate * (bidir_long_conv(z, filt[:, 0, order], filt[:, 1, order]) + p['hy_skip'][order] * z)
    return z.astype(u.dtype)

def token_mixers(u, p, ssd_init, ml_init, want_out):
    z, xbc, dt_raw, hy_u, ml_qk, ml_v, ml_o, ml_g = split_sizes(u, IN_SIZES)
    y_ssd, ssd_fin = ssd_mixer(z, xbc, dt_raw, p, ssd_init, want_out)
    y_ml, ml_fin = mlstm_mixer(ml_qk, ml_v, ml_o, ml_g, p, ml_init, want_out)
    if not want_out:
        return None, ssd_fin, ml_fin
    y_hy = hyena_mixer(hy_u, p)
    return jnp.concatenate([y_ssd, y_hy, y_ml], axis=-1), ssd_fin, ml_fin

def hier_moe(h, p):
    b, L, dm = h.shape
    t = h.reshape(b * L, dm)
    grp_prob = jax.nn.softmax((t @ p['grp_router_w'] + p['grp_router_b']).astype(jnp.float32), axis=-1)
    grp_p, grp_idx = lax.top_k(grp_prob, 1)
    exp_logits = (t @ p['exp_router_w'] + p['exp_router_b']).astype(jnp.float32)
    exp_logits = exp_logits.reshape(-1, N_GROUPS, EXPERTS_PER_GROUP)
    in_grp = jnp.take_along_axis(exp_logits, grp_idx[:, :, None], axis=1)[:, 0]
    top_p, top_idx = lax.top_k(jax.nn.softmax(in_grp, axis=-1), TOP_K_IN_GROUP)
    top_w = grp_p * top_p / jnp.sum(top_p, axis=-1, keepdims=True)
    expert_w = jnp.sum(jax.nn.one_hot(top_idx, EXPERTS_PER_GROUP) * top_w[..., None], axis=1)
    group_mask = jax.nn.one_hot(grp_idx[:, 0], N_GROUPS)
    out = jnp.zeros_like(t)
    for g in range(N_GROUPS):
        gate_w = (group_mask[:, g:g + 1] * expert_w).astype(t.dtype)
        hid = jax.nn.silu(jnp.einsum('td,edf->tef', t, p['moe_w_gate'][g])) * jnp.einsum('td,edf->tef', t, p['moe_w_up'][g])
        out = out + jnp.einsum('tef,efd->td', hid * gate_w[..., None], p['moe_w_down'][g])
    return out.reshape(b, L, dm)

def setup_inputs(seed: int = 0) -> dict:
    key = jax.random.key(seed)
    keys = list(jax.random.split(key, 48))
    f32 = jnp.float32

    def nrm(shape, scale):
        return jax.random.normal(keys.pop(), shape, f32) * scale

    def gain(shape):
        return 1.0 + nrm(shape, 0.02)

    def unif(shape, lo, hi):
        return jax.random.uniform(keys.pop(), shape, f32, minval=lo, maxval=hi)

    D, FH, HW = D_MODEL, HYENA_FILTER_HIDDEN, HYENA_WIDTH
    dt0 = jnp.exp(unif((DEPTH, 2, SSD_HEADS), math.log(1e-3), math.log(1e-1)))
    decay_lo, decay_hi = -math.log(1e-2) / 1.5, -math.log(1e-2) / 0.3
    decay = jnp.broadcast_to(jnp.linspace(decay_lo, decay_hi, HW, dtype=f32), (DEPTH, 2, HYENA_ORDER, HW))
    f_bias = jnp.linspace(3.0, 6.0, MLSTM_HEADS, dtype=f32) + nrm((DEPTH, 2, MLSTM_HEADS), 0.02)
    i_bias = nrm((DEPTH, 2, MLSTM_HEADS), 0.1)
    return {
        'x': nrm((BATCH, SEQ, D), 1.0),
        'c': nrm((BATCH, D), 1.0),
        'ctx': nrm((BATCH, CTX_LEN, D), 1.0),
        'c_ctx': nrm((D,), 1.0),
        'w_mod': nrm((DEPTH, D, N_MOD * D), 0.5 * D ** -0.5),
        'b_mod': nrm((DEPTH, N_MOD * D), 0.02),
        'norm1_w': gain((DEPTH, D)),
        'norm2_w': gain((DEPTH, D)),
        'w_in': nrm((DEPTH, D, IN_COLS), D ** -0.5),
        'w_out': nrm((DEPTH, D_MIX, D), D_MIX ** -0.5),
        'ssd_conv_w': nrm((DEPTH, SHORT_CONV, SSD_CONV_CH), SHORT_CONV ** -0.5),
        'ssd_conv_b': nrm((DEPTH, SSD_CONV_CH), 0.02),
        'ssd_dt_bias': dt0 + jnp.log(-jnp.expm1(-dt0)),
        'ssd_a_log': jnp.log(unif((DEPTH, 2, SSD_HEADS), 1.0, 16.0)),
        'ssd_d': gain((DEPTH, SSD_HEADS)),
        'ssd_norm_w': gain((DEPTH, SSD_WIDTH)),
        'hy_conv_w': nrm((DEPTH, SHORT_CONV, (HYENA_ORDER + 1) * HW), SHORT_CONV ** -0.5),
        'hy_conv_b': nrm((DEPTH, (HYENA_ORDER + 1) * HW), 0.02),
        'hy_pos_w1': nrm((DEPTH, HYENA_POS_DIM, FH), HYENA_POS_DIM ** -0.5),
        'hy_pos_b1': nrm((DEPTH, FH), 0.02),
        'hy_pos_w2': nrm((DEPTH, FH, FH), FH ** -0.5),
        'hy_pos_b2': nrm((DEPTH, FH), 0.02),
        'hy_pos_w3': nrm((DEPTH, FH, 2 * HYENA_ORDER * HW), FH ** -0.5),
        'hy_freq': gain((DEPTH, FH)),
        'hy_decay': decay + nrm((DEPTH, 2, HYENA_ORDER, HW), 0.02),
        'hy_skip': nrm((DEPTH, HYENA_ORDER, HW), 1.0),
        'ml_conv_w': nrm((DEPTH, SHORT_CONV, 2 * MLSTM_WIDTH), SHORT_CONV ** -0.5),
        'ml_conv_b': nrm((DEPTH, 2 * MLSTM_WIDTH), 0.02),
        'ml_gate_b': jnp.stack([i_bias, f_bias], axis=2),
        'ml_norm_w': gain((DEPTH, MLSTM_WIDTH)),
        'grp_router_w': nrm((DEPTH, D, N_GROUPS), D ** -0.5),
        'grp_router_b': nrm((DEPTH, N_GROUPS), 0.01),
        'exp_router_w': nrm((DEPTH, D, N_EXPERTS), D ** -0.5),
        'exp_router_b': nrm((DEPTH, N_EXPERTS), 0.01),
        'moe_w_gate': nrm((DEPTH, N_GROUPS, EXPERTS_PER_GROUP, D, EXPERT_HIDDEN), D ** -0.5),
        'moe_w_up': nrm((DEPTH, N_GROUPS, EXPERTS_PER_GROUP, D, EXPERT_HIDDEN), D ** -0.5),
        'moe_w_down': nrm((DEPTH, N_GROUPS, EXPERTS_PER_GROUP, EXPERT_HIDDEN, D), EXPERT_HIDDEN ** -0.5),
        'final_norm_w': gain((D,)),
    }

def reference(x, c, ctx, c_ctx, w_mod, b_mod, norm1_w, norm2_w, w_in, w_out,
              ssd_conv_w, ssd_conv_b, ssd_dt_bias, ssd_a_log, ssd_d, ssd_norm_w,
              hy_conv_w, hy_conv_b, hy_pos_w1, hy_pos_b1, hy_pos_w2, hy_pos_b2, hy_pos_w3,
              hy_freq, hy_decay, hy_skip, ml_conv_w, ml_conv_b, ml_gate_b, ml_norm_w,
              grp_router_w, grp_router_b, exp_router_w, exp_router_b,
              moe_w_gate, moe_w_up, moe_w_down, final_norm_w):
    layer_params = (
        ('ssd_conv_w', ssd_conv_w), ('ssd_conv_b', ssd_conv_b), ('ssd_dt_bias', ssd_dt_bias),
        ('ssd_a_log', ssd_a_log), ('ssd_d', ssd_d), ('ssd_norm_w', ssd_norm_w),
        ('hy_conv_w', hy_conv_w), ('hy_conv_b', hy_conv_b), ('hy_pos_w1', hy_pos_w1),
        ('hy_pos_b1', hy_pos_b1), ('hy_pos_w2', hy_pos_w2), ('hy_pos_b2', hy_pos_b2),
        ('hy_pos_w3', hy_pos_w3), ('hy_freq', hy_freq), ('hy_decay', hy_decay), ('hy_skip', hy_skip),
        ('ml_conv_w', ml_conv_w), ('ml_conv_b', ml_conv_b), ('ml_gate_b', ml_gate_b), ('ml_norm_w', ml_norm_w),
        ('grp_router_w', grp_router_w), ('grp_router_b', grp_router_b),
        ('exp_router_w', exp_router_w), ('exp_router_b', exp_router_b),
        ('moe_w_gate', moe_w_gate), ('moe_w_up', moe_w_up), ('moe_w_down', moe_w_down),
    )
    xl, xc = x, ctx
    ssd_zero, ml_zero = zero_states(ctx.shape[0])
    for i in range(DEPTH):
        last = i == DEPTH - 1
        p = {name: arr[i] for name, arr in layer_params}
        mod_l = jnp.split(jax.nn.silu(c) @ w_mod[i] + b_mod[i], N_MOD, axis=-1)
        mod_c = jnp.split(jax.nn.silu(c_ctx)[None, :] @ w_mod[i] + b_mod[i], N_MOD, axis=-1)
        uc = modulated_norm(xc, norm1_w[i], mod_c[0], mod_c[1]) @ w_in[i]
        yc, ssd_ctx, ml_ctx = token_mixers(uc, p, ssd_zero, ml_zero, not last)
        ul = modulated_norm(xl, norm1_w[i], mod_l[0], mod_l[1]) @ w_in[i]
        col_major = i % 2 == 1
        if col_major:
            ul = to_col_major(ul)
        yl, _, _ = token_mixers(ul, p, ssd_ctx, ml_ctx, True)
        if col_major:
            yl = to_row_major(yl)
        xl = xl + mod_l[2][:, None, :] * (yl @ w_out[i])
        xl = xl + mod_l[5][:, None, :] * hier_moe(modulated_norm(xl, norm2_w[i], mod_l[3], mod_l[4]), p)
        if not last:
            xc = xc + mod_c[2][:, None, :] * (yc @ w_out[i])
            xc = xc + mod_c[5][:, None, :] * hier_moe(modulated_norm(xc, norm2_w[i], mod_c[3], mod_c[4]), p)
    return rmsnorm(xl, final_norm_w)


_drawn_inputs = setup_inputs


def setup_inputs(seed=0):
    import zlib

    import numpy as np

    out = dict(_drawn_inputs(seed))
    spreads = {}
    factors = {'norm1_w': 3.203,
     'norm2_w': 4.133,
     'ssd_conv_b': 4.92,
     'ssd_d': 53.584,
     'ssd_norm_w': 7.519,
     'hy_conv_b': 4.265,
     'hy_pos_b1': 8.0,
     'hy_pos_b2': 8.0,
     'hy_freq': 8.0,
     'hy_decay': 3.163,
     'ml_conv_b': 6.026,
     'ml_norm_w': 7.795,
     'grp_router_b': 54.32,
     'exp_router_b': 5.613,
     'final_norm_w': 7.968}
    for name, (base, spread) in spreads.items():
        noise = np.random.default_rng([zlib.crc32(name.encode()), seed]).standard_normal(out[name].shape)
        drawn = base * np.exp(spread * noise) if base else spread * noise
        out[name] = jnp.asarray(drawn.astype(out[name].dtype))
    for name, factor in factors.items():
        out[name] = (out[name] * factor).astype(out[name].dtype)
    return out
```

```python
from contextlib import ExitStack

import concourse.bass as bass
from concourse import mybir
import numpy as np

F32 = mybir.dt.float32
BF16 = mybir.dt.bfloat16
ALU = mybir.AluOpType
ACT = mybir.ActivationFunctionType
AX = mybir.AxisListType

P = 128
D = 1024
KB = D // P
L = 256
DEPTH = 2
NT = 4
GRID_W = 64
ROWS = L // GRID_W
HD = 64
HEADS = 6
MIXW = HEADS * HD
HYW = 256
SSD_CH = MIXW + 256
FH = 64
POS = 33
N_GROUPS, PER_GROUP = 4, 8
EXPERTS = N_GROUPS * PER_GROUP
EH = 256
EPS = 1e-6
COL_Z, COL_XBC, COL_DT = 0, MIXW, MIXW + SSD_CH
COL_HY = COL_DT + 2 * HEADS
COL_QK = COL_HY + 3 * HYW
COL_V = COL_QK + 2 * MIXW
COL_O = COL_V + MIXW
COL_G = COL_O + MIXW
NEG = -1.0e30
MAGIC = 12582912.0
BANKS = 8
SLOTS = 4
PER_BODY = 4
BODIES = EXPERTS // PER_BODY
PREFETCH = SLOTS
BACK = (1, 0, 3, 2)
MOD_SLOTS = 6 * D // 256
MOD_FIRST = 2 * D // 256
MOD_LATER = [(0, n) for n in range(MOD_FIRST, MOD_SLOTS)] + [(1, n) for n in range(MOD_SLOTS)]
MOD_PER_UNIT = len(MOD_LATER) // (2 * NT)


class Tally:

    def __init__(self, at, first):
        self.at, self.first, self.count, self.sems = at, first, {}, {}
        self.turn = None

    def tick(self, sem, *names, by=1):
        self.count[sem] = self.count.get(sem, 0) + by
        for n in names:
            self.at[n] = (sem, self.count[sem])
            if self.turn is not None:
                self.at[("in", self.turn[0], n)] = True
        return by

    def due(self, name, turns_back=0):
        assert self.first or name in self.at, name
        sem, value = self.at.get(name, ("dve_done", 1000))
        if self.turn is not None and ("in", self.turn[0], name) in self.at:
            tag, i = self.turn
            per = self.at.get(("per", tag, sem), 1)
            return self.sems[sem], i * per + (value - turns_back * per)
        return self.sems[sem], value

    def looped(self, tag, before, turns):
        self.turn = None
        for sem in list(self.count):
            per = self.count[sem] - before.get(sem, 0)
            if per:
                self.at[("per", tag, sem)] = per
                self.count[sem] += per * (turns - 1)


def build(nc, A, out, at, first):
    tally = Tally(at, first)
    tick, due = tally.tick, tally.due
    with ExitStack() as ctx:
        def sb(name, cols, dt=F32):
            return ctx.enter_context(nc.sbuf_tensor(name, [P, cols], dt))

        def sem(name):
            tally.sems[name] = ctx.enter_context(nc.semaphore(name))
            return tally.sems[name]

        pe_done, act_done, dve_done = sem("pe_done"), sem("act_done"), sem("dve_done")
        consts_in, x_in, norm_in, out_written = sem("consts_in"), sem("x_in"), sem("norm_in"), sem("out_written")
        params_in = [sem(f"params{l}_in") for l in range(DEPTH)]
        slot_in = [sem(f"slot{s}_in") for s in range(SLOTS)]
        banks = [ctx.enter_context(nc.psum_tensor(f"bank{b}", [P, 512], F32)) for b in range(BANKS)]

        ident = sb("ident", P)
        ident16 = sb("ident16", P, BF16)
        ones = sb("ones", P)
        mask16 = sb("mask16", 2 * P, BF16)
        sel = sb("sel", 2 * 3 * P)
        keep = sb("keep", 4 * P)
        dftc = sb("dftc", 2 * L)
        dfts = sb("dfts", 2 * L)
        dftn = sb("dftn", 2 * 2 * P)
        invc = sb("invc", 2 * L)
        invs = sb("invs", 2 * L)
        feats = sb("feats", L)
        tcol = sb("tcol", 4)
        iom = sb("iom", EXPERTS)
        prow = sb("prow", P)
        pcol = sb("pcol", P)
        cond = sb("cond", 2 * KB)
        bmod = sb("bmod", DEPTH * 6 * KB)
        nw = sb("nw", 2 * KB)
        gcolp = sb("gcolp", 4)
        wg_raw = sb("wg_raw", KB * 36)
        rw = sb("rw", KB * 36)
        rb = sb("rb", 36)
        ssdd = sb("ssdd", HEADS)
        w1 = sb("w1", FH)
        w2 = sb("w2", FH)
        hcol = sb("hcol", 3)
        x = sb("x", NT * D)
        hT = sb("hT", KB * 4 * P)
        modc = sb("modc", DEPTH * 6 * KB * 2)
        ab = sb("ab", 4 * KB * 2)
        grow = sb("grow", 2 * D)
        small = sb("small", 64)
        xbc = sb("xbc", 5 * 512)
        qkT = sb("qkT", 6 * 512)
        hyT = sb("hyT", 6 * 512)
        ztok = sb("ztok", NT * MIXW)
        otok = sb("otok", NT * MIXW)
        vaug = sb("vaug", NT * HEADS * 65)
        big = sb("big", 9 * 512)
        hfilt = sb("hfilt", 5 * 512)
        xtok = sb("xtok", NT * 512)
        ktok = sb("ktok", NT * MIXW)
        ysum = sb("ysum", NT * MIXW)
        hsum = sb("hsum", NT * MIXW)
        ring = sb("ring", SLOTS * 2048)
        sst = sb("sst", 2 * MIXW)
        cst = sb("cst", 2 * HEADS * 65)
        if not first:
            print("sbuf left", nc.sbuf_bytes_remaining)

        wg, w3 = xtok[:, :], ktok[:, 0:1024]
        cols, dcb = hT[:, 1536:1536 + NT * 4 * P], hT[:, 3584:3584 + NT * P]
        wx, wv = hT[:, 0:1158], big[:, 0:2 * 4 * 384]

        modrow = grow[:, 3 * D // 2:2 * D]

        mask_v = mask16[:, :].rearrange("p (d s) -> p d s", d=2)
        sel_v = sel[:, :].rearrange("p (j i m) -> p j i m", j=2, i=3)
        dftc_v = dftc[:, :].rearrange("p (t f) -> p t f", t=2)
        dfts_v = dfts[:, :].rearrange("p (t f) -> p t f", t=2)
        dftn_v = dftn[:, :].rearrange("p (q t f) -> p q t f", q=2, t=2)
        invc_v = invc[:, :].rearrange("p (b t) -> p b t", b=2)
        invs_v = invs[:, :].rearrange("p (b t) -> p b t", b=2)
        cond_v = cond[:, :].rearrange("p (k s) -> p k s", s=2)
        bmod_v = bmod[:, :].rearrange("p (l m k) -> p l m k", l=DEPTH, m=6)
        nw_v = nw[:, :].rearrange("p (n k) -> p n k", n=2)
        wgr_v = wg_raw[:, :].rearrange("p (k n) -> p k n", k=KB)
        wg_v = wg[:, :].rearrange("p (k y r) -> p k y r", k=KB, y=2)
        rw_v = rw[:, :].rearrange("p (k n) -> p k n", k=KB)
        x_v = x[:, :].rearrange("p (t d) -> p t d", t=NT)
        hT_v = hT[:, :].rearrange("p (k n) -> p k n", k=KB)
        yT_v = hT_v
        modc_v = modc[:, :].rearrange("p (l m k s) -> p l m k s", l=DEPTH, m=6, s=2)
        ab_v = ab[:, :].rearrange("p (n k s) -> p n k s", n=4, s=2)
        grow_v = grow[:, :].rearrange("p (s d) -> p s d", s=2)
        xbc_v = xbc[:, :].rearrange("p (b n) -> p b n", n=512)
        qk_v = qkT[:, :].rearrange("p (b n) -> p b n", n=512)
        hy_v = hyT[:, :].rearrange("p (b n) -> p b n", n=512)
        z_v = ztok[:, :].rearrange("p (t c) -> p t c", t=NT)
        o_v = otok[:, :].rearrange("p (t c) -> p t c", t=NT)
        va_v = vaug[:, :].rearrange("p (t h c) -> p t h c", t=NT, h=HEADS)
        xtok_v = xtok[:, :].rearrange("p (t c) -> p t c", t=NT)
        ktok_v = ktok[:, :].rearrange("p (t c) -> p t c", t=NT)
        ys_v = ysum[:, :].rearrange("p (t c) -> p t c", t=NT)
        hs_v = hsum[:, :].rearrange("p (t c) -> p t c", t=NT)
        cols_v = cols[:, :].rearrange("p (c q r) -> p c q r", c=NT, q=4)
        dcb_v = dcb[:, :].rearrange("p (c r) -> p c r", c=NT)
        hf_v = hfilt[:, :].rearrange("p (b n) -> p b n", n=512)
        sst_v = sst[:, :].rearrange("p (d n) -> p d n", d=2)
        cst_v = cst[:, :].rearrange("p (d q j c) -> p d q j c", d=2, q=3, j=2)
        big_v = big[:, :].rearrange("p (r n) -> p r n", n=512)
        U, SP, CUM, EX, ES, ND, MX, RL, RS = (big_v[:, r, :] for r in range(9))
        t1, t2, t3 = (ysum[:, 512 * r:512 * r + 512] for r in range(3))
        xn_v = big[:, 0:4096].rearrange("p (t d) -> p t d", t=NT)
        taps_v = big[:, 0:2048].rearrange("p (t e o c) -> p t e o c", t=2, e=2, o=2)
        tabs_v = big[:, 2048:4096].rearrange("p (t e o c) -> p t e o c", t=2, e=2, o=2)
        hid_a, hid_b, hid_c = (hsum[:, 256 * r:256 * r + 256] for r in range(3))
        sc_v = wv[:, :].rearrange("p (u j n) -> p u j n", u=2, j=4)
        xdt, xde, ve, nds = wx[:, 0:384], wx[:, 384:768], wx[:, 768:1158], big[:, 3072:3462]
        rlm_v = grow[:, 0:2 * 2 * 384].rearrange("p (u j i n) -> p u j i n", u=2, j=2, i=3)
        ve_v = ve.rearrange("p (h c) -> p h c", h=HEADS)
        nds_v = nds.rearrange("p (h c) -> p h c", h=HEADS)
        zt_v = ysum[:, 0:1024].rearrange("p (t n) -> p t n", t=2)
        yf_v = wv[:, 0:2048].rearrange("p (b n) -> p b n", b=4)
        ht1, ht2 = hsum[:, 0:512], hsum[:, 512:1024]
        acc_v = big[:, 0:4096].rearrange("p (t d) -> p t d", t=NT)
        gwt = ztok[:, 0:NT * EXPERTS].rearrange("p (t e) -> p t e", t=NT)
        hid_v = qkT[:, 0:2 * 2 * 512].rearrange("p (u f n) -> p u f n", u=2, f=2)
        sg_v = hyT[:, 0:2 * 512].rearrange("p (u n) -> p u n", u=2)

        def slot_v(s, k):
            return ring[:, s * 2048:(s + 1) * 2048].rearrange("p (k n) -> p k n", k=k)

        products = []
        loads = []

        block = ctx.enter_context(nc.Block())

        @block.sync
        def _(sp):
            def weight(name, src, k):
                n = len(loads)
                s = n % SLOTS
                loads.append(name)
                at[("slot", name)] = s
                if n >= SLOTS:
                    sp.wait_ge(*due(("used", loads[n - SLOTS])))
                with nc.allow_non_contiguous_dma(reason="rows of a kilobyte"):
                    sp.dma_start(slot_v(s, k)[:, :, 0:src.shape[-1]], src).then_inc(
                        slot_in[s], tick(f"slot{s}_in", ("load", name), by=16))

            def fetch(group, dst, src):
                with nc.allow_non_contiguous_dma(reason="small parameters"):
                    sp.dma_start(dst, src).then_inc(tally.sems[group], tick(group, (group,), by=16))

            def parameters(l):
                g = f"params{l}_in"
                if l == 0:
                    sp.wait_ge(*due(("gcolp zero",)))
                else:
                    for who in ("pe", "act", "dve"):
                        sp.wait_ge(*due(("end", who, l - 1, "moe")))
                fetch(g, nw_v[:, 0, :], A["norm1_w"][l].rearrange("(p k) -> p k", k=KB))
                fetch(g, nw_v[:, 1, :], A["norm2_w"][l].rearrange("(p k) -> p k", k=KB))
                r = 0
                for name, n in (("ssd_conv_w", 15), ("ssd_conv_b", 5), ("hy_conv_w", 18), ("hy_conv_b", 6),
                                ("ml_conv_w", 18), ("ml_conv_b", 6), ("ssd_norm_w", 3), ("ml_norm_w", 3),
                                ("hy_skip", 4)):
                    src = A[name][l]
                    src = src.rearrange("w (b c) -> (w b) c", c=P) if len(src.shape) == 2 else \
                        src.rearrange("(b c) -> b c", c=P)
                    fetch(g, prow[r:r + n, :], src)
                    r += n
                for d in range(2):
                    fetch(g, gcolp[32 * d:32 * d + HEADS, 0:1], A["ssd_dt_bias"][l, d].unsqueeze(1))
                    fetch(g, gcolp[64 + 32 * d:64 + 32 * d + HEADS, 0:1], A["ml_gate_b"][l, d, 1].unsqueeze(1))
                    fetch(g, gcolp[64 + 32 * d:64 + 32 * d + HEADS, 1:2], A["ml_gate_b"][l, d, 0].unsqueeze(1))
                    fetch(g, gcolp[32 * d:32 * d + HEADS, 2:3], A["ssd_a_log"][l, d].unsqueeze(1))
                win = A["w_in"][l].rearrange("(p k) n -> p k n", k=KB)
                fetch(g, wgr_v[:, :, 0:12], win[:, :, COL_DT:COL_DT + 12])
                fetch(g, wgr_v[:, :, 12:36], win[:, :, COL_G:COL_G + 24])
                fetch(g, rw_v[:, :, 0:4], A["grp_router_w"][l].rearrange("(p k) n -> p k n", k=KB))
                fetch(g, rw_v[:, :, 4:36], A["exp_router_w"][l].rearrange("(p k) n -> p k n", k=KB))
                fetch(g, rb[:, 0:4], A["grp_router_b"][l].partition_broadcast(P))
                fetch(g, rb[:, 4:36], A["exp_router_b"][l].partition_broadcast(P))
                fetch(g, ssdd[:, :], A["ssd_d"][l].partition_broadcast(P))
                fetch(g, w1[0:POS, :], A["hy_pos_w1"][l])
                fetch(g, w2[0:FH, :], A["hy_pos_w2"][l])
                fetch(g, w3[0:FH, :], A["hy_pos_w3"][l])
                for c, name in enumerate(("hy_pos_b1", "hy_pos_b2", "hy_freq")):
                    fetch(g, hcol[0:FH, c:c + 1], A[name][l].unsqueeze(1))
                fetch(g, grow[:, 0:4 * HYW],
                      A["hy_decay"][l].rearrange("e o c -> (e o c)").partition_broadcast(P))

            fetch("consts_in", cond_v[:, :, 0], A["c"][0].rearrange("(p k) -> p k", k=KB))
            fetch("consts_in", cond_v[:, :, 1], A["c_ctx"].rearrange("(p k) -> p k", k=KB))
            for name, t in (("ident", ident), ("mask", big[:, 0:2 * P]), ("sel", sel), ("keep", keep),
                            ("dftc", dftc), ("dfts", dfts), ("dftn", dftn), ("invc", invc), ("invs", invs),
                            ("tcol", tcol), ("iom", iom)):
                fetch("consts_in", t[:, :], A["const_" + name])
            fetch("consts_in", feats[0:POS, :], A["const_feats"])
            for l in range(DEPTH):
                fetch("consts_in", bmod_v[:, l], A["b_mod"][l].rearrange("(m p k) -> p m k", m=6, k=KB))
            fetch("x_in", x_v[:, 0:2, :], A["ctx"][0].rearrange("(t p) d -> p t d", p=P))
            fetch("x_in", x_v[:, 2:4, :], A["x"][0].rearrange("(t p) d -> p t d", p=P))

            def modulation(l, n):
                wm = A["w_mod"][l].rearrange("(p k) n -> p k n", k=KB)
                weight(("mod", l, n), wm[:, :, 256 * n:256 * n + 256], KB)

            for l in range(DEPTH):
                parameters(l)
                if l == 0:
                    for n in range(MOD_FIRST):
                        modulation(0, n)
                win = A["w_in"][l].rearrange("(p k) n -> p k n", k=KB)
                for name, c0, n in (("qk", COL_QK, 768), ("xbc", COL_XBC, 640), ("v", COL_V, 384),
                                    ("z", COL_Z, 384), ("o", COL_O, 384), ("hy", COL_HY, 768)):
                    for q in range((n + 255) // 256):
                        w = min(256, n - 256 * q)
                        weight((name, l, q), win[:, :, c0 + 256 * q:c0 + 256 * q + w], KB)
                if l == 0:
                    for ml, n in MOD_LATER:
                        modulation(ml, n)
                wo = A["w_out"][l].rearrange("(k p) n -> p k n", p=P)
                for q in range(4):
                    weight(("wout", l, q), wo[:, :, 256 * q:256 * q + 256], KB)

                wgt = A["moe_w_gate"][l].rearrange("g e (p k) f -> (g e) p k f", k=KB)
                wup = A["moe_w_up"][l].rearrange("g e (p k) f -> (g e) p k f", k=KB)
                wdn = A["moe_w_down"][l].rearrange("g e (f p) d -> (g e) p f d", p=P)
                body = 3 * PER_BODY
                base = len(loads)

                def expert_src(j, e):
                    w = (wgt, wup, wdn)[j % 3]
                    return w[bass.ds(e, 1)].rearrange("e p k f -> (e p) k f") if not isinstance(e, int) else w[e]

                def expert_load(q, e):
                    j, s = q % body, (base + q) % SLOTS
                    at[("slot", ("expert", l, j))] = (base + j) % SLOTS
                    k = KB if j % 3 < 2 else 2
                    with nc.allow_non_contiguous_dma(reason="rows of a kilobyte"):
                        return sp.dma_start(slot_v(s, k), expert_src(j, e)), s

                def turns_first(q):
                    name = ("load", ("expert", l, q))
                    at[("in", ("moe", l), name)] = True
                    return name

                for q in range(PREFETCH):
                    sp.wait_ge(*due(("used", loads[base + q - SLOTS])))
                    ins, s = expert_load(q, q // 3)
                    ins.then_inc(slot_in[s], tick(f"slot{s}_in", turns_first(q), by=16))
                before = dict(tally.count)
                with sp.Fori(0, BODIES - 1) as i:
                    tally.turn = (("moe", l), i)
                    for q in range(PREFETCH, PREFETCH + body):
                        sp.wait_ge(*due(("used", ("expert", l, q - SLOTS))))
                        ins, s = expert_load(q, i * PER_BODY + q // 3)
                        names = [turns_first(q)] if q < body else []
                        ins.then_inc(slot_in[s], tick(f"slot{s}_in", *names, by=16))
                tally.looped(("moe", l), before, BODIES - 1)
                for q in range(PREFETCH, body):
                    sp.wait_ge(*due(("used", ("expert-last", l, q - SLOTS))))
                    ins, s = expert_load(q, EXPERTS - PER_BODY + q // 3)
                    ins.then_inc(slot_in[s], tick(f"slot{s}_in", by=16))
                for j in range(body):
                    loads.append(("expert-last", l, j))

            sp.wait_ge(*due(("fnw free",)))
            fetch("norm_in", grow[:, 0:D], A["final_norm_w"].partition_broadcast(P))
            for t in range(2):
                sp.wait_ge(*due(("result", t)))
                sp.dma_start(out[0, t * P:(t + 1) * P, :], xn_v[:, t, :]).then_inc(out_written, 16)
            sp.wait_ge(out_written, 32)

        @block.tensor
        def _(pe):
            def product(name):
                n = len(products)
                products.append(name)
                at[("bank", name)] = n % BANKS
                if n >= BANKS:
                    pe.wait_ge(*due(("read", products[n - BANKS])))
                return banks[n % BANKS]

            def made(name, *also):
                return tick("pe_done", ("made", name), *also)

            def mm(o, a, b, s=True, e=True, **k):
                return nc.tensor.matmul(o, a, b, start=s, stop=e, **k)

            def slot(name, k):
                return slot_v(at[("slot", name)], k)

            def stage_end(l, stage):
                pe.drain().then_inc(pe_done, tick("pe_done", ("end", "pe", l, stage)))
                pe.wait_ge(*due(("end", "act", l, stage)))
                pe.wait_ge(*due(("end", "dve", l, stage)))

            def modulation(l, n):
                m, q = n // 4, n % 4
                b = product(("mod", l, n))
                pe.wait_ge(*due(("load", ("mod", l, n))))
                w = slot(("mod", l, n), KB)
                for k in range(KB):
                    last = mm(b[0:2, 0:256], cond_v[:, k, :], w[:, k, :], k == 0, k == KB - 1)
                last.then_inc(pe_done, made(("mod", l, n), ("used", ("mod", l, n))))
                if q % 2:
                    b = product(("modc", l, m, q // 2))
                    pe.wait_ge(*due(("modrow", l, n)))
                    for k in range(KB):
                        last = nc.tensor.transpose(b[0:64, 2 * k:2 * k + 2], modrow[0:2, k::KB], ident[0:2, 0:2])
                    last.then_inc(pe_done, made(("modc", l, m, q // 2)))

            for l in range(DEPTH):
                t0 = 0 if l == 0 else 2
                n0 = t0 * P
                b = product(("pcol", l))
                pe.wait_ge(*due((f"params{l}_in",)))
                pe.wait_ge(*due(("consts_in",)))
                nc.tensor.transpose(b[:, 0:78], prow[0:78, :], ident[0:78, 0:78]).then_inc(pe_done, made(("pcol", l)))
                if l == 0:
                    pe.wait_ge(*due(("cond",)))
                    for n in range(MOD_FIRST):
                        modulation(0, n)
                b = product(("hid1", l))
                mm(b[0:FH, 0:L], w1[0:POS, :], feats[0:POS, :]).then_inc(pe_done, made(("hid1", l)))
                b = product(("hid2", l))
                pe.wait_ge(*due(("sin", l, 0)))
                mm(b[0:FH, 0:L], w2[0:FH, :], hid_c[0:FH, :]).then_inc(pe_done, made(("hid2", l)))
                for t in range(2):
                    for e in range(2):
                        b = product(("taps", l, t, e))
                        pe.wait_ge(*due(("sin", l, 1)))
                        mm(b[:, :], hid_c[0:FH, t * P:(t + 1) * P], w3[0:FH, 512 * e:512 * e + 512]).then_inc(pe_done, made(("taps", l, t, e)))
                b = product(("tapsum", l))
                pe.wait_ge(*due(("tabs", l)))
                for o in range(2):
                    for c in range(2):
                        n = 0
                        for t in range(2):
                            for e in range(2):
                                last = mm(b[:, 2 * o + c:2 * o + c + 1], tabs_v[:, t, e, o, c * P:(c + 1) * P],
                                          ones[:, 0:1], n == 0, n == 3)
                                n += 1
                last.then_inc(pe_done, made(("tapsum", l)))
                for n, (src, mat) in enumerate((("s", dftc_v[:, :, 0:P]), ("s", dftc_v[:, :, P:L]),
                                                ("d", dfts_v[:, :, 0:P]), ("d", dfts_v[:, :, P:L]),
                                                ("s", dftn_v[:, 0, :, :]))):
                    b = product(("spec", l, n))
                    pe.wait_ge(*due(("tapsd", l)))
                    rhs = taps_v[:, :, 0, :, :] if src == "s" else taps_v[:, :, 1, :, :]
                    for t in range(2):
                        last = mm(b[:, :], mat[:, t, :], rhs[:, t, :, :], t == 0, t == 1)
                    last.then_inc(pe_done, made(("spec", l, n)))
                stage_end(l, "mod")
                for k in range(KB):
                    for s in range(2):
                        b = product(("h1", l, k, s))
                        pe.wait_ge(*due(("xn", l, 1)))
                        for t in range(2):
                            last = nc.tensor.transpose(b[:, t * P:(t + 1) * P], xn_v[:, 2 * s + t, k::KB], ident[:, :])
                        last.then_inc(pe_done, made(("h1", l, k, s)))
                stage_end(l, "norm1")
                for y in range(2):
                    b = product(("gates", l, y))
                    pe.wait_ge(*due(("wg", l)))
                    for k in range(KB):
                        last = mm(b[:, :], wg_v[:, k, y, :], hT_v[:, k, :], k == 0, k == KB - 1)
                    last.then_inc(pe_done, made(("gates", l, y)))

                def channel_major(name, blocks, lo):
                    for q in range((blocks + 1) // 2):
                        pe.wait_ge(*due(("load", (name, l, q))))
                        w = slot((name, l, q), KB)
                        for i in range(min(2, blocks - 2 * q)):
                            blk = 2 * q + i
                            a0 = lo(blk)
                            b = product((name, l, blk))
                            for k in range(KB):
                                last = mm(b[:, a0:512], w[:, k, i * P:(i + 1) * P], hT_v[:, k, a0:512],
                                          k == 0, k == KB - 1)
                            used = [("used", (name, l, q))] if blk == min(2 * q + 1, blocks - 1) else []
                            last.then_inc(pe_done, made((name, l, blk), *used))

                def token_major(name, tiles):
                    pe.wait_ge(*due(("load", (name, l, 0))))
                    pe.wait_ge(*due(("load", (name, l, 1))))
                    for t in tiles:
                        b = product((name, l, t))
                        for q, (c0, c1) in enumerate(((0, 256), (256, 384))):
                            w = slot((name, l, q), KB)
                            for k in range(KB):
                                last = mm(b[:, c0:c1], hT_v[:, k, t * P:(t + 1) * P], w[:, k, 0:c1 - c0],
                                          k == 0, k == KB - 1)
                        used = [("used", (name, l, q)) for q in range(2)] if t == NT - 1 else []
                        last.then_inc(pe_done, made((name, l, t), *used))

                channel_major("qk", 6, lambda blk: n0 if blk < 3 else 0)
                channel_major("xbc", 5, lambda blk: 0)
                token_major("v", range(NT))
                token_major("z", range(t0, NT))
                token_major("o", range(t0, NT))
                channel_major("hy", 6, lambda blk: n0)
                for c in range(NT):
                    b = product(("xtok", l, c))
                    pe.wait_ge(*due(("xbc done", l)))
                    for blk in range(4):
                        last = nc.tensor.transpose(b[:, blk * P:(blk + 1) * P], xbc_v[:, blk, c * P:(c + 1) * P],
                                                   ident[:, :])
                    last.then_inc(pe_done, made(("xtok", l, c)))
                    b = product(("ktok", l, c))
                    pe.wait_ge(*due(("k done", l)))
                    for blk in range(3):
                        last = nc.tensor.transpose(b[:, blk * P:(blk + 1) * P], qk_v[:, 3 + blk, c * P:(c + 1) * P],
                                                   ident[:, :])
                    last.then_inc(pe_done, made(("ktok", l, c)))
                for c in range(NT):
                    b = product(("cols", l, c))
                    pe.wait_ge(*due(("rows", l)))
                    for q, r in enumerate((EX, ES, ND, RS)):
                        last = nc.tensor.transpose(b[:, q * P:(q + 1) * P], r[:, c * P:(c + 1) * P], ident[:, :])
                    last.then_inc(pe_done, made(("cols", l, c)))
                b = product(("dcb", l))
                pe.wait_ge(*due(("diag", l)))
                mm(b[:, :], ones[:, :], MX).then_inc(pe_done, made(("dcb", l)))
                stage_end(l, "inproj")

                units = [(i, d, i if d == 0 else BACK[i]) for i in range(NT) for d in range(2)]

                def weights_of(u):
                    i, d, c = units[u]
                    if c < t0:
                        return
                    ck = slice(c * P, (c + 1) * P)
                    for m in range(2):
                        r = slice(64 * m + 32 * d, 64 * m + 32 * d + 32)
                        for j in range(2):
                            b = product(("w", l, u, m, j))
                            mm(b[:, 0:384], ident16[:, :], mask_v[:, d:d + 1, :].broadcast_to([P, 3, P]), True, False)
                            pe.wait_ge(*due(("rlm", l, u)))
                            last = mm(b[:, 0:384], ones[r, :], rlm_v[r, u % 2, j, :, :], False, True)
                            last.then_inc(pe_done, made(("w", l, u, m, j)))
                    for g in range(2):
                        b = product(("cb", l, u, g))
                        mm(b[:, 0:P], xbc_v[64 * g:64 * g + 64, 3, ck], xbc_v[64 * g:64 * g + 64, 4, ck]).then_inc(pe_done, made(("cb", l, u, g)))
                    for j in range(2):
                        b = product(("qkp", l, u, j))
                        for q in range(3):
                            last = mm(b[:, q * P:(q + 1) * P], qk_v[64 * j:64 * j + 64, 3 + q, ck],
                                      qk_v[64 * j:64 * j + 64, q, ck])
                        last.then_inc(pe_done, made(("qkp", l, u, j)))

                def outputs_of(u):
                    i, d, c = units[u]
                    ck = slice(c * P, (c + 1) * P)
                    if c >= t0:
                        b = product(("ys", l, u))
                        pe.wait_ge(*due(("scores", l, u)))
                        pe.wait_ge(*due(("prep", l, u)))
                        for h in range(HEADS):
                            last = mm(b[:, h * HD:(h + 1) * HD], sc_v[:, u % 2, h // 3, (h % 3) * P:(h % 3 + 1) * P],
                                      xdt[:, h * HD:(h + 1) * HD])
                        last.then_inc(pe_done, made(("ys", l, u)))
                        b = product(("mn", l, u))
                        for h in range(HEADS):
                            last = mm(b[:, h * 65:h * 65 + 65],
                                      sc_v[:, u % 2, 2 + h % 2, (h // 2) * P:(h // 2 + 1) * P], va_v[:, c, h, :])
                        last.then_inc(pe_done, made(("mn", l, u)))
                        if i > 0:
                            b = product(("yi", l, u))
                            pe.wait_ge(*due(("state", l, u - 2)))
                            mm(b[:, 0:384], xbc_v[:, 4, ck], sst_v[:, d, :]).then_inc(pe_done, made(("yi", l, u)))
                            b = product(("mi", l, u))
                            for q in range(3):
                                last = mm(b[:, q * 130:q * 130 + 130], qk_v[:, q, ck], cst_v[:, d, q, :, :])
                            last.then_inc(pe_done, made(("mi", l, u)))
                    if i < NT - 1:
                        b = product(("ss", l, u))
                        pe.wait_ge(*due(("prep", l, u)))
                        for g in range(2):
                            last = mm(b[64 * g:64 * g + 64, 192 * g:192 * g + 192], xtok_v[:, c, 384 + 64 * g:384 + 64 * g + 64],
                                      xde[:, 192 * g:192 * g + 192])
                        last.then_inc(pe_done, made(("ss", l, u)))
                        b = product(("cs", l, u))
                        for h in range(HEADS):
                            j, q = h % 2, h // 2
                            last = mm(b[64 * j:64 * j + 64, h * 65:h * 65 + 65], ktok_v[:, c, h * HD:(h + 1) * HD],
                                      ve_v[:, h, :])
                        last.then_inc(pe_done, made(("cs", l, u)))

                weights_of(0)
                for u in range(len(units)):
                    if u + 1 < len(units):
                        weights_of(u + 1)
                    outputs_of(u)
                    if l == 0:
                        for ml, n in MOD_LATER[u * MOD_PER_UNIT:(u + 1) * MOD_PER_UNIT]:
                            modulation(ml, n)
                stage_end(l, "units")
                for t in range(t0, NT):
                    b = product(("yst", l, t))
                    pe.wait_ge(*due(("ssd out", l, t)))
                    for blk in range(3):
                        last = nc.tensor.transpose(b[:, blk * P:(blk + 1) * P], ys_v[:, t, blk * P:(blk + 1) * P],
                                                   ident[:, :])
                    last.then_inc(pe_done, made(("yst", l, t)))
                    b = product(("ymt", l, t))
                    pe.wait_ge(*due(("ml out", l, t)))
                    for blk in range(3):
                        last = nc.tensor.transpose(b[:, blk * P:(blk + 1) * P], hs_v[:, t, blk * P:(blk + 1) * P],
                                                   ident[:, :])
                    last.then_inc(pe_done, made(("ymt", l, t)))
                stage_end(l, "final")
                streams = range(0 if l == 0 else 1, 2)
                for o in range(2):
                    for s in streams:
                        b = product(("hz", l, o, s))
                        pe.wait_ge(*due(("hy z", l, o)))
                        for t in range(2):
                            for c in range(2):
                                last = nc.tensor.transpose(b[:, t * L + c * P:t * L + (c + 1) * P],
                                                           hy_v[:, c, s * L + t * P:s * L + (t + 1) * P], ident[:, :])
                        last.then_inc(pe_done, made(("hz", l, o, s)))
                    for n, mat in enumerate((dftc_v[:, :, 0:P], dftn_v[:, 1, :, :], dftc_v[:, :, P:L],
                                             dfts_v[:, :, P:L])):
                        b = product(("zf", l, o, n))
                        pe.wait_ge(*due(("zt", l, o)))
                        for t in range(2):
                            last = mm(b[:, n0:512], mat[:, t, :], zt_v[:, t, n0:512], t == 0, t == 1)
                        last.then_inc(pe_done, made(("zf", l, o, n)))
                    for c in range(2):
                        b = product(("yt", l, o, c))
                        pe.wait_ge(*due(("yf", l, o)))
                        for s in streams:
                            for q in range(4):
                                inv = invc_v if q < 2 else invs_v
                                last = mm(b[:, s * L:(s + 1) * L], yf_v[:, q, s * L + c * P:s * L + (c + 1) * P],
                                          inv[:, q % 2, :], q == 0, q == 3)
                        last.then_inc(pe_done, made(("yt", l, o, c)))
                stage_end(l, "hyena")
                for s in streams:
                    for q in range(2):
                        b = product(("grow", l, 0, s, q))
                        pe.wait_ge(*due(("gdiag", l, 0, s)))
                        mm(b[:, :], ones[:, :], hsum[:, 512 * q:512 * q + 512]).then_inc(pe_done, made(("grow", l, 0, s, q)))
                for q in range(4):
                    pe.wait_ge(*due(("load", ("wout", l, q))))
                for t in range(t0, NT):
                    for half in range(2):
                        b = product(("out", l, t, half))
                        for q in range(2):
                            w = slot(("wout", l, 2 * half + q), KB)
                            for k in range(KB):
                                last = mm(b[:, 256 * q:256 * q + 256], yT_v[:, k, t * P:(t + 1) * P], w[:, k, :],
                                          k == 0, k == KB - 1)
                        used = [("used", ("wout", l, q)) for q in range(4)] if (t, half) == (NT - 1, 1) else []
                        last.then_inc(pe_done, made(("out", l, t, half), *used))
                stage_end(l, "outproj")
                for k in range(KB):
                    for s in streams:
                        b = product(("h2", l, k, s))
                        pe.wait_ge(*due(("xn", l, 2)))
                        for t in range(2):
                            last = nc.tensor.transpose(b[:, t * P:(t + 1) * P], xn_v[:, 2 * s + t, k::KB], ident[:, :])
                        last.then_inc(pe_done, made(("h2", l, k, s)))
                b = product(("router", l))
                pe.wait_ge(*due(("h2T", l, "act")))
                pe.wait_ge(*due(("h2T", l, "dve")))
                for t in range(t0, NT):
                    for k in range(KB):
                        last = mm(b[:, t * 36:t * 36 + 36], hT_v[:, k, t * P:(t + 1) * P], rw_v[:, k, :],
                                  k == 0, k == KB - 1)
                last.then_inc(pe_done, made(("router", l)))
                for s in streams:
                    for q in range(2):
                        b = product(("grow", l, 1, s, q))
                        pe.wait_ge(*due(("gdiag", l, 1, s)))
                        mm(b[:, :], ones[:, :], hsum[:, 512 * q:512 * q + 512]).then_inc(pe_done, made(("grow", l, 1, s, q)))
                stage_end(l, "router")

                base = len(products)
                tag = ("moe", l)
                per_turn = PER_BODY * (4 + 2 * (NT - t0))
                body_names = []
                before = dict(tally.count)
                with pe.Fori(0, BODIES) as i:
                    tally.turn = (tag, i)

                    def turn_product(name):
                        n = len(body_names)
                        body_names.append(name)
                        at[("bank", name)] = (base + n) % BANKS
                        if n >= BANKS:
                            pe.wait_ge(*due(("read", body_names[n - BANKS])))
                        else:
                            pe.wait_ge(*due(("read", ("turn", l, per_turn - BANKS + n)), 1))
                        return banks[(base + n) % BANKS]

                    for j in range(PER_BODY):
                        for f in range(2):
                            for y in range(2):
                                key = ("expert", l, 3 * j + y)
                                n = len(body_names)
                                b = turn_product(("turn", l, n))
                                if f == 0:
                                    pe.wait_ge(*due(("load", key)))
                                w = slot(key, KB)
                                for k in range(KB):
                                    last = mm(b[:, n0:512], w[:, k, f * P:(f + 1) * P], hT_v[:, k, n0:512],
                                              k == 0, k == KB - 1)
                                last.then_inc(pe_done, made(("turn", l, n), *([("used", key)] if f == 1 else [])))
                        key = ("expert", l, 3 * j + 2)
                        pe.wait_ge(*due(("load", key)))
                        w = slot(key, 2)
                        pe.wait_ge(*due(("hid", l, j)))
                        for t in range(t0, NT):
                            for half in range(2):
                                n = len(body_names)
                                b = turn_product(("turn", l, n))
                                for f in range(2):
                                    last = mm(b[:, :], hid_v[:, j % 2, f, t * P:(t + 1) * P],
                                              w[:, f, 512 * half:512 * half + 512], f == 0, f == 1)
                                last.then_inc(pe_done, made(("turn", l, n), *([("used", key)] if (t, half) == (NT - 1, 1) else [])))
                tally.looped(tag, before, BODIES)
                per = at[("per", tag, "pe_done")]
                for j in range(3 * PER_BODY):
                    at[("used", ("expert-last", l, j))] = (
                        "pe_done", at[("used", ("expert", l, j))][1] + per * (BODIES - 1))
                for n in range(per_turn):
                    products.append(("turn", l, n))
                stage_end(l, "moe")

        def consumer(who, eng, sem_name):
            done = tally.sems[sem_name]

            def step(ins, *names):
                ins.then_inc(done, tick(sem_name, ("own", who), *names))
                eng.wait_ge(*due(("own", who)))

            def bank(name):
                return banks[at[("bank", name)]]

            def stage_end(l, stage):
                eng.drain().then_inc(done, tick(sem_name, ("end", who, l, stage)))
                for other in ("pe", "act", "dve"):
                    if other != who:
                        eng.wait_ge(*due(("end", other, l, stage)))
            return step, bank, stage_end

        @block.scalar
        def _(act):
            step, bank, stage_end = consumer("act", act, "act_done")

            def fn(o, i, f, *names, **k):
                step(nc.scalar.activation(o, i, f, **k), *names)

            act.wait_ge(*due(("consts_in",)))
            fn(cond[:, :], cond[:, :], ACT.Silu, ("cond",))
            def mod_rows(l, n):
                act.wait_ge(*due(("made", ("mod", l, n))))
                if n % 2 == 0 and (l, n) != (0, 0):
                    pl, pn = (l, n - 2) if n else (l - 1, MOD_SLOTS - 2)
                    act.wait_ge(*due(("made", ("modc", pl, pn // 4, pn % 4 // 2))))
                fn(modrow[0:2, 256 * (n % 2):256 * (n % 2) + 256], bank(("mod", l, n))[0:2, 0:256], ACT.Copy,
                   ("read", ("mod", l, n)), ("modrow", l, n))

            for l in range(DEPTH):
                t0 = 0 if l == 0 else 2
                n0 = t0 * P
                if l == 0:
                    for n in range(MOD_FIRST):
                        mod_rows(0, n)
                for n in range(2):
                    act.wait_ge(*due(("ranged", l, n)))
                    fn(hid_c[0:FH, :], hid_b[0:FH, :], ACT.Sin, ("sin", l, n))
                act.wait_ge(*due(("decay", l)))
                for t in range(2):
                    fn(tabs_v[:, t, :, :, :], grow[:, 0:1024].rearrange("p (e o c) -> p e o c", e=2, o=2), ACT.Exp,
                       ("window", l, t), scale=tcol[:, t:t + 1])
                act.wait_ge(*due(("tapped", l)))
                fn(tabs_v[:, :, :, :, :], taps_v[:, :, :, :, :], ACT.Abs, ("tabs", l))
                stage_end(l, "mod")

                def square_sums(n, src):
                    for t in range(t0 if n != 1 else 0, NT):
                        fn(hsum[:, 0:D], src[:, t, :], ACT.Square, ("ss", l, n, t), accum_out=small[:, t:t + 1])
                    act.wait_ge(*due(("rinv", l, n)))
                    fn(small[:, 4:8], small[:, 4:8], ACT.Sqrt, ("rstd", l, n))

                act.wait_ge(*due(("x_in",)))
                square_sums(1, x_v)
                for k in range(KB):
                    act.wait_ge(*due(("made", ("h1", l, k, 0))))
                    b = bank(("h1", l, k, 0))
                    fn(hT_v[:, k, 0:L], b[:, 0:L], ACT.Identity, ("read", ("h1", l, k, 0)),
                       scale=ab_v[:, 0, k, 1:2], bias=ab_v[:, 1, k, 1:2])
                stage_end(l, "norm1")
                act.wait_ge(*due(("g1", l)))
                fn(t1, U, ACT.Exp, ("g2", l))
                fn(t2, t1, ACT.Ln, ("g3", l), bias=1.0)
                fn(gcolp[:, 3:4], gcolp[:, 2:3], ACT.Exp, ("acoef", l))
                act.wait_ge(*due(("g4", l)))
                fn(EX, U, ACT.Exp)
                for c in range(NT):
                    fn(ES[:, c * P:(c + 1) * P], RS[:, c * P:(c + 1) * P], ACT.Exp, bias=small[:, 8 + c:9 + c])
                fn(ND[64:128, :], MX[64:128, :], ACT.Exp, ("rows", l), scale=-1.0)
                for blk in range(6):
                    a0 = n0 if blk < 3 else 0
                    act.wait_ge(*due(("conv", "qk", l, blk)))
                    fn(qk_v[:, blk, a0:512], qk_v[:, blk, a0:512], ACT.Silu, ("silu qk", l, blk))
                for blk in range(5):
                    act.wait_ge(*due(("conv", "xbc", l, blk)))
                    fn(xbc_v[:, blk, :], xbc_v[:, blk, :], ACT.Silu, ("xbc done", l))
                for t in range(NT):
                    act.wait_ge(*due(("made", ("v", l, t))))
                    b = bank(("v", l, t))
                    fn(va_v[:, t, :, 0:HD], b[:, 0:384].rearrange("p (h c) -> p h c", h=HEADS), ACT.Copy,
                       ("read", ("v", l, t)))
                for t in range(t0, NT):
                    act.wait_ge(*due(("made", ("z", l, t))))
                    b = bank(("z", l, t))
                    fn(z_v[:, t, :], b[:, 0:384], ACT.Silu, ("read", ("z", l, t)))
                for t in range(t0, NT):
                    act.wait_ge(*due(("made", ("o", l, t))))
                    b = bank(("o", l, t))
                    fn(o_v[:, t, :], b[:, 0:384], ACT.Sigmoid, ("read", ("o", l, t)))
                for c in range(NT):
                    act.wait_ge(*due(("made", ("xtok", l, c))))
                    b = bank(("xtok", l, c))
                    fn(xtok_v[:, c, :], b[:, :], ACT.Copy, ("read", ("xtok", l, c)))
                    act.wait_ge(*due(("made", ("ktok", l, c))))
                    b = bank(("ktok", l, c))
                    fn(ktok_v[:, c, :], b[:, 0:384], ACT.Copy, ("read", ("ktok", l, c)))
                for c in range(NT):
                    act.wait_ge(*due(("made", ("cols", l, c))))
                    b = bank(("cols", l, c))
                    fn(cols_v[:, c, :, :], b[:, :], ACT.Copy, ("read", ("cols", l, c)))
                act.wait_ge(*due(("made", ("dcb", l))))
                b = bank(("dcb", l))
                fn(dcb[:, :], b[:, :], ACT.Copy, ("read", ("dcb", l)))
                stage_end(l, "inproj")
                units = [(i, d, i if d == 0 else BACK[i]) for i in range(NT) for d in range(2)]
                def segments(u):
                    i, d, c = units[u]
                    if c < t0:
                        return
                    for m in range(2):
                        for j in range(2):
                            act.wait_ge(*due(("made", ("w", l, u, m, j))))
                            b = bank(("w", l, u, m, j))
                            if u >= 2 and units[u - 2][2] >= t0:
                                act.wait_ge(*due(("made", ("mn", l, u - 2))))
                            for q in range(3):
                                h = 3 * j + q if m == 0 else 2 * q + j
                                names = [("read", ("w", l, u, m, j)), ("seg", l, u, m, j)] if q == 2 else []
                                fn(sc_v[:, u % 2, 2 * m + j, q * P:(q + 1) * P], b[:, q * P:(q + 1) * P], ACT.Exp,
                                   *names, bias=cols_v[:, c, 3, 64 * m + 32 * d + h:64 * m + 32 * d + h + 1])

                segments(0)
                for u in range(len(units)):
                    if u + 1 < len(units):
                        segments(u + 1)
                    if l == 0:
                        for ml, n in MOD_LATER[u * MOD_PER_UNIT:(u + 1) * MOD_PER_UNIT]:
                            mod_rows(ml, n)
                stage_end(l, "units")
                for t in range(t0, NT):
                    act.wait_ge(*due(("gated", l, t)))
                    fn(wv[:, 0:384], ys_v[:, t, :], ACT.Square, ("ssq", l, t), accum_out=small[:, t:t + 1])
                act.wait_ge(*due(("rinv", l, 3)))
                fn(small[:, 4:8], small[:, 4:8], ACT.Sqrt, ("rstd", l, 3))
                act.wait_ge(*due(("rinv", l, 4)))
                fn(small[:, 12:12 + 6 * NT], small[:, 12:12 + 6 * NT], ACT.Sqrt, ("rstd", l, 4))
                for t in range(t0, NT):
                    for name, row, y0 in (("yst", 68, 0), ("ymt", 71, 5)):
                        act.wait_ge(*due(("made", (name, l, t))))
                        b = bank((name, l, t))
                        for blk in range(3):
                            names = [("read", (name, l, t))] if blk == 2 else []
                            o, i_ = yT_v[:, y0 + blk, t * P:(t + 1) * P], b[:, blk * P:(blk + 1) * P]
                            if l % 2:
                                w0 = (t - 2) * P // ROWS
                                o = yT_v[:, y0 + blk, L:2 * L].rearrange("p (r w) -> p w r", r=ROWS)[
                                    :, w0:w0 + P // ROWS, :]
                                i_ = i_.rearrange("p (w r) -> p w r", r=ROWS)
                            fn(o, i_, ACT.Copy, *names,
                               scale=pcol[:, row + blk:row + blk + 1])
                stage_end(l, "final")
                streams = range(0 if l == 0 else 1, 2)
                for o in range(2):
                    for s in streams:
                        act.wait_ge(*due(("made", ("hz", l, o, s))))
                        b = bank(("hz", l, o, s))
                        names = [("zt", l, o)] if s == 1 else []
                        fn(zt_v[:, :, s * L:(s + 1) * L], b[:, :].rearrange("p (t c) -> p t c", t=2), ACT.Copy,
                           ("read", ("hz", l, o, s)), *names)
                stage_end(l, "hyena")
                for s in streams:
                    for q in range(2):
                        act.wait_ge(*due(("made", ("grow", l, 0, s, q))))
                        b = bank(("grow", l, 0, s, q))
                        fn(grow_v[:, s, :].rearrange("p (j k) -> p k j", k=KB)[:, 4 * q:4 * q + 4, :], b[:, :].rearrange(
                            "p (k j) -> p k j", k=4), ACT.Copy, ("read", ("grow", l, 0, s, q)), ("grow in", l, 0, s))
                stage_end(l, "outproj")
                square_sums(2, x_v)
                if l == 0:
                    for k in range(KB):
                        act.wait_ge(*due(("made", ("h2", l, k, 0))))
                        b = bank(("h2", l, k, 0))
                        fn(hT_v[:, k, 0:L], b[:, 0:L], ACT.Identity, ("read", ("h2", l, k, 0)),
                           scale=ab_v[:, 2, k, 1:2], bias=ab_v[:, 3, k, 1:2])
                step(nc.scalar.activation(small[:, 40:41], small[:, 4:5], ACT.Copy), ("h2T", l, "act"))
                act.wait_ge(*due(("r1", l)))
                fn(otok[:, 0:16], otok[:, 0:16], ACT.Exp, ("r2", l))
                act.wait_ge(*due(("r3", l)))
                fn(otok[:, 16:20], otok[:, 16:20], ACT.Exp, ("r4", l))
                for s in streams:
                    for q in range(2):
                        act.wait_ge(*due(("made", ("grow", l, 1, s, q))))
                        b = bank(("grow", l, 1, s, q))
                        fn(grow_v[:, s, :].rearrange("p (j k) -> p k j", k=KB)[:, 4 * q:4 * q + 4, :], b[:, :].rearrange(
                            "p (k j) -> p k j", k=4), ACT.Copy, ("read", ("grow", l, 1, s, q)), ("grow in", l, 1, s))
                stage_end(l, "router")
                tag = ("moe", l)
                n_down = 2 * (NT - t0)
                before = dict(tally.count)
                with act.Fori(0, BODIES) as i:
                    tally.turn = (tag, i)
                    for j in range(PER_BODY):
                        for f in range(2):
                            n = j * (4 + n_down) + 2 * f
                            act.wait_ge(*due(("made", ("turn", l, n))))
                            b = bank(("turn", l, n))
                            if j:
                                act.wait_ge(*due(("hidf", l, j - 1, f)))
                            else:
                                act.wait_ge(*due(("hidf", l, PER_BODY - 1, f), 1))
                            fn(sg_v[:, f, n0:512], b[:, n0:512], ACT.Silu, ("read", ("turn", l, n)), ("sg", l, j, f))
                tally.looped(tag, before, BODIES)
                stage_end(l, "moe")
            t0 = 2
            for t in range(2, NT):
                act.wait_ge(*due(("x done", DEPTH - 1)))
                fn(hsum[:, 0:D], x_v[:, t, :], ACT.Square, ("ss", "f", t), accum_out=small[:, t:t + 1])
            act.wait_ge(*due(("rinv", "f")))
            fn(small[:, 4:8], small[:, 4:8], ACT.Sqrt, ("rstd", "f"), ("fnw free",))

        @block.vector
        def _(dve):
            step, bank, stage_end = consumer("dve", dve, "dve_done")
            V = nc.vector

            def ts(o, a, s1, s2, op0, op1, *names):
                step(V.tensor_scalar(o, a, s1, s2, op0, op1) if op1 is not None else
                     V.tensor_scalar(o, a, s1, None, op0), *names)

            def tt(o, a, b, op, *names):
                step(V.tensor_tensor(o, a, b, op), *names)

            def stt(o, a, s, b, op0, op1, *names):
                step(V.scalar_tensor_tensor(o, a, s, b, op0, op1), *names)

            def copy(o, a, *names):
                step(V.tensor_copy(o, a), *names)

            MUL, ADD, SUB, MAX, MIN = ALU.mult, ALU.add, ALU.subtract, ALU.max, ALU.min

            step(V.memset(gcolp[:, :], 0.0), ("gcolp zero",))
            step(V.memset(ones[:, :], 1.0))
            dve.wait_ge(*due(("consts_in",)))
            copy(ident16[:, :], ident[:, :])
            copy(mask16[:, :], big[:, 0:2 * P])
            step(V.memset(vaug[:, :], 1.0))
            step(V.memset(sst[:, :], 0.0))
            step(V.memset(cst[:, :], 0.0))
            step(V.memset(small[:, :], 1.0))
            step(V.memset(hT[:, :], 0.0))
            def mod_columns(l, n):
                m, h = n // 4, n % 4 // 2
                r = slice(64 * h, 64 * h + 64)
                dve.wait_ge(*due(("made", ("modc", l, m, h))))
                tt(modc_v[r, l, m, :, :], bank(("modc", l, m, h))[0:64, 0:16].rearrange("p (k s) -> p k s", s=2),
                   bmod_v[r, l, m, :].unsqueeze(2).broadcast_to([64, KB, 2]), ADD, ("read", ("modc", l, m, h)))

            for l in range(DEPTH):
                t0 = 0 if l == 0 else 2
                n0 = t0 * P
                streams = range(0 if l == 0 else 1, 2)

                def modulators(n):
                    stt(ab_v[:, 2 * n, :, :], modc_v[:, l, 3 * n + 1, :, :], 1.0,
                        nw_v[:, n, :].unsqueeze(2).broadcast_to([P, KB, 2]), ADD, MUL)
                    copy(ab_v[:, 2 * n + 1, :, :], modc_v[:, l, 3 * n, :, :], ("ab", l))

                dve.wait_ge(*due((f"params{l}_in",)))
                dve.wait_ge(*due(("made", ("pcol", l))))
                b = bank(("pcol", l))
                copy(pcol[:, 0:78], b[:, 0:78], ("read", ("pcol", l)))
                stt(grow[:, 0:1024], grow[:, 0:1024], -1.0, grow[:, 0:1024], MUL, MAX, ("decay", l))
                step(V.memset(wg, 0.0))
                for d in range(2):
                    copy(wg_v[:, :, 0, 32 * d:32 * d + 6], wgr_v[:, :, 6 * d:6 * d + 6])
                    copy(wg_v[:, :, 1, 64 + 32 * d:70 + 32 * d], wgr_v[:, :, 12 + 12 * d:18 + 12 * d])
                    copy(wg_v[:, :, 0, 64 + 32 * d:70 + 32 * d], wgr_v[:, :, 18 + 12 * d:24 + 12 * d], ("wg", l))
                if l == 0:
                    for n in range(1, MOD_FIRST, 2):
                        mod_columns(0, n)
                modulators(0)
                two_pi = 2 * np.pi
                c1 = 6.28125
                c2 = float(np.float32(two_pi - c1))
                c3 = float(np.float32(two_pi - c1 - c2))
                for n in range(2):
                    dve.wait_ge(*due(("made", (f"hid{n + 1}", l))))
                    b = bank((f"hid{n + 1}", l))
                    a, k_ = hid_b[0:FH, :], hid_a[0:FH, :]
                    ts(a, b[0:FH, 0:L], hcol[0:FH, n:n + 1], hcol[0:FH, 2:3], ADD, MUL, ("read", (f"hid{n + 1}", l)))
                    ts(k_, a, 1.0 / two_pi, MAGIC, MUL, ADD)
                    ts(k_, k_, MAGIC, None, SUB, None)
                    for cc in (c1, c2, c3):
                        stt(a, k_, -cc, a, MUL, ADD)
                    ts(a, a, 3.1415925, -3.1415925, MIN, MAX, ("ranged", l, n))
                for t in range(2):
                    for e in range(2):
                        dve.wait_ge(*due(("window", l, t)))
                        dve.wait_ge(*due(("made", ("taps", l, t, e))))
                        b = bank(("taps", l, t, e))
                        tt(taps_v[:, t, e, :, :], tabs_v[:, t, e, :, :], b[:, :].rearrange("p (o c) -> p o c", o=2), MUL,
                           ("read", ("taps", l, t, e)))
                ts(taps_v[:, 0, 1, :, :], taps_v[:, 0, 1, :, :], tcol[:, 2:3], None, MUL, None, ("tapped", l))
                dve.wait_ge(*due(("tabs", l)))
                hd = tabs_v[:, :, 0, :, :]
                dve.wait_ge(*due(("made", ("tapsum", l))))
                for t in range(2):
                    tt(hd[:, t], taps_v[:, t, 0], taps_v[:, t, 1], SUB)
                    tt(taps_v[:, t, 0], taps_v[:, t, 0], taps_v[:, t, 1], ADD)
                    copy(taps_v[:, t, 1], hd[:, t], ("tapsd", l))
                dve.wait_ge(*due(("made", ("tapsum", l))))
                b = bank(("tapsum", l))
                step(V.reciprocal(small[:, 44:48], b[:, 0:4]), ("read", ("tapsum", l)))
                for n in range(5):
                    dve.wait_ge(*due(("made", ("spec", l, n))))
                    b = bank(("spec", l, n))
                    copy(hf_v[:, n, :], b[:, :], ("read", ("spec", l, n)))
                stage_end(l, "mod")

                def rms(n, src, cols_, width, tiles, name=None):
                    ts(small[:, 4:8], small[:, 0:4], 1.0 / width, EPS, MUL, ADD)
                    step(V.reciprocal(small[:, 4:8], small[:, 4:8]), n)

                def norm(n, first_tile):
                    for t in range(first_tile, NT):
                        dve.wait_ge(*due(("ss", l, n, t)))
                    rms(("rinv", l, n), None, None, D, None)
                    dve.wait_ge(*due(("rstd", l, n)))
                    for t in range(first_tile, NT):
                        ts(xn_v[:, t, :], x_v[:, t, :], small[:, 4 + t:5 + t], None, MUL, None, ("xn", l, n))

                norm(1, 0)
                for k in range(KB):
                    dve.wait_ge(*due(("made", ("h1", l, k, 1))))
                    b = bank(("h1", l, k, 1))
                    o = hT_v[:, k, L:2 * L]
                    i_ = b[:, 0:L]
                    if l % 2:
                        o = o.rearrange("p (w r) -> p r w", r=ROWS)
                        i_ = i_.rearrange("p (r w) -> p r w", r=ROWS)
                    ts(o, i_, ab_v[:, 0, k, 0:1], ab_v[:, 1, k, 0:1], MUL, ADD, ("read", ("h1", l, k, 1)))
                stage_end(l, "norm1")
                dve.wait_ge(*due(("made", ("gates", l, 0))))
                b = bank(("gates", l, 0))
                sp_in, na = t3, U
                ts(sp_in, b[:, :], gcolp[:, 0:1], tcol[:, 3:4], ADD, MUL, ("read", ("gates", l, 0)))
                stt(na, sp_in, -1.0, sp_in, MUL, MIN, ("g1", l))
                dve.wait_ge(*due(("g3", l)))
                dve.wait_ge(*due(("acoef", l)))
                ts(SP, t1, 1.0, None, ADD, None)
                stt(U, SP, -1.0, t1, ADD, SUB)
                step(V.reciprocal(SP, SP))
                tt(U, U, SP, MUL)
                tt(t2, t2, U, SUB)
                stt(SP, sp_in, 0.0, t2, MAX, ADD)
                stt(t1, SP, -1.0, gcolp[:, 3:4].broadcast_to([P, 512]), MUL, MUL)
                for m in range(2):
                    f, r = slice(64 * m, 64 * m + 32), slice(64 * m + 32, 64 * m + 64)
                    step(V.tensor_tensor_scan(CUM[f, :], keep[f, :], t1[f, :], 0.0, MUL, ADD))
                    step(V.tensor_tensor_scan(CUM[r, ::-1], keep[r, ::-1], t1[r, ::-1], 0.0, MUL, ADD))
                s_, m_ = slice(0, 64), slice(64, 128)
                copy(RL[s_, :], CUM[s_, :])
                ts(RS[s_, :], CUM[s_, :], -1.0, None, MUL, None)
                copy(ND[s_, :], SP[s_, :])
                dve.wait_ge(*due(("made", ("gates", l, 1))))
                b = bank(("gates", l, 1))
                stt(RS[m_, :], b[m_, :], gcolp[m_, 1:2], CUM[m_, :], ADD, SUB, ("read", ("gates", l, 1)))
                step(V.memset(t2[m_, :], 0.0))
                copy(t2[64:96, P::P], CUM[64:96, P - 1:511:P])
                for a, z in ((127, 128), (511, 0), (383, 384)):
                    copy(t2[96:128, a:a + 1], CUM[96:128, z:z + 1])
                step(V.tensor_tensor_scan(MX[64:96, :], t2[64:96, :], RS[64:96, :], 0.0, ADD, MAX))
                step(V.tensor_tensor_scan(MX[96:128, 255::-1], t2[96:128, 255::-1], RS[96:128, 255::-1], 0.0, ADD, MAX))
                step(V.tensor_tensor_scan(MX[96:128, 511:255:-1], t2[96:128, 511:255:-1], RS[96:128, 511:255:-1],
                                          MX[96:128, 0:1], ADD, MAX))
                ts(RL[m_, :], MX[m_, :], -1.0, None, MUL, None)
                mc = small[:, 36:40]
                step(V.memset(mc[m_, :], 0.0))
                tt(mc[64:96, 1:4], CUM[64:96, P - 1:511:P], MX[64:96, P - 1:511:P], ADD)
                for c, z in ((0, 128), (3, 0), (2, 384)):
                    tt(mc[96:128, c:c + 1], CUM[96:128, z:z + 1], MX[96:128, z:z + 1], ADD)
                copy(U[s_, :], CUM[s_, :])
                for c in range(NT):
                    ts(U[m_, c * P:(c + 1) * P], RL[m_, c * P:(c + 1) * P], mc[m_, c:c + 1], None, ADD, None)
                for m in range(2):
                    copy(small[64 * m:64 * m + 32, 8:12], RL[64 * m:64 * m + 32, P - 1::P])
                    copy(small[64 * m + 32:64 * m + 64, 8:12], RL[64 * m + 32:64 * m + 64, 0::P])
                tt(MX[m_, :], MX[m_, :], CUM[m_, :], ADD, ("g4", l))
                def conv(name, blk, dst, w0, b0, nb, lo):
                    dve.wait_ge(*due(("made", (name, l, blk))))
                    b = bank((name, l, blk))
                    o = dst[:, blk, :].rearrange("p (s n) -> p s n", s=2)[:, lo:, :]
                    i_ = b[:, :].rearrange("p (s n) -> p s n", s=2)[:, lo:, :]
                    wc = [pcol[:, w0 + nb * k + blk:w0 + nb * k + blk + 1] for k in range(3)]
                    ts(o, i_, wc[1], pcol[:, b0 + blk:b0 + blk + 1], MUL, ADD)
                    stt(o[:, :, 1:L], i_[:, :, 0:L - 1], wc[0], o[:, :, 1:L], MUL, ADD)
                    stt(o[:, :, 0:L - 1], i_[:, :, 1:L], wc[2], o[:, :, 0:L - 1], MUL, ADD,
                        ("read", (name, l, blk)), ("conv", name, l, blk))

                for blk in range(6):
                    conv("qk", blk, qk_v, 44, 62, 6, t0 // 2 if blk < 3 else 0)
                for blk in range(3, 6):
                    dve.wait_ge(*due(("silu qk", l, blk)))
                    ts(qk_v[:, blk, :], qk_v[:, blk, :], HD ** -0.5, None, MUL, None, ("k done", l))
                for blk in range(5):
                    conv("xbc", blk, xbc_v, 0, 15, 5, 0)
                for blk in range(6):
                    conv("hy", blk, hy_v, 20, 38, 6, t0 // 2)
                dve.wait_ge(*due(("rows", l)))
                last_ex = small[:, 48:52]
                for m in range(2):
                    copy(last_ex[64 * m:64 * m + 32, :], EX[64 * m:64 * m + 32, P - 1::P])
                    copy(last_ex[64 * m + 32:64 * m + 64, :], EX[64 * m + 32:64 * m + 64, 0::P])
                tt(MX.rearrange("p (c r) -> p c r", c=NT), ident[:, :].unsqueeze(1).broadcast_to([P, NT, P]),
                   last_ex.unsqueeze(2).broadcast_to([P, NT, P]), MUL, ("diag", l))
                stage_end(l, "inproj")

                units = [(i, d, i if d == 0 else BACK[i]) for i in range(NT) for d in range(2)]
                written = set()

                def spread(u):
                    i, d, c = units[u]
                    if c < t0:
                        return
                    if u >= 2 and units[u - 2][2] >= t0:
                        dve.wait_ge(*due(("made", ("w", l, u - 2, 1, 1))))
                    for j in range(2):
                        tt(rlm_v[:, u % 2, j, :, :], sel_v[:, j, :, :],
                           RL[:, c * P:(c + 1) * P].unsqueeze(1).broadcast_to([P, 3, P]), MUL, ("rlm", l, u))

                def scores(u):
                    i, d, c = units[u]
                    if c < t0:
                        return
                    for g in range(2):
                        dve.wait_ge(*due(("made", ("cb", l, u, g))))
                        b = bank(("cb", l, u, g))
                        dve.wait_ge(*due(("seg", l, u, 0, g)))
                        s3 = sc_v[:, u % 2, g, :].rearrange("p (i n) -> p i n", i=3)
                        tt(s3, s3, b[:, 0:P].unsqueeze(1).broadcast_to([P, 3, P]), MUL, ("read", ("cb", l, u, g)))
                    for j in range(2):
                        dve.wait_ge(*due(("made", ("qkp", l, u, j))))
                        b = bank(("qkp", l, u, j))
                        dve.wait_ge(*due(("seg", l, u, 1, j)))
                        tt(sc_v[:, u % 2, 2 + j, :], sc_v[:, u % 2, 2 + j, :], b[:, 0:384], MUL,
                           ("read", ("qkp", l, u, j)), ("scores", l, u))

                def col(c, kind, r0, n, width, step_=1):
                    return cols_v[:, c, kind, r0:r0 + n * step_ - (step_ - 1):step_].unsqueeze(2).broadcast_to(
                        [P, n, width])

                def prep(u):
                    i, d, c = units[u]
                    if u:
                        pi, pd, pc = units[u - 1]
                        if pi < NT - 1:
                            dve.wait_ge(*due(("made", ("cs", l, u - 1))))
                        elif pc >= t0:
                            dve.wait_ge(*due(("made", ("ys", l, u - 1))))
                    x3 = xtok_v[:, c, 0:384].rearrange("p (h c) -> p h c", h=HEADS)
                    xd3 = xdt.rearrange("p (h c) -> p h c", h=HEADS)
                    tt(xd3, x3, col(c, 2, 32 * d, 6, HD), MUL)
                    tt(xde.rearrange("p (h c) -> p h c", h=HEADS), xd3, col(c, 1, 32 * d, 6, HD), MUL)
                    tt(ve_v, va_v[:, c, :, :], col(c, 1, 64 + 32 * d, 6, 65), MUL, ("prep", l, u))

                def combine(u):
                    i, d, c = units[u]
                    if c >= t0:
                        dve.wait_ge(*due(("made", ("ys", l, u))))
                        b = bank(("ys", l, u))
                        y = ys_v[:, c, :]
                        if ("y", c) in written:
                            tt(y, b[:, 0:384], y, ADD, ("read", ("ys", l, u)))
                        else:
                            copy(y, b[:, 0:384], ("read", ("ys", l, u)))
                        written.add(("y", c))
                        if i > 0:
                            dve.wait_ge(*due(("made", ("yi", l, u))))
                            b = bank(("yi", l, u))
                            tt(nds[:, 0:384].rearrange("p (h c) -> p h c", h=HEADS),
                               b[:, 0:384].rearrange("p (h c) -> p h c", h=HEADS), col(c, 0, 32 * d, HEADS, HD), MUL,
                               ("read", ("yi", l, u)))
                            tt(y, y, nds[:, 0:384], ADD)
                            dve.wait_ge(*due(("made", ("mi", l, u))))
                            b = bank(("mi", l, u))
                            tt(nds_v, b[:, 0:390].rearrange("p (h c) -> p h c", h=HEADS),
                               col(c, 0, 64 + 32 * d, HEADS, 65), MUL, ("read", ("mi", l, u)))
                            dve.wait_ge(*due(("made", ("mn", l, u))))
                            b = bank(("mn", l, u))
                            tt(nds, b[:, 0:390], nds, ADD, ("read", ("mn", l, u)))
                        else:
                            dve.wait_ge(*due(("made", ("mn", l, u))))
                            b = bank(("mn", l, u))
                            copy(nds, b[:, 0:390], ("read", ("mn", l, u)))
                        den = small[:, 54:60]
                        stt(den, nds_v[:, :, 64], -1.0, nds_v[:, :, 64], MUL, MAX)
                        tt(den, den, cols_v[:, c, 2, 64 + 32 * d:70 + 32 * d], MAX)
                        step(V.reciprocal(den, den))
                        den3 = den.unsqueeze(2).broadcast_to([P, HEADS, HD])
                        h3 = hs_v[:, c, :].rearrange("p (h c) -> p h c", h=HEADS)
                        if ("h", c) in written:
                            tt(nds_v[:, :, 0:HD], nds_v[:, :, 0:HD], den3, MUL)
                            tt(h3, h3, nds_v[:, :, 0:HD], ADD)
                        else:
                            tt(h3, nds_v[:, :, 0:HD], den3, MUL)
                        written.add(("h", c))
                    if i < NT - 1:
                        dve.wait_ge(*due(("made", ("ss", l, u))))
                        b = bank(("ss", l, u))
                        for g in range(2):
                            r, n = slice(64 * g, 64 * g + 64), slice(192 * g, 192 * g + 192)
                            names = [("read", ("ss", l, u))] if g else []
                            if i == 0:
                                copy(sst_v[r, d, n], b[r, n], *names)
                            else:
                                s3 = sst_v[r, d, n].rearrange("p (h c) -> p h c", h=3)
                                tt(s3, s3, dcb_v[r, c, 32 * d + 3 * g:32 * d + 3 * g + 3].unsqueeze(2).broadcast_to(
                                    [64, 3, HD]), MUL)
                                tt(sst_v[r, d, n], b[r, n], sst_v[r, d, n], ADD, *names)
                        dve.wait_ge(*due(("made", ("cs", l, u))))
                        b4 = bank(("cs", l, u))[:, 0:390].rearrange("p (q j c) -> p q j c", q=3, j=2)
                        for j in range(2):
                            r = slice(64 * j, 64 * j + 64)
                            names = [("read", ("cs", l, u)), ("state", l, u)] if j else []
                            s3 = cst_v[r, d, :, j, :]
                            if i == 0:
                                copy(s3, b4[r, :, j, :], *names)
                            else:
                                r0 = 64 + 32 * d + j
                                tt(s3, s3, dcb_v[r, c, r0:r0 + 5:2].unsqueeze(2).broadcast_to([64, 3, 65]), MUL)
                                tt(s3, b4[r, :, j, :], s3, ADD, *names)

                spread(0)
                spread(1)
                scores(0)
                for u in range(len(units)):
                    if u + 2 < len(units):
                        spread(u + 2)
                    prep(u)
                    if u + 1 < len(units):
                        scores(u + 1)
                    combine(u)
                    if l == 0:
                        for ml, n in MOD_LATER[u * MOD_PER_UNIT:(u + 1) * MOD_PER_UNIT]:
                            if n % 2:
                                mod_columns(ml, n)
                stage_end(l, "units")
                fin = big[:, 512:896]
                for t in range(t0, NT):
                    y, y3 = ys_v[:, t, :], ys_v[:, t, :].rearrange("p (h c) -> p h c", h=HEADS)
                    xd3 = fin.rearrange("p (h c) -> p h c", h=HEADS)
                    tt(xd3, xtok_v[:, t, 0:384].rearrange("p (h c) -> p h c", h=HEADS),
                       ssdd[:, :].unsqueeze(2).broadcast_to([P, HEADS, HD]), MUL)
                    tt(y, y, fin, ADD)
                    tt(y, y, z_v[:, t, :], MUL, ("gated", l, t))
                for t in range(t0, NT):
                    dve.wait_ge(*due(("ssq", l, t)))
                rms(("rinv", l, 3), None, None, MIXW, None)
                dve.wait_ge(*due(("rstd", l, 3)))
                for t in range(t0, NT):
                    ts(ys_v[:, t, :], ys_v[:, t, :], small[:, 4 + t:5 + t], None, MUL, None, ("ssd out", l, t))
                for t in range(t0, NT):
                    h3 = hs_v[:, t, :].rearrange("p (h c) -> p h c", h=HEADS)
                    mu = small[:, 54:60]
                    step(V.tensor_reduce(mu, h3, AX.X, ADD))
                    ts(mu, mu, 1.0 / HD, None, MUL, None)
                    tt(h3, h3, mu.unsqueeze(2).broadcast_to([P, HEADS, HD]), SUB)
                    tt(fin, hs_v[:, t, :], hs_v[:, t, :], MUL)
                    step(V.tensor_reduce(small[:, 12 + 6 * t:18 + 6 * t], fin.rearrange("p (h c) -> p h c", h=HEADS),
                                         AX.X, ADD))
                if t0:
                    step(V.memset(small[:, 12:24], 1.0))
                ts(small[:, 12:36], small[:, 12:36], 1.0 / HD, EPS, MUL, ADD)
                step(V.reciprocal(small[:, 12:36], small[:, 12:36]), ("rinv", l, 4))
                dve.wait_ge(*due(("rstd", l, 4)))
                for t in range(t0, NT):
                    h3 = hs_v[:, t, :].rearrange("p (h c) -> p h c", h=HEADS)
                    tt(h3, h3, small[:, 12 + 6 * t:18 + 6 * t].unsqueeze(2).broadcast_to([P, HEADS, HD]), MUL)
                    tt(hs_v[:, t, :], hs_v[:, t, :], o_v[:, t, :], MUL, ("ml out", l, t))
                stage_end(l, "final")
                step(V.memset(small[:, 60:61], 0.0), ("hy z", l, 0))
                n = 512 - n0
                ns = len(streams)
                for o in range(2):
                    hc = hf_v[:, 0, o * L:(o + 1) * L]

                    def filt(k):
                        return hf_v[:, k, o * L:(o + 1) * L].unsqueeze(1).broadcast_to([P, ns, L])

                    def spec(ap):
                        return ap.rearrange("p (s n) -> p s n", n=L)

                    for fb in range(2):
                        dve.wait_ge(*due(("made", ("zf", l, o, 2 * fb))))
                        dve.wait_ge(*due(("made", ("zf", l, o, 2 * fb + 1))))
                        zr, zi = bank(("zf", l, o, 2 * fb)), bank(("zf", l, o, 2 * fb + 1))
                        zr, zi = spec(zr[:, n0:512]), spec(zi[:, n0:512])
                        a, c_ = spec(ht1[:, n0:512]), spec(ht2[:, n0:512])
                        yr, yi = spec(yf_v[:, fb, n0:512]), spec(yf_v[:, 2 + fb, n0:512])
                        tt(yr, zr, filt(fb), MUL)
                        tt(a, zi, filt(2 + fb), MUL)
                        tt(yr, yr, a, SUB)
                        tt(a, zr, filt(2 + fb), MUL, ("read", ("zf", l, o, 2 * fb)))
                        tt(c_, zi, filt(4 if fb == 0 else 1), MUL, ("read", ("zf", l, o, 2 * fb + 1)))
                        tt(yi, a, c_, ADD, *([("yf", l, o)] if fb == 1 else []))
                    for c in range(2):
                        dve.wait_ge(*due(("made", ("yt", l, o, c))))
                        b = bank(("yt", l, o, c))
                        z = hy_v[:, c, n0:512]
                        ts(ht1[:, n0:512], b[:, n0:512], small[:, 44 + 2 * o + c:45 + 2 * o + c], None, MUL, None,
                           ("read", ("yt", l, o, c)))
                        stt(ht1[:, n0:512], z, pcol[:, 74 + 2 * o + c:75 + 2 * o + c], ht1[:, n0:512], MUL, ADD)
                        dst = z if o == 0 else yT_v[:, 3 + c, n0:512]
                        a, g_ = ht1[:, n0:512], hy_v[:, 2 + 2 * o + c, n0:512]
                        if o == 1 and l % 2:
                            dst = dst.rearrange("p (r w) -> p w r", r=ROWS)
                            a, g_ = (q.rearrange("p (w r) -> p w r", r=ROWS) for q in (a, g_))
                        tt(dst, a, g_, MUL, ("hy z", l, o + 1))
                stage_end(l, "hyena")

                def gate_diagonals(n):
                    for s in streams:
                        if s != streams[0]:
                            for q in range(2):
                                dve.wait_ge(*due(("made", ("grow", l, n, s - 1, q))))
                        tt(hsum[:, 0:1024].rearrange("p (k j) -> p k j", k=KB),
                           ident[:, :].unsqueeze(1).broadcast_to([P, KB, P]),
                           modc_v[:, l, 3 * n + 2, :, 1 - s:2 - s].broadcast_to([P, KB, P]), MUL, ("gdiag", l, n, s))

                gate_diagonals(0)
                for t in range(t0, NT):
                    for half in range(2):
                        cs_ = slice(512 * half, 512 * half + 512)
                        dve.wait_ge(*due(("made", ("out", l, t, half))))
                        b = bank(("out", l, t, half))
                        dve.wait_ge(*due(("grow in", l, 0, t // 2)))
                        tt(ysum[:, 0:512], b[:, :], grow_v[:, t // 2, cs_], MUL, ("read", ("out", l, t, half)))
                        tt(x_v[:, t, cs_], x_v[:, t, cs_], ysum[:, 0:512], ADD)
                stage_end(l, "outproj")
                modulators(1)
                norm(2, t0)
                for k in range(KB):
                    dve.wait_ge(*due(("made", ("h2", l, k, 1))))
                    b = bank(("h2", l, k, 1))
                    ts(hT_v[:, k, L:2 * L], b[:, 0:L], ab_v[:, 2, k, 0:1], ab_v[:, 3, k, 0:1], MUL, ADD,
                       ("read", ("h2", l, k, 1)), ("h2T", l, "dve"))
                R = ysum[:, 0:144].rearrange("p (t n) -> p t n", t=NT)
                dve.wait_ge(*due(("made", ("router", l))))
                b = bank(("router", l))
                tt(R[:, t0:, :], b[:, t0 * 36:144].rearrange("p (t n) -> p t n", n=36),
                   rb[:, :].unsqueeze(1).broadcast_to([P, NT - t0, 36]), ADD, ("read", ("router", l)))
                if t0:
                    step(V.memset(ysum[:, 0:72], 0.0))
                scr = ysum[:, 256:1024]

                def pick(vals, n, mx, mask, w):
                    step(V.tensor_reduce(mx, vals, AX.X, MAX))
                    im = iom[:, 0:n].unsqueeze(1).broadcast_to([P, NT, n])
                    tt(mask, vals, mx.unsqueeze(2).broadcast_to([P, NT, n]), ALU.is_equal)
                    tt(mask, mask, im, MUL)
                    step(V.tensor_reduce(w, mask, AX.X, MIN))
                    tt(mask, im, w.unsqueeze(2).broadcast_to([P, NT, n]), ALU.is_equal)

                def area(a, n):
                    return scr[:, a:a + NT * n].rearrange("p (t n) -> p t n", t=NT)

                gmax, gsum, tmp4 = small[:, 54:58], small[:, 60:64], ysum[:, 1024:1028]
                gmask = area(0, 4)
                pick(R[:, :, 0:4], 4, gmax, gmask, tmp4)
                ge = otok[:, 0:16].rearrange("p (t n) -> p t n", t=NT)
                tt(ge, R[:, :, 0:4], gmax.unsqueeze(2).broadcast_to([P, NT, 4]), SUB, ("r1", l))
                E = area(16, 32)
                pen = area(144, 4)
                ts(pen, gmask, -NEG, NEG, MUL, ADD)
                for t in range(NT):
                    e4 = E[:, t, :].rearrange("p (g e) -> p g e", g=N_GROUPS)
                    tt(e4, R[:, t, 4:36].rearrange("p (g e) -> p g e", g=N_GROUPS),
                       gmask[:, t, :].unsqueeze(2).broadcast_to([P, N_GROUPS, PER_GROUP]), MUL)
                    tt(e4, e4, pen[:, t, :].unsqueeze(2).broadcast_to([P, N_GROUPS, PER_GROUP]), ADD)
                m1, m2 = ysum[:, 1032:1036], ysum[:, 1036:1040]
                k1, k2 = area(160, 32), area(288, 32)
                pick(E, 32, m1, k1, tmp4)
                stt(E, k1, 2 * NEG, E, MUL, ADD)
                pick(E, 32, m2, k2, tmp4)
                dve.wait_ge(*due(("r2", l)))
                tt(otok[:, 16:20], m2, m1, SUB, ("r3", l))
                step(V.tensor_reduce(gsum, ge, AX.X, ADD))
                dve.wait_ge(*due(("r4", l)))
                den = ysum[:, 1040:1044]
                ts(den, otok[:, 16:20], 1.0, None, ADD, None)
                tt(den, den, gsum, MUL)
                step(V.reciprocal(den, den))
                tt(m2, den, otok[:, 16:20], MUL)
                tt(k1, k1, den.unsqueeze(2).broadcast_to([P, NT, 32]), MUL)
                tt(k2, k2, m2.unsqueeze(2).broadcast_to([P, NT, 32]), MUL)
                tt(gwt, k1, k2, ADD)
                gate_diagonals(1)
                stage_end(l, "router")
                step(V.memset(big[:, 0:4096], 0.0))
                tag = ("moe", l)
                n_down = 2 * (NT - t0)
                before = dict(tally.count)
                with dve.Fori(0, BODIES) as i:
                    tally.turn = (tag, i)
                    for j in range(PER_BODY):
                        n = j * (4 + n_down)
                        if j >= 2:
                            dve.wait_ge(*due(("made", ("turn", l, (j - 1) * (4 + n_down) - 1))))
                        else:
                            dve.wait_ge(*due(("made", ("turn", l, (j + PER_BODY - 1) * (4 + n_down) - 1)), 1))
                        for f in range(2):
                            dve.wait_ge(*due(("made", ("turn", l, n + 2 * f + 1))))
                            b = bank(("turn", l, n + 2 * f + 1))
                            dve.wait_ge(*due(("sg", l, j, f)))
                            tt(hid_v[:, j % 2, f, n0:512], sg_v[:, f, n0:512], b[:, n0:512], MUL,
                               ("read", ("turn", l, n + 2 * f + 1)), ("hid", l, j), ("hidf", l, j, f))
                        for q in range(n_down):
                            t, half = t0 + q // 2, q % 2
                            dve.wait_ge(*due(("made", ("turn", l, n + 4 + q))))
                            b = bank(("turn", l, n + 4 + q))
                            a = acc_v[:, t, 512 * half:512 * half + 512]
                            stt(a, b[:, :], gwt[:, t, bass.ds(i * PER_BODY + j, 1)], a, MUL, ADD,
                                ("read", ("turn", l, n + 4 + q)))
                tally.looped(tag, before, BODIES)
                for t in range(t0, NT):
                    tt(acc_v[:, t, :], acc_v[:, t, :], grow_v[:, t // 2, :], MUL)
                    tt(x_v[:, t, :], x_v[:, t, :], acc_v[:, t, :], ADD, ("x done", l))
                stage_end(l, "moe")
            for t in range(2, NT):
                dve.wait_ge(*due(("ss", "f", t)))
            rms(("rinv", "f"), None, None, D, None)
            dve.wait_ge(*due(("rstd", "f")))
            dve.wait_ge(*due(("norm_in",)))
            for t in range(2):
                stt(xn_v[:, t, :], x_v[:, 2 + t, :], small[:, 6 + t:7 + t], grow[:, 0:D], MUL, MUL, ("result", t))


def constants():
    f4 = np.float32
    p, t = np.arange(P), np.arange(L)
    s_gt_l = p[:, None] > p[None, :]
    mask = np.stack([np.where(s_gt_l, NEG, 0.0), np.where(s_gt_l.T, NEG, 0.0)], 1)
    sel = np.zeros((P, 2, 3, P), f4)
    for r in range(P):
        for j in range(2):
            for i in range(3):
                if r % 32 == (3 * j + i if r < 64 else 2 * i + j):
                    sel[r, j, i] = 1.0
    keep = np.ones((P, 4, P), f4)
    keep[(p // 32) % 2 == 0, :, 0] = 0.0
    keep[(p // 32) % 2 == 1, :, P - 1] = 0.0
    ang = 2 * np.pi * ((t[:, None] * t[None, :]) % (2 * L)) / (2 * L)
    cos, sin = np.cos(ang), -np.sin(ang)
    nyq = (-1.0) ** t
    cn, sn = cos.copy(), sin.copy()
    cn[:, 0], sn[:, 0] = nyq, nyq
    tp = lambda m: m.reshape(2, P, -1).transpose(1, 0, 2)
    dftn = np.stack([tp(cn[:, :P]), tp(sn[:, :P])], 1)
    scale = np.where(t == 0, 1.0, 2.0) / (2 * L)
    ic, is_ = cos * scale[:, None], sin * scale[:, None]
    is_[0] = nyq / (2 * L)
    tf = t.astype(f4)
    tu = tf / f4(L - 1)
    bands = np.linspace(1e-4, 15, 16).astype(f4)
    fa = (f4(2 * np.pi / L) * tf[:, None] * bands[None, :]).astype(f4)
    feats = np.concatenate([tu[:, None], np.cos(fa), -np.sin(fa)], -1).T
    tcol = np.zeros((P, 4), f4)
    tcol[:, 0], tcol[:, 1] = -tu[:P], -tu[P:]
    tcol[:, 2] = p != 0
    tcol[:, 3] = np.where(p < 64, 1.0, -1.0)
    c = dict(ident=np.eye(P), mask=mask, sel=sel, keep=keep, dftc=tp(cos), dfts=tp(sin), dftn=dftn,
             invc=tp(ic), invs=tp(is_), feats=feats, tcol=tcol, iom=np.tile(np.arange(EXPERTS) - 99.0, (P, 1)))
    c = {k: np.ascontiguousarray(a.reshape(a.shape[0], -1).astype(f4)) for k, a in c.items()}
    return c


_INS = ['x', 'c', 'ctx', 'c_ctx', 'w_mod', 'b_mod', 'norm1_w', 'norm2_w', 'w_in', 'w_out', 'ssd_conv_w',
        'ssd_conv_b', 'ssd_dt_bias', 'ssd_a_log', 'ssd_d', 'ssd_norm_w', 'hy_conv_w', 'hy_conv_b', 'hy_pos_w1',
        'hy_pos_b1', 'hy_pos_w2', 'hy_pos_b2', 'hy_pos_w3', 'hy_freq', 'hy_decay', 'hy_skip', 'ml_conv_w',
        'ml_conv_b', 'ml_gate_b', 'ml_norm_w', 'grp_router_w', 'grp_router_b', 'exp_router_w', 'exp_router_b',
        'moe_w_gate', 'moe_w_up', 'moe_w_down', 'final_norm_w']


def kernel(**inputs):
    import concourse.bacc as _bacc
    from concourse.bass_utils import run_bass_kernel_spmd as _run

    arrays = {n: np.ascontiguousarray(inputs[n]) for n in _INS}
    arrays.update({"const_" + k: a for k, a in constants().items()})
    at = {}
    for first in (True, False):
        nc = _bacc.Bacc("TRN2", target_bir_lowering=False, num_devices=1)
        args = {n: nc.dram_tensor(f"in_{n}", a.shape, mybir.dt.from_np(a.dtype), kind="ExternalInput").ap()
                for n, a in arrays.items()}
        res = nc.dram_tensor("out_0", (1, L, D), F32, kind="ExternalOutput").ap()
        build(nc, args, res, at, first)
    r = _run(nc, [{f"in_{n}": a for n, a in arrays.items()}], core_ids=[0])
    return r.results[0]["out_0"]
```

```python
from contextlib import ExitStack

import concourse.bass as bass
from concourse import mybir
import numpy as np

F32 = mybir.dt.float32
U32 = mybir.dt.uint32
I32 = mybir.dt.int32
BF16 = mybir.dt.bfloat16
ALU = mybir.AluOpType
ACT = mybir.ActivationFunctionType
AX = mybir.AxisListType

P = 128
D = 1024
KB = D // P
L = 256
DEPTH = 2
NT = 4
GRID_W = 64
ROWS = L // GRID_W
HD = 64
HEADS = 6
MIXW = HEADS * HD
HYW = 256
SSD_CH = MIXW + 256
FH = 64
POS = 33
N_GROUPS, PER_GROUP = 4, 8
EXPERTS = N_GROUPS * PER_GROUP
EH = 256
EPS = 1e-6
COL_Z, COL_XBC, COL_DT = 0, MIXW, MIXW + SSD_CH
COL_HY = COL_DT + 2 * HEADS
COL_QK = COL_HY + 3 * HYW
COL_V = COL_QK + 2 * MIXW
COL_O = COL_V + MIXW
COL_G = COL_O + MIXW
NEG = -1.0e30
MAGIC = 12582912.0
BANKS = 8
SLOTS = 4
PER_BODY = 4
BODIES = EXPERTS // PER_BODY
PREFETCH = SLOTS
MOST_PAIRS = 2 * NT * P
MORE_ITEMS = 8
assert MORE_ITEMS >= (MOST_PAIRS - EXPERTS) // P
ITEMS = EXPERTS + MORE_ITEMS
AHEAD = 3
NOWHERE = 4096.0
TURN = []
for _j in range(PER_BODY):
    TURN += [("gathered", _j, 0), ("gathered", _j, 1)] + ([("hidden", _j - 1)] if _j else [])
    TURN += [("gate up", _j)] + ([("down", _j - 1, 0), ("down", _j - 1, 1)] if _j else [])
TURN += [("hidden", PER_BODY - 1), ("down", PER_BODY - 1, 0), ("down", PER_BODY - 1, 1)]
assert len(TURN) % BANKS == 0
MORE_PRODUCTS, MORE_DVE = 4, 6
BACK = (1, 0, 3, 2)
MOD_SLOTS = 6 * D // 256
MOD_FIRST = 2 * D // 256
MOD_LATER = [(0, n) for n in range(MOD_FIRST, MOD_SLOTS)] + [(1, n) for n in range(MOD_SLOTS)]
MOD_PER_UNIT = len(MOD_LATER) // (2 * NT)


class Tally:

    def __init__(self, at, first):
        self.at, self.first, self.count, self.sems = at, first, {}, {}
        self.turn = None

    def tick(self, sem, *names, by=1):
        self.count[sem] = self.count.get(sem, 0) + by
        for n in names:
            self.at[n] = (sem, self.count[sem])
            if self.turn is not None:
                self.at[("in", self.turn[0], n)] = True
        return by

    def due(self, name, turns_back=0):
        assert self.first or name in self.at, name
        sem, value = self.at.get(name, ("dve_done", 1000))
        if self.turn is not None and ("in", self.turn[0], name) in self.at:
            tag, i = self.turn
            per = self.at.get(("per", tag, sem), 1)
            return self.sems[sem], i * per + (value - turns_back * per)
        return self.sems[sem], value

    def looped(self, tag, before, turns):
        self.turn = None
        for sem in list(self.count):
            per = self.count[sem] - before.get(sem, 0)
            if per:
                self.at[("per", tag, sem)] = per
                self.count[sem] += per * (turns - 1)


def build(nc, A, out, at, first):
    tally = Tally(at, first)
    tick, due = tally.tick, tally.due
    with ExitStack() as ctx:
        def sb(name, cols, dt=F32):
            return ctx.enter_context(nc.sbuf_tensor(name, [P, cols], dt))

        def sem(name):
            tally.sems[name] = ctx.enter_context(nc.semaphore(name))
            return tally.sems[name]

        pe_done, act_done, dve_done = sem("pe_done"), sem("act_done"), sem("dve_done")
        consts_in, x_in, norm_in, out_written = sem("consts_in"), sem("x_in"), sem("norm_in"), sem("out_written")
        params_in = [sem(f"params{l}_in") for l in range(DEPTH)]
        slot_in = [sem(f"slot{s}_in") for s in range(SLOTS)]
        route_in = [sem(f"route{l}_in") for l in range(DEPTH)]
        rows_in = [sem(f"rows{b}_in") for b in range(4)]
        rows_out = [sem(f"rows{b}_out") for b in range(2)]
        pairs_in = [sem(f"pairs{t}_in") for t in range(NT)]
        pool_done = sem("pool_done")
        more_pe = [sem(f"more_pe{l}") for l in range(DEPTH)]
        more_act = [sem(f"more_act{l}") for l in range(DEPTH)]
        more_dve = [sem(f"more_dve{l}") for l in range(DEPTH)]
        more_rows_in = [sem(f"more_rows{l}_in") for l in range(DEPTH)]
        more_rows_out = [sem(f"more_rows{l}_out") for l in range(DEPTH)]
        more_weights = [sem(f"more_weights{l}_in") for l in range(DEPTH)]
        h2_rows = nc.dram_tensor("h2_rows", (NT * P, D), F32).ap()
        pair_rows = nc.dram_tensor("pair_rows", (MOST_PAIRS, D), F32).ap()
        banks = [ctx.enter_context(nc.psum_tensor(f"bank{b}", [P, 512], F32)) for b in range(BANKS)]

        ident = sb("ident", P)
        ident16 = sb("ident16", P, BF16)
        ones = sb("ones", P)
        mask16 = sb("mask16", 2 * P, BF16)
        sel = sb("sel", 2 * 3 * P)
        keep = sb("keep", 4 * P)
        dftc = sb("dftc", 2 * L)
        dfts = sb("dfts", 2 * L)
        dftn = sb("dftn", 2 * 2 * P)
        invc = sb("invc", 2 * L)
        invs = sb("invs", 2 * L)
        feats = sb("feats", L)
        tcol = sb("tcol", 4)
        iom = sb("iom", EXPERTS)
        prow = sb("prow", P)
        pcol = sb("pcol", P)
        cond = sb("cond", 2 * KB)
        bmod = sb("bmod", DEPTH * 6 * KB)
        nw = sb("nw", 2 * KB)
        gcolp = sb("gcolp", 4)
        wg_raw = sb("wg_raw", KB * 36)
        rw = sb("rw", KB * 36)
        rb = sb("rb", 36)
        ssdd = sb("ssdd", HEADS)
        w1 = sb("w1", FH)
        w2 = sb("w2", FH)
        hcol = sb("hcol", 3)
        x = sb("x", NT * D)
        hT = sb("hT", KB * 4 * P)
        modc = sb("modc", DEPTH * 6 * KB * 2)
        ab = sb("ab", 4 * KB * 2)
        grow = sb("grow", 2 * D)
        small = sb("small", 64)
        xbc = sb("xbc", 5 * 512)
        qkT = sb("qkT", 6 * 512)
        hyT = sb("hyT", 6 * 512)
        ztok = sb("ztok", NT * MIXW)
        otok = sb("otok", NT * MIXW)
        vaug = sb("vaug", NT * HEADS * 65)
        big = sb("big", 9 * 512)
        hfilt = sb("hfilt", 5 * 512)
        xtok = sb("xtok", NT * 512)
        ktok = sb("ktok", NT * MIXW)
        ysum = sb("ysum", NT * MIXW)
        hsum = sb("hsum", NT * MIXW)
        ring = sb("ring", SLOTS * 2048)
        sst = sb("sst", 2 * MIXW)
        cst = sb("cst", 2 * HEADS * 65)
        index = sb("index", 4 + 2, U32)
        if not first:
            print("sbuf left", nc.sbuf_bytes_remaining)

        wg, w3 = xtok[:, :], ktok[:, 0:1024]
        cols, dcb = hT[:, 1536:1536 + NT * 4 * P], hT[:, 3584:3584 + NT * P]
        wx, wv = hT[:, 0:1158], big[:, 0:2 * 4 * 384]

        modrow = grow[:, 3 * D // 2:2 * D]

        mask_v = mask16[:, :].rearrange("p (d s) -> p d s", d=2)
        sel_v = sel[:, :].rearrange("p (j i m) -> p j i m", j=2, i=3)
        dftc_v = dftc[:, :].rearrange("p (t f) -> p t f", t=2)
        dfts_v = dfts[:, :].rearrange("p (t f) -> p t f", t=2)
        dftn_v = dftn[:, :].rearrange("p (q t f) -> p q t f", q=2, t=2)
        invc_v = invc[:, :].rearrange("p (b t) -> p b t", b=2)
        invs_v = invs[:, :].rearrange("p (b t) -> p b t", b=2)
        cond_v = cond[:, :].rearrange("p (k s) -> p k s", s=2)
        bmod_v = bmod[:, :].rearrange("p (l m k) -> p l m k", l=DEPTH, m=6)
        nw_v = nw[:, :].rearrange("p (n k) -> p n k", n=2)
        wgr_v = wg_raw[:, :].rearrange("p (k n) -> p k n", k=KB)
        wg_v = wg[:, :].rearrange("p (k y r) -> p k y r", k=KB, y=2)
        rw_v = rw[:, :].rearrange("p (k n) -> p k n", k=KB)
        x_v = x[:, :].rearrange("p (t d) -> p t d", t=NT)
        hT_v = hT[:, :].rearrange("p (k n) -> p k n", k=KB)
        yT_v = hT_v
        modc_v = modc[:, :].rearrange("p (l m k s) -> p l m k s", l=DEPTH, m=6, s=2)
        ab_v = ab[:, :].rearrange("p (n k s) -> p n k s", n=4, s=2)
        grow_v = grow[:, :].rearrange("p (s d) -> p s d", s=2)
        xbc_v = xbc[:, :].rearrange("p (b n) -> p b n", n=512)
        qk_v = qkT[:, :].rearrange("p (b n) -> p b n", n=512)
        hy_v = hyT[:, :].rearrange("p (b n) -> p b n", n=512)
        z_v = ztok[:, :].rearrange("p (t c) -> p t c", t=NT)
        o_v = otok[:, :].rearrange("p (t c) -> p t c", t=NT)
        va_v = vaug[:, :].rearrange("p (t h c) -> p t h c", t=NT, h=HEADS)
        xtok_v = xtok[:, :].rearrange("p (t c) -> p t c", t=NT)
        ktok_v = ktok[:, :].rearrange("p (t c) -> p t c", t=NT)
        ys_v = ysum[:, :].rearrange("p (t c) -> p t c", t=NT)
        hs_v = hsum[:, :].rearrange("p (t c) -> p t c", t=NT)
        cols_v = cols[:, :].rearrange("p (c q r) -> p c q r", c=NT, q=4)
        dcb_v = dcb[:, :].rearrange("p (c r) -> p c r", c=NT)
        hf_v = hfilt[:, :].rearrange("p (b n) -> p b n", n=512)
        sst_v = sst[:, :].rearrange("p (d n) -> p d n", d=2)
        cst_v = cst[:, :].rearrange("p (d q j c) -> p d q j c", d=2, q=3, j=2)
        big_v = big[:, :].rearrange("p (r n) -> p r n", n=512)
        U, SP, CUM, EX, ES, ND, MX, RL, RS = (big_v[:, r, :] for r in range(9))
        t1, t2, t3 = (ysum[:, 512 * r:512 * r + 512] for r in range(3))
        xn_v = big[:, 0:4096].rearrange("p (t d) -> p t d", t=NT)
        taps_v = big[:, 0:2048].rearrange("p (t e o c) -> p t e o c", t=2, e=2, o=2)
        tabs_v = big[:, 2048:4096].rearrange("p (t e o c) -> p t e o c", t=2, e=2, o=2)
        hid_a, hid_b, hid_c = (hsum[:, 256 * r:256 * r + 256] for r in range(3))
        sc_v = wv[:, :].rearrange("p (u j n) -> p u j n", u=2, j=4)
        xdt, xde, ve, nds = wx[:, 0:384], wx[:, 384:768], wx[:, 768:1158], big[:, 3072:3462]
        rlm_v = grow[:, 0:2 * 2 * 384].rearrange("p (u j i n) -> p u j i n", u=2, j=2, i=3)
        ve_v = ve.rearrange("p (h c) -> p h c", h=HEADS)
        nds_v = nds.rearrange("p (h c) -> p h c", h=HEADS)
        zt_v = ysum[:, 0:1024].rearrange("p (t n) -> p t n", t=2)
        yf_v = wv[:, 0:2048].rearrange("p (b n) -> p b n", b=4)
        ht1, ht2 = hsum[:, 0:512], hsum[:, 512:1024]
        chosen_v = ysum[:, 1088:1088 + NT * EXPERTS].rearrange("p (t e) -> p t e", t=NT)
        tri, iota = hfilt[:, 0:P], hfilt[:, P:2 * P]
        items, pair_no = hfilt[:, 2 * P:2 * P + ITEMS], hfilt[:, 2 * P + ITEMS:2 * P + ITEMS + 2 * NT]
        slot_hot = xtok[:, 0:2 * NT * P].rearrange("p (n s) -> p n s", n=2 * NT)
        item_hot = xtok[:, 2 * NT * P:2 * NT * (P + 3 * ITEMS)].rearrange("p (n v i) -> p n v i", n=2 * NT, v=3)
        weight_of = ztok[:, 0:44]
        token_of, pair_of = ztok[:, 64:64 + 44].bitcast(U32), ztok[:, 128:128 + 44].bitcast(U32)
        more_expert, more_flag = ztok[:, 192:192 + MORE_ITEMS].bitcast(I32), ztok[:, 208:209].bitcast(I32)
        rows_v = xn_v
        rowsT_v = qkT[:, 0:2 * D].rearrange("p (u k n) -> p u k n", u=2, k=KB)
        sg_v = xbc[:, 0:2 * EH].rearrange("p (u n) -> p u n", u=2)
        hid_v = xbc[:, 512:512 + 2 * EH].rearrange("p (u n) -> p u n", u=2)
        hidT_v = xbc[:, 1024:1024 + 2 * EH].rearrange("p (u n) -> p u n", u=2)
        res_v = hyT[:, 0:2 * D].rearrange("p (u n) -> p u n", u=2)
        two_v = [a.rearrange("p (y d) -> p y d", y=2) for a in (big[:, 0:2048], big[:, 2048:4096],
                                                              hT[:, 0:2048], hT[:, 2048:4096])]

        def slot_v(s, k):
            return ring[:, s * 2048:(s + 1) * 2048].rearrange("p (k n) -> p k n", k=k)

        products = []
        loads = []

        block = ctx.enter_context(nc.Block())

        @block.sync
        def _(sp):
            def weight(name, src, k):
                n = len(loads)
                s = n % SLOTS
                loads.append(name)
                at[("slot", name)] = s
                if n >= SLOTS:
                    sp.wait_ge(*due(("used", loads[n - SLOTS])))
                with nc.allow_non_contiguous_dma(reason="rows of a kilobyte"):
                    sp.dma_start(slot_v(s, k)[:, :, 0:src.shape[-1]], src).then_inc(
                        slot_in[s], tick(f"slot{s}_in", ("load", name), by=16))

            def fetch(group, dst, src):
                with nc.allow_non_contiguous_dma(reason="small parameters"):
                    sp.dma_start(dst, src).then_inc(tally.sems[group], tick(group, (group,), by=16))

            def parameters(l):
                g = f"params{l}_in"
                if l == 0:
                    sp.wait_ge(*due(("gcolp zero",)))
                else:
                    sp.wait_ge(*due(("x done", l - 1)))
                fetch(g, nw_v[:, 0, :], A["norm1_w"][l].rearrange("(p k) -> p k", k=KB))
                fetch(g, nw_v[:, 1, :], A["norm2_w"][l].rearrange("(p k) -> p k", k=KB))
                r = 0
                for name, n in (("ssd_conv_w", 15), ("ssd_conv_b", 5), ("hy_conv_w", 18), ("hy_conv_b", 6),
                                ("ml_conv_w", 18), ("ml_conv_b", 6), ("ssd_norm_w", 3), ("ml_norm_w", 3),
                                ("hy_skip", 4)):
                    src = A[name][l]
                    src = src.rearrange("w (b c) -> (w b) c", c=P) if len(src.shape) == 2 else \
                        src.rearrange("(b c) -> b c", c=P)
                    fetch(g, prow[r:r + n, :], src)
                    r += n
                for d in range(2):
                    fetch(g, gcolp[32 * d:32 * d + HEADS, 0:1], A["ssd_dt_bias"][l, d].unsqueeze(1))
                    fetch(g, gcolp[64 + 32 * d:64 + 32 * d + HEADS, 0:1], A["ml_gate_b"][l, d, 1].unsqueeze(1))
                    fetch(g, gcolp[64 + 32 * d:64 + 32 * d + HEADS, 1:2], A["ml_gate_b"][l, d, 0].unsqueeze(1))
                    fetch(g, gcolp[32 * d:32 * d + HEADS, 2:3], A["ssd_a_log"][l, d].unsqueeze(1))
                win = A["w_in"][l].rearrange("(p k) n -> p k n", k=KB)
                fetch(g, wgr_v[:, :, 0:12], win[:, :, COL_DT:COL_DT + 12])
                fetch(g, wgr_v[:, :, 12:36], win[:, :, COL_G:COL_G + 24])
                fetch(g, rw_v[:, :, 0:4], A["grp_router_w"][l].rearrange("(p k) n -> p k n", k=KB))
                fetch(g, rw_v[:, :, 4:36], A["exp_router_w"][l].rearrange("(p k) n -> p k n", k=KB))
                fetch(g, rb[:, 0:4], A["grp_router_b"][l].partition_broadcast(P))
                fetch(g, rb[:, 4:36], A["exp_router_b"][l].partition_broadcast(P))
                fetch(g, ssdd[:, :], A["ssd_d"][l].partition_broadcast(P))
                fetch(g, w1[0:POS, :], A["hy_pos_w1"][l])
                fetch(g, w2[0:FH, :], A["hy_pos_w2"][l])
                fetch(g, w3[0:FH, :], A["hy_pos_w3"][l])
                for c, name in enumerate(("hy_pos_b1", "hy_pos_b2", "hy_freq")):
                    fetch(g, hcol[0:FH, c:c + 1], A[name][l].unsqueeze(1))
                fetch(g, grow[:, 0:4 * HYW],
                      A["hy_decay"][l].rearrange("e o c -> (e o c)").partition_broadcast(P))

            fetch("consts_in", cond_v[:, :, 0], A["c"][0].rearrange("(p k) -> p k", k=KB))
            fetch("consts_in", cond_v[:, :, 1], A["c_ctx"].rearrange("(p k) -> p k", k=KB))
            for name, t in (("ident", ident), ("mask", big[:, 0:2 * P]), ("sel", sel), ("keep", keep),
                            ("dftc", dftc), ("dfts", dfts), ("dftn", dftn), ("invc", invc), ("invs", invs),
                            ("tcol", tcol), ("iom", iom)):
                fetch("consts_in", t[:, :], A["const_" + name])
            fetch("consts_in", feats[0:POS, :], A["const_feats"])
            for l in range(DEPTH):
                fetch("consts_in", bmod_v[:, l], A["b_mod"][l].rearrange("(m p k) -> p m k", m=6, k=KB))
            fetch("x_in", x_v[:, 0:2, :], A["ctx"][0].rearrange("(t p) d -> p t d", p=P))
            fetch("x_in", x_v[:, 2:4, :], A["x"][0].rearrange("(t p) d -> p t d", p=P))

            def modulation(l, n):
                wm = A["w_mod"][l].rearrange("(p k) n -> p k n", k=KB)
                weight(("mod", l, n), wm[:, :, 256 * n:256 * n + 256], KB)

            for l in range(DEPTH):
                t0 = 0 if l == 0 else 2
                parameters(l)
                if l == 0:
                    for n in range(MOD_FIRST):
                        modulation(0, n)
                win = A["w_in"][l].rearrange("(p k) n -> p k n", k=KB)
                for name, c0, n in (("qk", COL_QK, 768), ("xbc", COL_XBC, 640), ("v", COL_V, 384),
                                    ("z", COL_Z, 384), ("o", COL_O, 384), ("hy", COL_HY, 768)):
                    for q in range((n + 255) // 256):
                        w = min(256, n - 256 * q)
                        weight((name, l, q), win[:, :, c0 + 256 * q:c0 + 256 * q + w], KB)
                if l == 0:
                    for ml, n in MOD_LATER:
                        modulation(ml, n)
                wo = A["w_out"][l].rearrange("(k p) n -> p k n", p=P)
                for q in range(4):
                    weight(("wout", l, q), wo[:, :, 256 * q:256 * q + 256], KB)

                for who in ("pe", "act", "dve"):
                    sp.wait_ge(*due(("end", who, l, "hyena")))
                for name, dst in (("tri", tri), ("iota", iota), ("items", items), ("pair_no", pair_no)):
                    fetch(f"route{l}_in", dst, A["const_" + name])
                wgt = A["moe_w_gate"][l].rearrange("g e (p k) f -> (g e) p k f", k=KB)
                wup = A["moe_w_up"][l].rearrange("g e (p k) f -> (g e) p k f", k=KB)
                wdn = A["moe_w_down"][l].rearrange("g e (f p) d -> (g e) p f d", p=P)
                body = 3 * PER_BODY
                base = len(loads)

                def expert_src(j, e):
                    w = (wgt, wup, wdn)[j % 3]
                    return w[bass.ds(e, 1)].rearrange("e p k f -> (e p) k f") if not isinstance(e, int) else w[e]

                def expert_load(q, e):
                    j, s = q % body, (base + q) % SLOTS
                    at[("slot", ("expert", l, j))] = (base + j) % SLOTS
                    k = KB if j % 3 < 2 else 2
                    with nc.allow_non_contiguous_dma(reason="rows of a kilobyte"):
                        return sp.dma_start(slot_v(s, k), expert_src(j, e)), s

                def turns_first(q):
                    name = ("load", ("expert", l, q))
                    at[("in", ("moe", l), name)] = True
                    return name

                for q in range(PREFETCH):
                    sp.wait_ge(*due(("used", loads[base + q - SLOTS])))
                    ins, s = expert_load(q, q // 3)
                    ins.then_inc(slot_in[s], tick(f"slot{s}_in", turns_first(q), by=16))
                before = dict(tally.count)
                with sp.Fori(0, BODIES - 1) as i:
                    tally.turn = (("moe", l), i)
                    for q in range(PREFETCH, PREFETCH + body):
                        sp.wait_ge(*due(("used", ("expert", l, q - SLOTS))))
                        ins, s = expert_load(q, i * PER_BODY + q // 3)
                        names = [turns_first(q)] if q < body else []
                        ins.then_inc(slot_in[s], tick(f"slot{s}_in", *names, by=16))
                tally.looped(("moe", l), before, BODIES - 1)
                for q in range(PREFETCH, body):
                    sp.wait_ge(*due(("used", ("expert-last", l, q - SLOTS))))
                    ins, s = expert_load(q, EXPERTS - PER_BODY + q // 3)
                    ins.then_inc(slot_in[s], tick(f"slot{s}_in", by=16))
                for j in range(body):
                    loads.append(("expert-last", l, j))
                for who in ("pe", "act", "dve"):
                    sp.wait_ge(*due(("end", who, l, "moe")))
                with sp.If(sp.value_load(more_flag[0:1, :], min_val=0, max_val=MORE_ITEMS) != 0):
                    with sp.Fori(0, MORE_ITEMS) as i:
                        e = sp.value_load(more_expert[0:1, bass.ds(i, 1)], min_val=0, max_val=EXPERTS - 1)
                        sp.wait_ge(more_pe[l], i * MORE_PRODUCTS + 1)
                        with nc.allow_non_contiguous_dma(reason="rows of a kilobyte"):
                            sp.dma_start(slot_v(0, KB), wgt[bass.ds(e, 1)].rearrange("e p k f -> (e p) k f")).then_inc(more_weights[l], 16)
                            sp.dma_start(slot_v(1, KB), wup[bass.ds(e, 1)].rearrange("e p k f -> (e p) k f")).then_inc(more_weights[l], 16)
                            sp.dma_start(slot_v(2, 2), wdn[bass.ds(e, 1)].rearrange("e p k f -> (e p) k f")).then_inc(more_weights[l], 16)
                    sp.wait_ge(more_pe[l], MORE_ITEMS * MORE_PRODUCTS + 1)
                for t in range(t0, NT):
                    if t == t0:
                        sp.wait_ge(*due(("pairs written", l)))
                    sp.dma_start(two_v[t - t0], pair_rows.rearrange("(y t p) d -> t p y d", y=2, p=P)[t]).then_inc(
                        pairs_in[t], tick(f"pairs{t}_in", ("pairs", l, t), by=16))

            sp.wait_ge(*due(("fnw free",)))
            fetch("norm_in", grow[:, 0:D], A["final_norm_w"].partition_broadcast(P))
            for t in range(2):
                sp.wait_ge(*due(("result", t)))
                sp.dma_start(out[0, t * P:(t + 1) * P, :], xn_v[:, t, :]).then_inc(out_written, 16)
            sp.wait_ge(out_written, 32)

        @block.tensor
        def _(pe):
            def product(name):
                n = len(products)
                products.append(name)
                at[("bank", name)] = n % BANKS
                if n >= BANKS:
                    pe.wait_ge(*due(("read", products[n - BANKS])))
                return banks[n % BANKS]

            def made(name, *also):
                return tick("pe_done", ("made", name), *also)

            def mm(o, a, b, s=True, e=True, **k):
                return nc.tensor.matmul(o, a, b, start=s, stop=e, **k)

            def slot(name, k):
                return slot_v(at[("slot", name)], k)

            def stage_end(l, stage):
                pe.drain().then_inc(pe_done, tick("pe_done", ("end", "pe", l, stage)))
                pe.wait_ge(*due(("end", "act", l, stage)))
                pe.wait_ge(*due(("end", "dve", l, stage)))

            def modulation(l, n):
                m, q = n // 4, n % 4
                b = product(("mod", l, n))
                pe.wait_ge(*due(("load", ("mod", l, n))))
                w = slot(("mod", l, n), KB)
                for k in range(KB):
                    last = mm(b[0:2, 0:256], cond_v[:, k, :], w[:, k, :], k == 0, k == KB - 1)
                last.then_inc(pe_done, made(("mod", l, n), ("used", ("mod", l, n))))
                if q % 2:
                    b = product(("modc", l, m, q // 2))
                    pe.wait_ge(*due(("modrow", l, n)))
                    for k in range(KB):
                        last = nc.tensor.transpose(b[0:64, 2 * k:2 * k + 2], modrow[0:2, k::KB], ident[0:2, 0:2])
                    last.then_inc(pe_done, made(("modc", l, m, q // 2)))

            for l in range(DEPTH):
                t0 = 0 if l == 0 else 2
                n0 = t0 * P
                b = product(("pcol", l))
                pe.wait_ge(*due((f"params{l}_in",)))
                pe.wait_ge(*due(("consts_in",)))
                nc.tensor.transpose(b[:, 0:78], prow[0:78, :], ident[0:78, 0:78]).then_inc(pe_done, made(("pcol", l)))
                if l == 0:
                    pe.wait_ge(*due(("cond",)))
                    for n in range(MOD_FIRST):
                        modulation(0, n)
                b = product(("hid1", l))
                mm(b[0:FH, 0:L], w1[0:POS, :], feats[0:POS, :]).then_inc(pe_done, made(("hid1", l)))
                b = product(("hid2", l))
                pe.wait_ge(*due(("sin", l, 0)))
                mm(b[0:FH, 0:L], w2[0:FH, :], hid_c[0:FH, :]).then_inc(pe_done, made(("hid2", l)))
                for t in range(2):
                    for e in range(2):
                        b = product(("taps", l, t, e))
                        pe.wait_ge(*due(("sin", l, 1)))
                        mm(b[:, :], hid_c[0:FH, t * P:(t + 1) * P], w3[0:FH, 512 * e:512 * e + 512]).then_inc(pe_done, made(("taps", l, t, e)))
                b = product(("tapsum", l))
                pe.wait_ge(*due(("tabs", l)))
                for o in range(2):
                    for c in range(2):
                        n = 0
                        for t in range(2):
                            for e in range(2):
                                last = mm(b[:, 2 * o + c:2 * o + c + 1], tabs_v[:, t, e, o, c * P:(c + 1) * P],
                                          ones[:, 0:1], n == 0, n == 3)
                                n += 1
                last.then_inc(pe_done, made(("tapsum", l)))
                for n, (src, mat) in enumerate((("s", dftc_v[:, :, 0:P]), ("s", dftc_v[:, :, P:L]),
                                                ("d", dfts_v[:, :, 0:P]), ("d", dfts_v[:, :, P:L]),
                                                ("s", dftn_v[:, 0, :, :]))):
                    b = product(("spec", l, n))
                    pe.wait_ge(*due(("tapsd", l)))
                    rhs = taps_v[:, :, 0, :, :] if src == "s" else taps_v[:, :, 1, :, :]
                    for t in range(2):
                        last = mm(b[:, :], mat[:, t, :], rhs[:, t, :, :], t == 0, t == 1)
                    last.then_inc(pe_done, made(("spec", l, n)))
                stage_end(l, "mod")
                for k in range(KB):
                    for s in range(2):
                        b = product(("h1", l, k, s))
                        pe.wait_ge(*due(("xn", l, 1)))
                        for t in range(2):
                            last = nc.tensor.transpose(b[:, t * P:(t + 1) * P], xn_v[:, 2 * s + t, k::KB], ident[:, :])
                        last.then_inc(pe_done, made(("h1", l, k, s)))
                stage_end(l, "norm1")
                for y in range(2):
                    b = product(("gates", l, y))
                    pe.wait_ge(*due(("wg", l)))
                    for k in range(KB):
                        last = mm(b[:, :], wg_v[:, k, y, :], hT_v[:, k, :], k == 0, k == KB - 1)
                    last.then_inc(pe_done, made(("gates", l, y)))

                def channel_major(name, blocks, lo):
                    for q in range((blocks + 1) // 2):
                        pe.wait_ge(*due(("load", (name, l, q))))
                        w = slot((name, l, q), KB)
                        for i in range(min(2, blocks - 2 * q)):
                            blk = 2 * q + i
                            a0 = lo(blk)
                            b = product((name, l, blk))
                            for k in range(KB):
                                last = mm(b[:, a0:512], w[:, k, i * P:(i + 1) * P], hT_v[:, k, a0:512],
                                          k == 0, k == KB - 1)
                            used = [("used", (name, l, q))] if blk == min(2 * q + 1, blocks - 1) else []
                            last.then_inc(pe_done, made((name, l, blk), *used))

                def token_major(name, tiles):
                    pe.wait_ge(*due(("load", (name, l, 0))))
                    pe.wait_ge(*due(("load", (name, l, 1))))
                    for t in tiles:
                        b = product((name, l, t))
                        for q, (c0, c1) in enumerate(((0, 256), (256, 384))):
                            w = slot((name, l, q), KB)
                            for k in range(KB):
                                last = mm(b[:, c0:c1], hT_v[:, k, t * P:(t + 1) * P], w[:, k, 0:c1 - c0],
                                          k == 0, k == KB - 1)
                        used = [("used", (name, l, q)) for q in range(2)] if t == NT - 1 else []
                        last.then_inc(pe_done, made((name, l, t), *used))

                channel_major("qk", 6, lambda blk: n0 if blk < 3 else 0)
                channel_major("xbc", 5, lambda blk: 0)
                token_major("v", range(NT))
                token_major("z", range(t0, NT))
                token_major("o", range(t0, NT))
                channel_major("hy", 6, lambda blk: n0)
                for c in range(NT):
                    b = product(("xtok", l, c))
                    pe.wait_ge(*due(("xbc done", l)))
                    for blk in range(4):
                        last = nc.tensor.transpose(b[:, blk * P:(blk + 1) * P], xbc_v[:, blk, c * P:(c + 1) * P],
                                                   ident[:, :])
                    last.then_inc(pe_done, made(("xtok", l, c)))
                    b = product(("ktok", l, c))
                    pe.wait_ge(*due(("k done", l)))
                    for blk in range(3):
                        last = nc.tensor.transpose(b[:, blk * P:(blk + 1) * P], qk_v[:, 3 + blk, c * P:(c + 1) * P],
                                                   ident[:, :])
                    last.then_inc(pe_done, made(("ktok", l, c)))
                for c in range(NT):
                    b = product(("cols", l, c))
                    pe.wait_ge(*due(("rows", l)))
                    for q, r in enumerate((EX, ES, ND, RS)):
                        last = nc.tensor.transpose(b[:, q * P:(q + 1) * P], r[:, c * P:(c + 1) * P], ident[:, :])
                    last.then_inc(pe_done, made(("cols", l, c)))
                b = product(("dcb", l))
                pe.wait_ge(*due(("diag", l)))
                mm(b[:, :], ones[:, :], MX).then_inc(pe_done, made(("dcb", l)))
                stage_end(l, "inproj")

                units = [(i, d, i if d == 0 else BACK[i]) for i in range(NT) for d in range(2)]

                def weights_of(u):
                    i, d, c = units[u]
                    if c < t0:
                        return
                    ck = slice(c * P, (c + 1) * P)
                    for m in range(2):
                        r = slice(64 * m + 32 * d, 64 * m + 32 * d + 32)
                        for j in range(2):
                            b = product(("w", l, u, m, j))
                            mm(b[:, 0:384], ident16[:, :], mask_v[:, d:d + 1, :].broadcast_to([P, 3, P]), True, False)
                            pe.wait_ge(*due(("rlm", l, u)))
                            last = mm(b[:, 0:384], ones[r, :], rlm_v[r, u % 2, j, :, :], False, True)
                            last.then_inc(pe_done, made(("w", l, u, m, j)))
                    for g in range(2):
                        b = product(("cb", l, u, g))
                        mm(b[:, 0:P], xbc_v[64 * g:64 * g + 64, 3, ck], xbc_v[64 * g:64 * g + 64, 4, ck]).then_inc(pe_done, made(("cb", l, u, g)))
                    for j in range(2):
                        b = product(("qkp", l, u, j))
                        for q in range(3):
                            last = mm(b[:, q * P:(q + 1) * P], qk_v[64 * j:64 * j + 64, 3 + q, ck],
                                      qk_v[64 * j:64 * j + 64, q, ck])
                        last.then_inc(pe_done, made(("qkp", l, u, j)))

                def outputs_of(u):
                    i, d, c = units[u]
                    ck = slice(c * P, (c + 1) * P)
                    if c >= t0:
                        b = product(("ys", l, u))
                        pe.wait_ge(*due(("scores", l, u)))
                        pe.wait_ge(*due(("prep", l, u)))
                        for h in range(HEADS):
                            last = mm(b[:, h * HD:(h + 1) * HD], sc_v[:, u % 2, h // 3, (h % 3) * P:(h % 3 + 1) * P],
                                      xdt[:, h * HD:(h + 1) * HD])
                        last.then_inc(pe_done, made(("ys", l, u)))
                        b = product(("mn", l, u))
                        for h in range(HEADS):
                            last = mm(b[:, h * 65:h * 65 + 65],
                                      sc_v[:, u % 2, 2 + h % 2, (h // 2) * P:(h // 2 + 1) * P], va_v[:, c, h, :])
                        last.then_inc(pe_done, made(("mn", l, u)))
                        if i > 0:
                            b = product(("yi", l, u))
                            pe.wait_ge(*due(("state", l, u - 2)))
                            mm(b[:, 0:384], xbc_v[:, 4, ck], sst_v[:, d, :]).then_inc(pe_done, made(("yi", l, u)))
                            b = product(("mi", l, u))
                            for q in range(3):
                                last = mm(b[:, q * 130:q * 130 + 130], qk_v[:, q, ck], cst_v[:, d, q, :, :])
                            last.then_inc(pe_done, made(("mi", l, u)))
                    if i < NT - 1:
                        b = product(("ss", l, u))
                        pe.wait_ge(*due(("prep", l, u)))
                        for g in range(2):
                            last = mm(b[64 * g:64 * g + 64, 192 * g:192 * g + 192], xtok_v[:, c, 384 + 64 * g:384 + 64 * g + 64],
                                      xde[:, 192 * g:192 * g + 192])
                        last.then_inc(pe_done, made(("ss", l, u)))
                        b = product(("cs", l, u))
                        for h in range(HEADS):
                            j, q = h % 2, h // 2
                            last = mm(b[64 * j:64 * j + 64, h * 65:h * 65 + 65], ktok_v[:, c, h * HD:(h + 1) * HD],
                                      ve_v[:, h, :])
                        last.then_inc(pe_done, made(("cs", l, u)))

                weights_of(0)
                for u in range(len(units)):
                    if u + 1 < len(units):
                        weights_of(u + 1)
                    outputs_of(u)
                    if l == 0:
                        for ml, n in MOD_LATER[u * MOD_PER_UNIT:(u + 1) * MOD_PER_UNIT]:
                            modulation(ml, n)
                stage_end(l, "units")
                for t in range(t0, NT):
                    b = product(("yst", l, t))
                    pe.wait_ge(*due(("ssd out", l, t)))
                    for blk in range(3):
                        last = nc.tensor.transpose(b[:, blk * P:(blk + 1) * P], ys_v[:, t, blk * P:(blk + 1) * P],
                                                   ident[:, :])
                    last.then_inc(pe_done, made(("yst", l, t)))
                    b = product(("ymt", l, t))
                    pe.wait_ge(*due(("ml out", l, t)))
                    for blk in range(3):
                        last = nc.tensor.transpose(b[:, blk * P:(blk + 1) * P], hs_v[:, t, blk * P:(blk + 1) * P],
                                                   ident[:, :])
                    last.then_inc(pe_done, made(("ymt", l, t)))
                stage_end(l, "final")
                streams = range(0 if l == 0 else 1, 2)
                for o in range(2):
                    for s in streams:
                        b = product(("hz", l, o, s))
                        pe.wait_ge(*due(("hy z", l, o)))
                        for t in range(2):
                            for c in range(2):
                                last = nc.tensor.transpose(b[:, t * L + c * P:t * L + (c + 1) * P],
                                                           hy_v[:, c, s * L + t * P:s * L + (t + 1) * P], ident[:, :])
                        last.then_inc(pe_done, made(("hz", l, o, s)))
                    for n, mat in enumerate((dftc_v[:, :, 0:P], dftn_v[:, 1, :, :], dftc_v[:, :, P:L],
                                             dfts_v[:, :, P:L])):
                        b = product(("zf", l, o, n))
                        pe.wait_ge(*due(("zt", l, o)))
                        for t in range(2):
                            last = mm(b[:, n0:512], mat[:, t, :], zt_v[:, t, n0:512], t == 0, t == 1)
                        last.then_inc(pe_done, made(("zf", l, o, n)))
                    for c in range(2):
                        b = product(("yt", l, o, c))
                        pe.wait_ge(*due(("yf", l, o)))
                        for s in streams:
                            for q in range(4):
                                inv = invc_v if q < 2 else invs_v
                                last = mm(b[:, s * L:(s + 1) * L], yf_v[:, q, s * L + c * P:s * L + (c + 1) * P],
                                          inv[:, q % 2, :], q == 0, q == 3)
                        last.then_inc(pe_done, made(("yt", l, o, c)))
                stage_end(l, "hyena")
                for s in streams:
                    for q in range(2):
                        b = product(("grow", l, 0, s, q))
                        pe.wait_ge(*due(("gdiag", l, 0, s)))
                        mm(b[:, :], ones[:, :], hsum[:, 512 * q:512 * q + 512]).then_inc(pe_done, made(("grow", l, 0, s, q)))
                for q in range(4):
                    pe.wait_ge(*due(("load", ("wout", l, q))))
                for t in range(t0, NT):
                    for half in range(2):
                        b = product(("out", l, t, half))
                        for q in range(2):
                            w = slot(("wout", l, 2 * half + q), KB)
                            for k in range(KB):
                                last = mm(b[:, 256 * q:256 * q + 256], yT_v[:, k, t * P:(t + 1) * P], w[:, k, :],
                                          k == 0, k == KB - 1)
                        used = [("used", ("wout", l, q)) for q in range(4)] if (t, half) == (NT - 1, 1) else []
                        last.then_inc(pe_done, made(("out", l, t, half), *used))
                stage_end(l, "outproj")
                for k in range(KB):
                    for s in streams:
                        b = product(("h2", l, k, s))
                        pe.wait_ge(*due(("xn", l, 2)))
                        for t in range(2):
                            last = nc.tensor.transpose(b[:, t * P:(t + 1) * P], xn_v[:, 2 * s + t, k::KB], ident[:, :])
                        last.then_inc(pe_done, made(("h2", l, k, s)))
                b = product(("router", l))
                pe.wait_ge(*due(("h2T", l, "act")))
                pe.wait_ge(*due(("h2T", l, "dve")))
                for t in range(t0, NT):
                    for k in range(KB):
                        last = mm(b[:, t * 36:t * 36 + 36], hT_v[:, k, t * P:(t + 1) * P], rw_v[:, k, :],
                                  k == 0, k == KB - 1)
                last.then_inc(pe_done, made(("router", l)))
                for t in range(t0, NT):
                    for half in range(2):
                        b = product(("h2 rows", l, t, half))
                        for k in range(4):
                            last = nc.tensor.transpose(b[:, k * P:(k + 1) * P], hT_v[:, 4 * half + k, t * P:(t + 1) * P],
                                                       ident[:, :])
                        last.then_inc(pe_done, made(("h2 rows", l, t, half)))
                b = product(("rank", l))
                pe.wait_ge(*due((f"route{l}_in",)))
                pe.wait_ge(*due(("chosen", l)))
                for t in range(t0, NT):
                    for before in range(t0, t):
                        mm(b[:, 32 * t:32 * t + 32], ones[:, :], chosen_v[:, before, :], before == t0, False)
                    mm(b[:, 32 * t:32 * t + 32], tri, chosen_v[:, t, :], t == t0, True)
                for t in range(t0, NT):
                    last = mm(b[:, P:P + 32], ones[:, :], chosen_v[:, t, :], t == t0, t == NT - 1)
                last.then_inc(pe_done, made(("rank", l)))
                b = product(("tables", l))
                combos = [y * NT + t for y in range(2) for t in range(t0, NT)]
                for n in combos:
                    pe.wait_ge(*due(("one-hot", l, n)))
                    last = mm(b[:, 0:3 * ITEMS], slot_hot[:, n, :], item_hot[:, n, :, :], n == combos[0], n == combos[-1])
                last.then_inc(pe_done, made(("tables", l)))
                for s in streams:
                    for q in range(2):
                        b = product(("grow", l, 1, s, q))
                        pe.wait_ge(*due(("gdiag", l, 1, s)))
                        mm(b[:, :], ones[:, :], hsum[:, 512 * q:512 * q + 512]).then_inc(pe_done, made(("grow", l, 1, s, q)))
                stage_end(l, "router")

                base = len(products)
                tag = ("moe", l)
                before = dict(tally.count)
                with pe.Fori(0, BODIES) as i:
                    tally.turn = (tag, i)
                    for n, (what, j, *half) in enumerate(TURN):
                        name = ("turn", l, n)
                        at[("bank", name)] = (base + n) % BANKS
                        if n >= BANKS:
                            pe.wait_ge(*due(("read", ("turn", l, n - BANKS))))
                        else:
                            pe.wait_ge(*due(("read", ("turn", l, len(TURN) - BANKS + n)), 1))
                        b = banks[(base + n) % BANKS]
                        used = []
                        if what == "gathered":
                            if half[0] == 0:
                                pe.wait_ge(*due(("rows", l, j)))
                            for k in range(4):
                                c0 = (4 * half[0] + k) * P
                                last = nc.tensor.transpose(b[:, k * P:(k + 1) * P], rows_v[:, j, c0:c0 + P], ident[:, :])
                        elif what == "gate up":
                            pe.wait_ge(*due(("rowsT", l, j, 0)))
                            pe.wait_ge(*due(("rowsT", l, j, 1)))
                            for y in range(2):
                                key = ("expert", l, 3 * j + y)
                                used.append(("used", key))
                                pe.wait_ge(*due(("load", key)))
                                w = slot(key, KB)
                                for k in range(KB):
                                    last = mm(b[:, EH * y:EH * y + EH], rowsT_v[:, j % 2, k, :], w[:, k, :],
                                              k == 0, k == KB - 1)
                        elif what == "hidden":
                            pe.wait_ge(*due(("hid", l, j)))
                            for f in range(2):
                                last = nc.tensor.transpose(b[:, f * P:(f + 1) * P], hid_v[:, j % 2, f * P:(f + 1) * P],
                                                           ident[:, :])
                        else:
                            key = ("expert", l, 3 * j + 2)
                            if half[0] == 0:
                                pe.wait_ge(*due(("load", key)))
                                pe.wait_ge(*due(("hidT", l, j)))
                            else:
                                used.append(("used", key))
                            w = slot(key, 2)
                            for f in range(2):
                                last = mm(b[:, :], hidT_v[:, j % 2, f * P:(f + 1) * P],
                                          w[:, f, 512 * half[0]:512 * half[0] + 512], f == 0, f == 1)
                        last.then_inc(pe_done, made(name, *used))
                tally.looped(tag, before, BODIES)
                per = at[("per", tag, "pe_done")]
                for j in range(3 * PER_BODY):
                    at[("used", ("expert-last", l, j))] = (
                        "pe_done", at[("used", ("expert", l, j))][1] + per * (BODIES - 1))
                for n in range(len(TURN)):
                    products.append(("turn", l, n))
                stage_end(l, "moe")
                with pe.If(pe.value_load(more_flag[0:1, :], min_val=0, max_val=MORE_ITEMS) != 0):
                    pe.nop().then_inc(more_pe[l], 1)
                    with pe.Fori(0, MORE_ITEMS) as i:
                        pe.wait_ge(more_rows_in[l], i * 16 + 16)
                        for k in range(KB):
                            last = nc.tensor.transpose(banks[k // 4][:, k % 4 * P:(k % 4 + 1) * P],
                                                       rows_v[:, 3, k * P:(k + 1) * P], ident[:, :])
                        last.then_inc(more_pe[l], 1)
                        pe.wait_ge(more_dve[l], i * MORE_DVE + 2)
                        pe.wait_ge(more_weights[l], i * 48 + 48)
                        for y in range(2):
                            for k in range(KB):
                                last = mm(banks[2][:, EH * y:EH * y + EH], rowsT_v[:, 0, k, :], slot_v(y, KB)[:, k, :],
                                          k == 0, k == KB - 1)
                        last.then_inc(more_pe[l], 1)
                        pe.wait_ge(more_dve[l], i * MORE_DVE + 3)
                        for f in range(2):
                            last = nc.tensor.transpose(banks[3][:, f * P:(f + 1) * P], hid_v[:, 0, f * P:(f + 1) * P],
                                                       ident[:, :])
                        last.then_inc(more_pe[l], 1)
                        pe.wait_ge(more_dve[l], i * MORE_DVE + 4)
                        for half in range(2):
                            for f in range(2):
                                last = mm(banks[4 + half][:, :], hidT_v[:, 0, f * P:(f + 1) * P],
                                          slot_v(2, 2)[:, f, 512 * half:512 * half + 512], f == 0, f == 1)
                        last.then_inc(more_pe[l], 1)
                    pe.wait_ge(more_dve[l], MORE_ITEMS * MORE_DVE)

        def consumer(who, eng, sem_name):
            done = tally.sems[sem_name]

            def step(ins, *names):
                ins.then_inc(done, tick(sem_name, ("own", who), *names))
                eng.wait_ge(*due(("own", who)))

            def bank(name):
                return banks[at[("bank", name)]]

            def stage_end(l, stage):
                eng.drain().then_inc(done, tick(sem_name, ("end", who, l, stage)))
                for other in ("pe", "act", "dve"):
                    if other != who:
                        eng.wait_ge(*due(("end", other, l, stage)))
            return step, bank, stage_end

        @block.gpsimd
        def _(pool):
            def rows_of(column, dst, src, n, out_side, bound):
                nc.gpsimd.tensor_copy(index[:, n:n + 1], column)
                pool.drain()
                where = bass.IndirectOffsetOnAxis(index[:, n:n + 1], 0)
                return nc.gpsimd.indirect_dma_start(dst, where if out_side else None, src,
                                                    None if out_side else where, bounds_check=bound,
                                                    oob_is_err=False)

            for l in range(DEPTH):
                t0 = 0 if l == 0 else 2
                for t in range(t0, NT):
                    pool.wait_ge(*due(("h2 staged", l, t)))
                    pool.dma_start(h2_rows[t * P:(t + 1) * P, :], xn_v[:, t, :]).then_inc(
                        rows_out[t % 2], tick(f"rows{t % 2}_out", ("h2 written", l, t % 2), by=16))
                pool.wait_ge(*due(("h2 written", l, 0)))
                pool.wait_ge(*due(("h2 written", l, 1)))
                pool.wait_ge(*due(("item tables", l)))
                tag = ("moe", l)
                for j in range(AHEAD):
                    name = ("rows", l, j)
                    at[("in", tag, name)] = True
                    rows_of(token_of[:, j:j + 1], rows_v[:, j, :], h2_rows, j, False, NT * P - 1).then_inc(
                        rows_in[j], tick(f"rows{j}_in", name, by=16))
                before = dict(tally.count)
                with pool.Fori(0, BODIES) as i:
                    tally.turn = (tag, i)
                    for j in range(PER_BODY):
                        if j:
                            pool.wait_ge(*due(("made", ("turn", l, TURN.index(("gathered", j - 1, 1))))))
                        else:
                            pool.wait_ge(*due(("made", ("turn", l, TURN.index(("gathered", PER_BODY - 1, 1)))), 1))
                        u = (j + AHEAD) % 4
                        rows_of(token_of[:, bass.ds(i * PER_BODY + j + AHEAD, 1)], rows_v[:, u, :], h2_rows, u, False,
                                NT * P - 1).then_inc(
                            rows_in[u], tick(f"rows{u}_in", *([("rows", l, u)] if j == 0 else []), by=16))
                        pool.wait_ge(*due(("result", l, j, "act")))
                        pool.wait_ge(*due(("result", l, j, "dve")))
                        rows_of(pair_of[:, bass.ds(i * PER_BODY + j, 1)], pair_rows, res_v[:, j % 2, :], 4 + j % 2,
                                True, MOST_PAIRS - 1).then_inc(
                            rows_out[j % 2], tick(f"rows{j % 2}_out", ("scattered", l, j), by=16))
                tally.looped(tag, before, BODIES)
                for u in range(2):
                    pool.wait_ge(rows_out[u], tally.count[f"rows{u}_out"])
                for u in range(4):
                    pool.wait_ge(rows_in[u], tally.count[f"rows{u}_in"])
                for who in ("pe", "act", "dve"):
                    pool.wait_ge(*due(("end", who, l, "moe")))
                with pool.If(pool.value_load(more_flag[0:1, :], min_val=0, max_val=MORE_ITEMS) != 0):
                    with pool.Fori(0, MORE_ITEMS) as i:
                        pool.wait_ge(more_pe[l], i * MORE_PRODUCTS + 1)
                        rows_of(token_of[:, bass.ds(i + EXPERTS, 1)], rows_v[:, 3, :], h2_rows, 3, False,
                                NT * P - 1).then_inc(more_rows_in[l], 16)
                        pool.wait_ge(more_dve[l], i * MORE_DVE + MORE_DVE)
                        rows_of(pair_of[:, bass.ds(i + EXPERTS, 1)], pair_rows, res_v[:, 0, :], 4, True,
                                MOST_PAIRS - 1).then_inc(more_rows_out[l], 16)
                        pool.wait_ge(more_rows_out[l], i * 16 + 16)
                pool.drain().then_inc(pool_done, tick("pool_done", ("pairs written", l)))

        @block.scalar
        def _(act):
            step, bank, stage_end = consumer("act", act, "act_done")

            def fn(o, i, f, *names, **k):
                step(nc.scalar.activation(o, i, f, **k), *names)

            act.wait_ge(*due(("consts_in",)))
            fn(cond[:, :], cond[:, :], ACT.Silu, ("cond",))
            def mod_rows(l, n):
                act.wait_ge(*due(("made", ("mod", l, n))))
                if n % 2 == 0 and (l, n) != (0, 0):
                    pl, pn = (l, n - 2) if n else (l - 1, MOD_SLOTS - 2)
                    act.wait_ge(*due(("made", ("modc", pl, pn // 4, pn % 4 // 2))))
                fn(modrow[0:2, 256 * (n % 2):256 * (n % 2) + 256], bank(("mod", l, n))[0:2, 0:256], ACT.Copy,
                   ("read", ("mod", l, n)), ("modrow", l, n))

            for l in range(DEPTH):
                t0 = 0 if l == 0 else 2
                n0 = t0 * P
                if l == 0:
                    for n in range(MOD_FIRST):
                        mod_rows(0, n)
                for n in range(2):
                    act.wait_ge(*due(("ranged", l, n)))
                    fn(hid_c[0:FH, :], hid_b[0:FH, :], ACT.Sin, ("sin", l, n))
                act.wait_ge(*due(("decay", l)))
                for t in range(2):
                    fn(tabs_v[:, t, :, :, :], grow[:, 0:1024].rearrange("p (e o c) -> p e o c", e=2, o=2), ACT.Exp,
                       ("window", l, t), scale=tcol[:, t:t + 1])
                act.wait_ge(*due(("tapped", l)))
                fn(tabs_v[:, :, :, :, :], taps_v[:, :, :, :, :], ACT.Abs, ("tabs", l))
                stage_end(l, "mod")

                def square_sums(n, src):
                    for t in range(t0 if n != 1 else 0, NT):
                        fn(hsum[:, 0:D], src[:, t, :], ACT.Square, ("ss", l, n, t), accum_out=small[:, t:t + 1])
                    act.wait_ge(*due(("rinv", l, n)))
                    fn(small[:, 4:8], small[:, 4:8], ACT.Sqrt, ("rstd", l, n))

                act.wait_ge(*due(("x_in",)))
                square_sums(1, x_v)
                for k in range(KB):
                    act.wait_ge(*due(("made", ("h1", l, k, 0))))
                    b = bank(("h1", l, k, 0))
                    fn(hT_v[:, k, 0:L], b[:, 0:L], ACT.Identity, ("read", ("h1", l, k, 0)),
                       scale=ab_v[:, 0, k, 1:2], bias=ab_v[:, 1, k, 1:2])
                stage_end(l, "norm1")
                act.wait_ge(*due(("g1", l)))
                fn(t1, U, ACT.Exp, ("g2", l))
                fn(t2, t1, ACT.Ln, ("g3", l), bias=1.0)
                fn(gcolp[:, 3:4], gcolp[:, 2:3], ACT.Exp, ("acoef", l))
                act.wait_ge(*due(("g4", l)))
                fn(EX, U, ACT.Exp)
                for c in range(NT):
                    fn(ES[:, c * P:(c + 1) * P], RS[:, c * P:(c + 1) * P], ACT.Exp, bias=small[:, 8 + c:9 + c])
                fn(ND[64:128, :], MX[64:128, :], ACT.Exp, ("rows", l), scale=-1.0)
                for blk in range(6):
                    a0 = n0 if blk < 3 else 0
                    act.wait_ge(*due(("conv", "qk", l, blk)))
                    fn(qk_v[:, blk, a0:512], qk_v[:, blk, a0:512], ACT.Silu, ("silu qk", l, blk))
                for blk in range(5):
                    act.wait_ge(*due(("conv", "xbc", l, blk)))
                    fn(xbc_v[:, blk, :], xbc_v[:, blk, :], ACT.Silu, ("xbc done", l))
                for t in range(NT):
                    act.wait_ge(*due(("made", ("v", l, t))))
                    b = bank(("v", l, t))
                    fn(va_v[:, t, :, 0:HD], b[:, 0:384].rearrange("p (h c) -> p h c", h=HEADS), ACT.Copy,
                       ("read", ("v", l, t)))
                for t in range(t0, NT):
                    act.wait_ge(*due(("made", ("z", l, t))))
                    b = bank(("z", l, t))
                    fn(z_v[:, t, :], b[:, 0:384], ACT.Silu, ("read", ("z", l, t)))
                for t in range(t0, NT):
                    act.wait_ge(*due(("made", ("o", l, t))))
                    b = bank(("o", l, t))
                    fn(o_v[:, t, :], b[:, 0:384], ACT.Sigmoid, ("read", ("o", l, t)))
                for c in range(NT):
                    act.wait_ge(*due(("made", ("xtok", l, c))))
                    b = bank(("xtok", l, c))
                    fn(xtok_v[:, c, :], b[:, :], ACT.Copy, ("read", ("xtok", l, c)))
                    act.wait_ge(*due(("made", ("ktok", l, c))))
                    b = bank(("ktok", l, c))
                    fn(ktok_v[:, c, :], b[:, 0:384], ACT.Copy, ("read", ("ktok", l, c)))
                for c in range(NT):
                    act.wait_ge(*due(("made", ("cols", l, c))))
                    b = bank(("cols", l, c))
                    fn(cols_v[:, c, :, :], b[:, :], ACT.Copy, ("read", ("cols", l, c)))
                act.wait_ge(*due(("made", ("dcb", l))))
                b = bank(("dcb", l))
                fn(dcb[:, :], b[:, :], ACT.Copy, ("read", ("dcb", l)))
                stage_end(l, "inproj")
                units = [(i, d, i if d == 0 else BACK[i]) for i in range(NT) for d in range(2)]
                def segments(u):
                    i, d, c = units[u]
                    if c < t0:
                        return
                    for m in range(2):
                        for j in range(2):
                            act.wait_ge(*due(("made", ("w", l, u, m, j))))
                            b = bank(("w", l, u, m, j))
                            if u >= 2 and units[u - 2][2] >= t0:
                                act.wait_ge(*due(("made", ("mn", l, u - 2))))
                            for q in range(3):
                                h = 3 * j + q if m == 0 else 2 * q + j
                                names = [("read", ("w", l, u, m, j)), ("seg", l, u, m, j)] if q == 2 else []
                                fn(sc_v[:, u % 2, 2 * m + j, q * P:(q + 1) * P], b[:, q * P:(q + 1) * P], ACT.Exp,
                                   *names, bias=cols_v[:, c, 3, 64 * m + 32 * d + h:64 * m + 32 * d + h + 1])

                segments(0)
                for u in range(len(units)):
                    if u + 1 < len(units):
                        segments(u + 1)
                    if l == 0:
                        for ml, n in MOD_LATER[u * MOD_PER_UNIT:(u + 1) * MOD_PER_UNIT]:
                            mod_rows(ml, n)
                stage_end(l, "units")
                for t in range(t0, NT):
                    act.wait_ge(*due(("gated", l, t)))
                    fn(wv[:, 0:384], ys_v[:, t, :], ACT.Square, ("ssq", l, t), accum_out=small[:, t:t + 1])
                act.wait_ge(*due(("rinv", l, 3)))
                fn(small[:, 4:8], small[:, 4:8], ACT.Sqrt, ("rstd", l, 3))
                act.wait_ge(*due(("rinv", l, 4)))
                fn(small[:, 12:12 + 6 * NT], small[:, 12:12 + 6 * NT], ACT.Sqrt, ("rstd", l, 4))
                for t in range(t0, NT):
                    for name, row, y0 in (("yst", 68, 0), ("ymt", 71, 5)):
                        act.wait_ge(*due(("made", (name, l, t))))
                        b = bank((name, l, t))
                        for blk in range(3):
                            names = [("read", (name, l, t))] if blk == 2 else []
                            o, i_ = yT_v[:, y0 + blk, t * P:(t + 1) * P], b[:, blk * P:(blk + 1) * P]
                            if l % 2:
                                w0 = (t - 2) * P // ROWS
                                o = yT_v[:, y0 + blk, L:2 * L].rearrange("p (r w) -> p w r", r=ROWS)[
                                    :, w0:w0 + P // ROWS, :]
                                i_ = i_.rearrange("p (w r) -> p w r", r=ROWS)
                            fn(o, i_, ACT.Copy, *names,
                               scale=pcol[:, row + blk:row + blk + 1])
                stage_end(l, "final")
                streams = range(0 if l == 0 else 1, 2)
                for o in range(2):
                    for s in streams:
                        act.wait_ge(*due(("made", ("hz", l, o, s))))
                        b = bank(("hz", l, o, s))
                        names = [("zt", l, o)] if s == 1 else []
                        fn(zt_v[:, :, s * L:(s + 1) * L], b[:, :].rearrange("p (t c) -> p t c", t=2), ACT.Copy,
                           ("read", ("hz", l, o, s)), *names)
                stage_end(l, "hyena")
                for s in streams:
                    for q in range(2):
                        act.wait_ge(*due(("made", ("grow", l, 0, s, q))))
                        b = bank(("grow", l, 0, s, q))
                        fn(grow_v[:, s, :].rearrange("p (j k) -> p k j", k=KB)[:, 4 * q:4 * q + 4, :], b[:, :].rearrange(
                            "p (k j) -> p k j", k=4), ACT.Copy, ("read", ("grow", l, 0, s, q)), ("grow in", l, 0, s))
                stage_end(l, "outproj")
                square_sums(2, x_v)
                if l == 0:
                    for k in range(KB):
                        act.wait_ge(*due(("made", ("h2", l, k, 0))))
                        b = bank(("h2", l, k, 0))
                        fn(hT_v[:, k, 0:L], b[:, 0:L], ACT.Identity, ("read", ("h2", l, k, 0)),
                           scale=ab_v[:, 2, k, 1:2], bias=ab_v[:, 3, k, 1:2])
                step(nc.scalar.activation(small[:, 40:41], small[:, 4:5], ACT.Copy), ("h2T", l, "act"))
                for t in range(t0, NT):
                    for half in range(2):
                        act.wait_ge(*due(("made", ("h2 rows", l, t, half))))
                        fn(xn_v[:, t, 512 * half:512 * half + 512], bank(("h2 rows", l, t, half))[:, :], ACT.Copy,
                           ("read", ("h2 rows", l, t, half)), ("h2 staged", l, t))
                act.wait_ge(*due(("r1", l)))
                fn(otok[:, 0:16], otok[:, 0:16], ACT.Exp, ("r2", l))
                act.wait_ge(*due(("r3", l)))
                fn(otok[:, 16:20], otok[:, 16:20], ACT.Exp, ("r4", l))
                for s in streams:
                    for q in range(2):
                        act.wait_ge(*due(("made", ("grow", l, 1, s, q))))
                        b = bank(("grow", l, 1, s, q))
                        fn(grow_v[:, s, :].rearrange("p (j k) -> p k j", k=KB)[:, 4 * q:4 * q + 4, :], b[:, :].rearrange(
                            "p (k j) -> p k j", k=4), ACT.Copy, ("read", ("grow", l, 1, s, q)), ("grow in", l, 1, s))
                stage_end(l, "router")
                tag = ("moe", l)
                before = dict(tally.count)
                with act.Fori(0, BODIES) as i:
                    tally.turn = (tag, i)
                    for n, (what, j, *half) in enumerate(TURN):
                        name = ("turn", l, n)
                        if what == "hidden" or half == [0]:
                            continue
                        if what == "gathered":
                            if j >= 2:
                                act.wait_ge(*due(("made", ("turn", l, TURN.index(("gate up", j - 2))))))
                            else:
                                act.wait_ge(*due(("made", ("turn", l, TURN.index(("gate up", j + 2)))), 1))
                            act.wait_ge(*due(("made", name)))
                            fn(rowsT_v[:, j % 2, 4:8, :], bank(name)[:, :].rearrange("p (k n) -> p k n", k=4), ACT.Copy,
                               ("read", name), ("rowsT", l, j, 1))
                        elif what == "gate up":
                            if j >= 2:
                                act.wait_ge(*due(("hid", l, j - 2)))
                            else:
                                act.wait_ge(*due(("hid", l, j + 2), 1))
                            act.wait_ge(*due(("made", name)))
                            fn(sg_v[:, j % 2, :], bank(name)[:, 0:EH], ACT.Silu, ("sg", l, j))
                        else:
                            if j >= 2:
                                act.wait_ge(*due(("scattered", l, j - 2)))
                            else:
                                act.wait_ge(*due(("scattered", l, j + 2), 1))
                            act.wait_ge(*due(("made", name)))
                            fn(res_v[:, j % 2, 512:1024], bank(name)[:, :], ACT.Copy, ("read", name),
                               ("result", l, j, "act"), scale=weight_of[:, bass.ds(i * PER_BODY + j, 1)])
                tally.looped(tag, before, BODIES)
                stage_end(l, "moe")
                with act.If(act.value_load(more_flag[0:1, :], min_val=0, max_val=MORE_ITEMS) != 0):
                    with act.Fori(0, MORE_ITEMS) as i:
                        act.wait_ge(more_pe[l], i * MORE_PRODUCTS + 3)
                        nc.scalar.activation(sg_v[:, 0, :], banks[2][:, 0:EH], ACT.Silu).then_inc(more_act[l], 1)
            t0 = 2
            for t in range(2, NT):
                act.wait_ge(*due(("x done", DEPTH - 1)))
                fn(hsum[:, 0:D], x_v[:, t, :], ACT.Square, ("ss", "f", t), accum_out=small[:, t:t + 1])
            act.wait_ge(*due(("rinv", "f")))
            fn(small[:, 4:8], small[:, 4:8], ACT.Sqrt, ("rstd", "f"), ("fnw free",))

        @block.vector
        def _(dve):
            step, bank, stage_end = consumer("dve", dve, "dve_done")
            V = nc.vector

            def ts(o, a, s1, s2, op0, op1, *names):
                step(V.tensor_scalar(o, a, s1, s2, op0, op1) if op1 is not None else
                     V.tensor_scalar(o, a, s1, None, op0), *names)

            def tt(o, a, b, op, *names):
                step(V.tensor_tensor(o, a, b, op), *names)

            def stt(o, a, s, b, op0, op1, *names):
                step(V.scalar_tensor_tensor(o, a, s, b, op0, op1), *names)

            def copy(o, a, *names):
                step(V.tensor_copy(o, a), *names)

            MUL, ADD, SUB, MAX, MIN = ALU.mult, ALU.add, ALU.subtract, ALU.max, ALU.min

            step(V.memset(gcolp[:, :], 0.0), ("gcolp zero",))
            step(V.memset(ones[:, :], 1.0))
            dve.wait_ge(*due(("consts_in",)))
            copy(ident16[:, :], ident[:, :])
            copy(mask16[:, :], big[:, 0:2 * P])
            step(V.memset(vaug[:, :], 1.0))
            step(V.memset(sst[:, :], 0.0))
            step(V.memset(cst[:, :], 0.0))
            step(V.memset(small[:, :], 1.0))
            step(V.memset(hT[:, :], 0.0))
            def mod_columns(l, n):
                m, h = n // 4, n % 4 // 2
                r = slice(64 * h, 64 * h + 64)
                dve.wait_ge(*due(("made", ("modc", l, m, h))))
                tt(modc_v[r, l, m, :, :], bank(("modc", l, m, h))[0:64, 0:16].rearrange("p (k s) -> p k s", s=2),
                   bmod_v[r, l, m, :].unsqueeze(2).broadcast_to([64, KB, 2]), ADD, ("read", ("modc", l, m, h)))

            for l in range(DEPTH):
                t0 = 0 if l == 0 else 2
                n0 = t0 * P
                streams = range(0 if l == 0 else 1, 2)

                def modulators(n):
                    stt(ab_v[:, 2 * n, :, :], modc_v[:, l, 3 * n + 1, :, :], 1.0,
                        nw_v[:, n, :].unsqueeze(2).broadcast_to([P, KB, 2]), ADD, MUL)
                    copy(ab_v[:, 2 * n + 1, :, :], modc_v[:, l, 3 * n, :, :], ("ab", l))

                dve.wait_ge(*due((f"params{l}_in",)))
                dve.wait_ge(*due(("made", ("pcol", l))))
                b = bank(("pcol", l))
                copy(pcol[:, 0:78], b[:, 0:78], ("read", ("pcol", l)))
                stt(grow[:, 0:1024], grow[:, 0:1024], -1.0, grow[:, 0:1024], MUL, MAX, ("decay", l))
                step(V.memset(wg, 0.0))
                for d in range(2):
                    copy(wg_v[:, :, 0, 32 * d:32 * d + 6], wgr_v[:, :, 6 * d:6 * d + 6])
                    copy(wg_v[:, :, 1, 64 + 32 * d:70 + 32 * d], wgr_v[:, :, 12 + 12 * d:18 + 12 * d])
                    copy(wg_v[:, :, 0, 64 + 32 * d:70 + 32 * d], wgr_v[:, :, 18 + 12 * d:24 + 12 * d], ("wg", l))
                if l == 0:
                    for n in range(1, MOD_FIRST, 2):
                        mod_columns(0, n)
                modulators(0)
                two_pi = 2 * np.pi
                c1 = 6.28125
                c2 = float(np.float32(two_pi - c1))
                c3 = float(np.float32(two_pi - c1 - c2))
                for n in range(2):
                    dve.wait_ge(*due(("made", (f"hid{n + 1}", l))))
                    b = bank((f"hid{n + 1}", l))
                    a, k_ = hid_b[0:FH, :], hid_a[0:FH, :]
                    ts(a, b[0:FH, 0:L], hcol[0:FH, n:n + 1], hcol[0:FH, 2:3], ADD, MUL, ("read", (f"hid{n + 1}", l)))
                    ts(k_, a, 1.0 / two_pi, MAGIC, MUL, ADD)
                    ts(k_, k_, MAGIC, None, SUB, None)
                    for cc in (c1, c2, c3):
                        stt(a, k_, -cc, a, MUL, ADD)
                    ts(a, a, 3.1415925, -3.1415925, MIN, MAX, ("ranged", l, n))
                for t in range(2):
                    for e in range(2):
                        dve.wait_ge(*due(("window", l, t)))
                        dve.wait_ge(*due(("made", ("taps", l, t, e))))
                        b = bank(("taps", l, t, e))
                        tt(taps_v[:, t, e, :, :], tabs_v[:, t, e, :, :], b[:, :].rearrange("p (o c) -> p o c", o=2), MUL,
                           ("read", ("taps", l, t, e)))
                ts(taps_v[:, 0, 1, :, :], taps_v[:, 0, 1, :, :], tcol[:, 2:3], None, MUL, None, ("tapped", l))
                dve.wait_ge(*due(("tabs", l)))
                hd = tabs_v[:, :, 0, :, :]
                dve.wait_ge(*due(("made", ("tapsum", l))))
                for t in range(2):
                    tt(hd[:, t], taps_v[:, t, 0], taps_v[:, t, 1], SUB)
                    tt(taps_v[:, t, 0], taps_v[:, t, 0], taps_v[:, t, 1], ADD)
                    copy(taps_v[:, t, 1], hd[:, t], ("tapsd", l))
                dve.wait_ge(*due(("made", ("tapsum", l))))
                b = bank(("tapsum", l))
                step(V.reciprocal(small[:, 44:48], b[:, 0:4]), ("read", ("tapsum", l)))
                for n in range(5):
                    dve.wait_ge(*due(("made", ("spec", l, n))))
                    b = bank(("spec", l, n))
                    copy(hf_v[:, n, :], b[:, :], ("read", ("spec", l, n)))
                stage_end(l, "mod")

                def rms(n, src, cols_, width, tiles, name=None):
                    ts(small[:, 4:8], small[:, 0:4], 1.0 / width, EPS, MUL, ADD)
                    step(V.reciprocal(small[:, 4:8], small[:, 4:8]), n)

                def norm(n, first_tile):
                    for t in range(first_tile, NT):
                        dve.wait_ge(*due(("ss", l, n, t)))
                    rms(("rinv", l, n), None, None, D, None)
                    dve.wait_ge(*due(("rstd", l, n)))
                    for t in range(first_tile, NT):
                        ts(xn_v[:, t, :], x_v[:, t, :], small[:, 4 + t:5 + t], None, MUL, None, ("xn", l, n))

                norm(1, 0)
                for k in range(KB):
                    dve.wait_ge(*due(("made", ("h1", l, k, 1))))
                    b = bank(("h1", l, k, 1))
                    o = hT_v[:, k, L:2 * L]
                    i_ = b[:, 0:L]
                    if l % 2:
                        o = o.rearrange("p (w r) -> p r w", r=ROWS)
                        i_ = i_.rearrange("p (r w) -> p r w", r=ROWS)
                    ts(o, i_, ab_v[:, 0, k, 0:1], ab_v[:, 1, k, 0:1], MUL, ADD, ("read", ("h1", l, k, 1)))
                stage_end(l, "norm1")
                dve.wait_ge(*due(("made", ("gates", l, 0))))
                b = bank(("gates", l, 0))
                sp_in, na = t3, U
                ts(sp_in, b[:, :], gcolp[:, 0:1], tcol[:, 3:4], ADD, MUL, ("read", ("gates", l, 0)))
                stt(na, sp_in, -1.0, sp_in, MUL, MIN, ("g1", l))
                dve.wait_ge(*due(("g3", l)))
                dve.wait_ge(*due(("acoef", l)))
                ts(SP, t1, 1.0, None, ADD, None)
                stt(U, SP, -1.0, t1, ADD, SUB)
                step(V.reciprocal(SP, SP))
                tt(U, U, SP, MUL)
                tt(t2, t2, U, SUB)
                stt(SP, sp_in, 0.0, t2, MAX, ADD)
                stt(t1, SP, -1.0, gcolp[:, 3:4].broadcast_to([P, 512]), MUL, MUL)
                for m in range(2):
                    f, r = slice(64 * m, 64 * m + 32), slice(64 * m + 32, 64 * m + 64)
                    step(V.tensor_tensor_scan(CUM[f, :], keep[f, :], t1[f, :], 0.0, MUL, ADD))
                    step(V.tensor_tensor_scan(CUM[r, ::-1], keep[r, ::-1], t1[r, ::-1], 0.0, MUL, ADD))
                s_, m_ = slice(0, 64), slice(64, 128)
                copy(RL[s_, :], CUM[s_, :])
                ts(RS[s_, :], CUM[s_, :], -1.0, None, MUL, None)
                copy(ND[s_, :], SP[s_, :])
                dve.wait_ge(*due(("made", ("gates", l, 1))))
                b = bank(("gates", l, 1))
                stt(RS[m_, :], b[m_, :], gcolp[m_, 1:2], CUM[m_, :], ADD, SUB, ("read", ("gates", l, 1)))
                step(V.memset(t2[m_, :], 0.0))
                copy(t2[64:96, P::P], CUM[64:96, P - 1:511:P])
                for a, z in ((127, 128), (511, 0), (383, 384)):
                    copy(t2[96:128, a:a + 1], CUM[96:128, z:z + 1])
                step(V.tensor_tensor_scan(MX[64:96, :], t2[64:96, :], RS[64:96, :], 0.0, ADD, MAX))
                step(V.tensor_tensor_scan(MX[96:128, 255::-1], t2[96:128, 255::-1], RS[96:128, 255::-1], 0.0, ADD, MAX))
                step(V.tensor_tensor_scan(MX[96:128, 511:255:-1], t2[96:128, 511:255:-1], RS[96:128, 511:255:-1],
                                          MX[96:128, 0:1], ADD, MAX))
                ts(RL[m_, :], MX[m_, :], -1.0, None, MUL, None)
                mc = small[:, 36:40]
                step(V.memset(mc[m_, :], 0.0))
                tt(mc[64:96, 1:4], CUM[64:96, P - 1:511:P], MX[64:96, P - 1:511:P], ADD)
                for c, z in ((0, 128), (3, 0), (2, 384)):
                    tt(mc[96:128, c:c + 1], CUM[96:128, z:z + 1], MX[96:128, z:z + 1], ADD)
                copy(U[s_, :], CUM[s_, :])
                for c in range(NT):
                    ts(U[m_, c * P:(c + 1) * P], RL[m_, c * P:(c + 1) * P], mc[m_, c:c + 1], None, ADD, None)
                for m in range(2):
                    copy(small[64 * m:64 * m + 32, 8:12], RL[64 * m:64 * m + 32, P - 1::P])
                    copy(small[64 * m + 32:64 * m + 64, 8:12], RL[64 * m + 32:64 * m + 64, 0::P])
                tt(MX[m_, :], MX[m_, :], CUM[m_, :], ADD, ("g4", l))
                def conv(name, blk, dst, w0, b0, nb, lo):
                    dve.wait_ge(*due(("made", (name, l, blk))))
                    b = bank((name, l, blk))
                    o = dst[:, blk, :].rearrange("p (s n) -> p s n", s=2)[:, lo:, :]
                    i_ = b[:, :].rearrange("p (s n) -> p s n", s=2)[:, lo:, :]
                    wc = [pcol[:, w0 + nb * k + blk:w0 + nb * k + blk + 1] for k in range(3)]
                    ts(o, i_, wc[1], pcol[:, b0 + blk:b0 + blk + 1], MUL, ADD)
                    stt(o[:, :, 1:L], i_[:, :, 0:L - 1], wc[0], o[:, :, 1:L], MUL, ADD)
                    stt(o[:, :, 0:L - 1], i_[:, :, 1:L], wc[2], o[:, :, 0:L - 1], MUL, ADD,
                        ("read", (name, l, blk)), ("conv", name, l, blk))

                for blk in range(6):
                    conv("qk", blk, qk_v, 44, 62, 6, t0 // 2 if blk < 3 else 0)
                for blk in range(3, 6):
                    dve.wait_ge(*due(("silu qk", l, blk)))
                    ts(qk_v[:, blk, :], qk_v[:, blk, :], HD ** -0.5, None, MUL, None, ("k done", l))
                for blk in range(5):
                    conv("xbc", blk, xbc_v, 0, 15, 5, 0)
                for blk in range(6):
                    conv("hy", blk, hy_v, 20, 38, 6, t0 // 2)
                dve.wait_ge(*due(("rows", l)))
                last_ex = small[:, 48:52]
                for m in range(2):
                    copy(last_ex[64 * m:64 * m + 32, :], EX[64 * m:64 * m + 32, P - 1::P])
                    copy(last_ex[64 * m + 32:64 * m + 64, :], EX[64 * m + 32:64 * m + 64, 0::P])
                tt(MX.rearrange("p (c r) -> p c r", c=NT), ident[:, :].unsqueeze(1).broadcast_to([P, NT, P]),
                   last_ex.unsqueeze(2).broadcast_to([P, NT, P]), MUL, ("diag", l))
                stage_end(l, "inproj")

                units = [(i, d, i if d == 0 else BACK[i]) for i in range(NT) for d in range(2)]
                written = set()

                def spread(u):
                    i, d, c = units[u]
                    if c < t0:
                        return
                    if u >= 2 and units[u - 2][2] >= t0:
                        dve.wait_ge(*due(("made", ("w", l, u - 2, 1, 1))))
                    for j in range(2):
                        tt(rlm_v[:, u % 2, j, :, :], sel_v[:, j, :, :],
                           RL[:, c * P:(c + 1) * P].unsqueeze(1).broadcast_to([P, 3, P]), MUL, ("rlm", l, u))

                def scores(u):
                    i, d, c = units[u]
                    if c < t0:
                        return
                    for g in range(2):
                        dve.wait_ge(*due(("made", ("cb", l, u, g))))
                        b = bank(("cb", l, u, g))
                        dve.wait_ge(*due(("seg", l, u, 0, g)))
                        s3 = sc_v[:, u % 2, g, :].rearrange("p (i n) -> p i n", i=3)
                        tt(s3, s3, b[:, 0:P].unsqueeze(1).broadcast_to([P, 3, P]), MUL, ("read", ("cb", l, u, g)))
                    for j in range(2):
                        dve.wait_ge(*due(("made", ("qkp", l, u, j))))
                        b = bank(("qkp", l, u, j))
                        dve.wait_ge(*due(("seg", l, u, 1, j)))
                        tt(sc_v[:, u % 2, 2 + j, :], sc_v[:, u % 2, 2 + j, :], b[:, 0:384], MUL,
                           ("read", ("qkp", l, u, j)), ("scores", l, u))

                def col(c, kind, r0, n, width, step_=1):
                    return cols_v[:, c, kind, r0:r0 + n * step_ - (step_ - 1):step_].unsqueeze(2).broadcast_to(
                        [P, n, width])

                def prep(u):
                    i, d, c = units[u]
                    if u:
                        pi, pd, pc = units[u - 1]
                        if pi < NT - 1:
                            dve.wait_ge(*due(("made", ("cs", l, u - 1))))
                        elif pc >= t0:
                            dve.wait_ge(*due(("made", ("ys", l, u - 1))))
                    x3 = xtok_v[:, c, 0:384].rearrange("p (h c) -> p h c", h=HEADS)
                    xd3 = xdt.rearrange("p (h c) -> p h c", h=HEADS)
                    tt(xd3, x3, col(c, 2, 32 * d, 6, HD), MUL)
                    tt(xde.rearrange("p (h c) -> p h c", h=HEADS), xd3, col(c, 1, 32 * d, 6, HD), MUL)
                    tt(ve_v, va_v[:, c, :, :], col(c, 1, 64 + 32 * d, 6, 65), MUL, ("prep", l, u))

                def combine(u):
                    i, d, c = units[u]
                    if c >= t0:
                        dve.wait_ge(*due(("made", ("ys", l, u))))
                        b = bank(("ys", l, u))
                        y = ys_v[:, c, :]
                        if ("y", c) in written:
                            tt(y, b[:, 0:384], y, ADD, ("read", ("ys", l, u)))
                        else:
                            copy(y, b[:, 0:384], ("read", ("ys", l, u)))
                        written.add(("y", c))
                        if i > 0:
                            dve.wait_ge(*due(("made", ("yi", l, u))))
                            b = bank(("yi", l, u))
                            tt(nds[:, 0:384].rearrange("p (h c) -> p h c", h=HEADS),
                               b[:, 0:384].rearrange("p (h c) -> p h c", h=HEADS), col(c, 0, 32 * d, HEADS, HD), MUL,
                               ("read", ("yi", l, u)))
                            tt(y, y, nds[:, 0:384], ADD)
                            dve.wait_ge(*due(("made", ("mi", l, u))))
                            b = bank(("mi", l, u))
                            tt(nds_v, b[:, 0:390].rearrange("p (h c) -> p h c", h=HEADS),
                               col(c, 0, 64 + 32 * d, HEADS, 65), MUL, ("read", ("mi", l, u)))
                            dve.wait_ge(*due(("made", ("mn", l, u))))
                            b = bank(("mn", l, u))
                            tt(nds, b[:, 0:390], nds, ADD, ("read", ("mn", l, u)))
                        else:
                            dve.wait_ge(*due(("made", ("mn", l, u))))
                            b = bank(("mn", l, u))
                            copy(nds, b[:, 0:390], ("read", ("mn", l, u)))
                        den = small[:, 54:60]
                        stt(den, nds_v[:, :, 64], -1.0, nds_v[:, :, 64], MUL, MAX)
                        tt(den, den, cols_v[:, c, 2, 64 + 32 * d:70 + 32 * d], MAX)
                        step(V.reciprocal(den, den))
                        den3 = den.unsqueeze(2).broadcast_to([P, HEADS, HD])
                        h3 = hs_v[:, c, :].rearrange("p (h c) -> p h c", h=HEADS)
                        if ("h", c) in written:
                            tt(nds_v[:, :, 0:HD], nds_v[:, :, 0:HD], den3, MUL)
                            tt(h3, h3, nds_v[:, :, 0:HD], ADD)
                        else:
                            tt(h3, nds_v[:, :, 0:HD], den3, MUL)
                        written.add(("h", c))
                    if i < NT - 1:
                        dve.wait_ge(*due(("made", ("ss", l, u))))
                        b = bank(("ss", l, u))
                        for g in range(2):
                            r, n = slice(64 * g, 64 * g + 64), slice(192 * g, 192 * g + 192)
                            names = [("read", ("ss", l, u))] if g else []
                            if i == 0:
                                copy(sst_v[r, d, n], b[r, n], *names)
                            else:
                                s3 = sst_v[r, d, n].rearrange("p (h c) -> p h c", h=3)
                                tt(s3, s3, dcb_v[r, c, 32 * d + 3 * g:32 * d + 3 * g + 3].unsqueeze(2).broadcast_to(
                                    [64, 3, HD]), MUL)
                                tt(sst_v[r, d, n], b[r, n], sst_v[r, d, n], ADD, *names)
                        dve.wait_ge(*due(("made", ("cs", l, u))))
                        b4 = bank(("cs", l, u))[:, 0:390].rearrange("p (q j c) -> p q j c", q=3, j=2)
                        for j in range(2):
                            r = slice(64 * j, 64 * j + 64)
                            names = [("read", ("cs", l, u)), ("state", l, u)] if j else []
                            s3 = cst_v[r, d, :, j, :]
                            if i == 0:
                                copy(s3, b4[r, :, j, :], *names)
                            else:
                                r0 = 64 + 32 * d + j
                                tt(s3, s3, dcb_v[r, c, r0:r0 + 5:2].unsqueeze(2).broadcast_to([64, 3, 65]), MUL)
                                tt(s3, b4[r, :, j, :], s3, ADD, *names)

                spread(0)
                spread(1)
                scores(0)
                for u in range(len(units)):
                    if u + 2 < len(units):
                        spread(u + 2)
                    prep(u)
                    if u + 1 < len(units):
                        scores(u + 1)
                    combine(u)
                    if l == 0:
                        for ml, n in MOD_LATER[u * MOD_PER_UNIT:(u + 1) * MOD_PER_UNIT]:
                            if n % 2:
                                mod_columns(ml, n)
                stage_end(l, "units")
                fin = big[:, 512:896]
                for t in range(t0, NT):
                    y, y3 = ys_v[:, t, :], ys_v[:, t, :].rearrange("p (h c) -> p h c", h=HEADS)
                    xd3 = fin.rearrange("p (h c) -> p h c", h=HEADS)
                    tt(xd3, xtok_v[:, t, 0:384].rearrange("p (h c) -> p h c", h=HEADS),
                       ssdd[:, :].unsqueeze(2).broadcast_to([P, HEADS, HD]), MUL)
                    tt(y, y, fin, ADD)
                    tt(y, y, z_v[:, t, :], MUL, ("gated", l, t))
                for t in range(t0, NT):
                    dve.wait_ge(*due(("ssq", l, t)))
                rms(("rinv", l, 3), None, None, MIXW, None)
                dve.wait_ge(*due(("rstd", l, 3)))
                for t in range(t0, NT):
                    ts(ys_v[:, t, :], ys_v[:, t, :], small[:, 4 + t:5 + t], None, MUL, None, ("ssd out", l, t))
                for t in range(t0, NT):
                    h3 = hs_v[:, t, :].rearrange("p (h c) -> p h c", h=HEADS)
                    mu = small[:, 54:60]
                    step(V.tensor_reduce(mu, h3, AX.X, ADD))
                    ts(mu, mu, 1.0 / HD, None, MUL, None)
                    tt(h3, h3, mu.unsqueeze(2).broadcast_to([P, HEADS, HD]), SUB)
                    tt(fin, hs_v[:, t, :], hs_v[:, t, :], MUL)
                    step(V.tensor_reduce(small[:, 12 + 6 * t:18 + 6 * t], fin.rearrange("p (h c) -> p h c", h=HEADS),
                                         AX.X, ADD))
                if t0:
                    step(V.memset(small[:, 12:24], 1.0))
                ts(small[:, 12:36], small[:, 12:36], 1.0 / HD, EPS, MUL, ADD)
                step(V.reciprocal(small[:, 12:36], small[:, 12:36]), ("rinv", l, 4))
                dve.wait_ge(*due(("rstd", l, 4)))
                for t in range(t0, NT):
                    h3 = hs_v[:, t, :].rearrange("p (h c) -> p h c", h=HEADS)
                    tt(h3, h3, small[:, 12 + 6 * t:18 + 6 * t].unsqueeze(2).broadcast_to([P, HEADS, HD]), MUL)
                    tt(hs_v[:, t, :], hs_v[:, t, :], o_v[:, t, :], MUL, ("ml out", l, t))
                stage_end(l, "final")
                step(V.memset(small[:, 60:61], 0.0), ("hy z", l, 0))
                n = 512 - n0
                ns = len(streams)
                for o in range(2):
                    hc = hf_v[:, 0, o * L:(o + 1) * L]

                    def filt(k):
                        return hf_v[:, k, o * L:(o + 1) * L].unsqueeze(1).broadcast_to([P, ns, L])

                    def spec(ap):
                        return ap.rearrange("p (s n) -> p s n", n=L)

                    for fb in range(2):
                        dve.wait_ge(*due(("made", ("zf", l, o, 2 * fb))))
                        dve.wait_ge(*due(("made", ("zf", l, o, 2 * fb + 1))))
                        zr, zi = bank(("zf", l, o, 2 * fb)), bank(("zf", l, o, 2 * fb + 1))
                        zr, zi = spec(zr[:, n0:512]), spec(zi[:, n0:512])
                        a, c_ = spec(ht1[:, n0:512]), spec(ht2[:, n0:512])
                        yr, yi = spec(yf_v[:, fb, n0:512]), spec(yf_v[:, 2 + fb, n0:512])
                        tt(yr, zr, filt(fb), MUL)
                        tt(a, zi, filt(2 + fb), MUL)
                        tt(yr, yr, a, SUB)
                        tt(a, zr, filt(2 + fb), MUL, ("read", ("zf", l, o, 2 * fb)))
                        tt(c_, zi, filt(4 if fb == 0 else 1), MUL, ("read", ("zf", l, o, 2 * fb + 1)))
                        tt(yi, a, c_, ADD, *([("yf", l, o)] if fb == 1 else []))
                    for c in range(2):
                        dve.wait_ge(*due(("made", ("yt", l, o, c))))
                        b = bank(("yt", l, o, c))
                        z = hy_v[:, c, n0:512]
                        ts(ht1[:, n0:512], b[:, n0:512], small[:, 44 + 2 * o + c:45 + 2 * o + c], None, MUL, None,
                           ("read", ("yt", l, o, c)))
                        stt(ht1[:, n0:512], z, pcol[:, 74 + 2 * o + c:75 + 2 * o + c], ht1[:, n0:512], MUL, ADD)
                        dst = z if o == 0 else yT_v[:, 3 + c, n0:512]
                        a, g_ = ht1[:, n0:512], hy_v[:, 2 + 2 * o + c, n0:512]
                        if o == 1 and l % 2:
                            dst = dst.rearrange("p (r w) -> p w r", r=ROWS)
                            a, g_ = (q.rearrange("p (w r) -> p w r", r=ROWS) for q in (a, g_))
                        tt(dst, a, g_, MUL, ("hy z", l, o + 1))
                stage_end(l, "hyena")

                def gate_diagonals(n):
                    for s in streams:
                        if s != streams[0]:
                            for q in range(2):
                                dve.wait_ge(*due(("made", ("grow", l, n, s - 1, q))))
                        tt(hsum[:, 0:1024].rearrange("p (k j) -> p k j", k=KB),
                           ident[:, :].unsqueeze(1).broadcast_to([P, KB, P]),
                           modc_v[:, l, 3 * n + 2, :, 1 - s:2 - s].broadcast_to([P, KB, P]), MUL, ("gdiag", l, n, s))

                gate_diagonals(0)
                for t in range(t0, NT):
                    for half in range(2):
                        cs_ = slice(512 * half, 512 * half + 512)
                        dve.wait_ge(*due(("made", ("out", l, t, half))))
                        b = bank(("out", l, t, half))
                        dve.wait_ge(*due(("grow in", l, 0, t // 2)))
                        tt(ysum[:, 0:512], b[:, :], grow_v[:, t // 2, cs_], MUL, ("read", ("out", l, t, half)))
                        tt(x_v[:, t, cs_], x_v[:, t, cs_], ysum[:, 0:512], ADD)
                stage_end(l, "outproj")
                modulators(1)
                norm(2, t0)
                for k in range(KB):
                    dve.wait_ge(*due(("made", ("h2", l, k, 1))))
                    b = bank(("h2", l, k, 1))
                    ts(hT_v[:, k, L:2 * L], b[:, 0:L], ab_v[:, 2, k, 0:1], ab_v[:, 3, k, 0:1], MUL, ADD,
                       ("read", ("h2", l, k, 1)), ("h2T", l, "dve"))
                R = ysum[:, 0:144].rearrange("p (t n) -> p t n", t=NT)
                dve.wait_ge(*due(("made", ("router", l))))
                b = bank(("router", l))
                tt(R[:, t0:, :], b[:, t0 * 36:144].rearrange("p (t n) -> p t n", n=36),
                   rb[:, :].unsqueeze(1).broadcast_to([P, NT - t0, 36]), ADD, ("read", ("router", l)))
                if t0:
                    step(V.memset(ysum[:, 0:72], 0.0))
                scr = ysum[:, 256:1024]

                def pick(vals, n, mx, mask, w):
                    step(V.tensor_reduce(mx, vals, AX.X, MAX))
                    im = iom[:, 0:n].unsqueeze(1).broadcast_to([P, NT, n])
                    tt(mask, vals, mx.unsqueeze(2).broadcast_to([P, NT, n]), ALU.is_equal)
                    tt(mask, mask, im, MUL)
                    step(V.tensor_reduce(w, mask, AX.X, MIN))
                    tt(mask, im, w.unsqueeze(2).broadcast_to([P, NT, n]), ALU.is_equal)

                def area(a, n):
                    return scr[:, a:a + NT * n].rearrange("p (t n) -> p t n", t=NT)

                gmax, gsum, tmp4 = small[:, 54:58], small[:, 60:64], ysum[:, 1024:1028]
                gmask = area(0, 4)
                pick(R[:, :, 0:4], 4, gmax, gmask, tmp4)
                ge = otok[:, 0:16].rearrange("p (t n) -> p t n", t=NT)
                tt(ge, R[:, :, 0:4], gmax.unsqueeze(2).broadcast_to([P, NT, 4]), SUB, ("r1", l))
                E = area(16, 32)
                pen = area(144, 4)
                ts(pen, gmask, -NEG, NEG, MUL, ADD)
                for t in range(NT):
                    e4 = E[:, t, :].rearrange("p (g e) -> p g e", g=N_GROUPS)
                    tt(e4, R[:, t, 4:36].rearrange("p (g e) -> p g e", g=N_GROUPS),
                       gmask[:, t, :].unsqueeze(2).broadcast_to([P, N_GROUPS, PER_GROUP]), MUL)
                    tt(e4, e4, pen[:, t, :].unsqueeze(2).broadcast_to([P, N_GROUPS, PER_GROUP]), ADD)
                m1, m2 = ysum[:, 1032:1036], ysum[:, 1036:1040]
                k1, k2 = area(160, 32), area(288, 32)
                pick(E, 32, m1, k1, tmp4)
                stt(E, k1, 2 * NEG, E, MUL, ADD)
                pick(E, 32, m2, k2, tmp4)
                dve.wait_ge(*due(("r2", l)))
                tt(otok[:, 16:20], m2, m1, SUB, ("r3", l))
                step(V.tensor_reduce(gsum, ge, AX.X, ADD))
                dve.wait_ge(*due(("r4", l)))
                chosen = chosen_v[:, t0:, :]
                tt(chosen, k1[:, t0:, :], k2[:, t0:, :], ADD, ("chosen", l))
                den = ysum[:, 1040:1044]
                ts(den, otok[:, 16:20], 1.0, None, ADD, None)
                tt(den, den, gsum, MUL)
                step(V.reciprocal(den, den))
                tt(m2, den, otok[:, 16:20], MUL)
                nt = NT - t0
                taken = [0]

                def room(n):
                    taken[0] += n
                    return ktok[:, taken[0] - n:taken[0]]

                def tiles(n):
                    return room(nt * n).rearrange("p (t n) -> p t n", t=nt)

                rank, blk, item, tmp = tiles(32), tiles(32), tiles(32), tiles(32)
                count, more, upto, first_of = room(32), room(32), room(32), room(32)
                slot_of, item_of = room(8), room(8)
                dve.wait_ge(*due(("made", ("rank", l))))
                dve.wait_ge(*due((f"route{l}_in",)))
                b = bank(("rank", l))
                copy(rank, b[:, 32 * t0:P].rearrange("p (t n) -> p t n", n=32))
                copy(count, b[:, P:P + 32], ("read", ("rank", l)))
                ts(more, count, float(P), None, ALU.is_gt, None)
                stt(more, count, 2.0 * P, more, ALU.is_gt, ADD)
                stt(more, count, 3.0 * P, more, ALU.is_gt, ADD)
                step(V.tensor_tensor_scan(upto, ones[:, 0:32], more, 0.0, MUL, ADD))
                tt(first_of, upto, more, SUB)
                step(V.tensor_tensor(tmp[:, 0, :], first_of, items[:, 0:32], SUB))
                ts(tmp[:, 0, :], tmp[:, 0, :], EXPERTS - 1.0, None, ADD, None)
                ts(blk, rank, float(P), None, ALU.is_ge, None)
                stt(blk, rank, 2.0 * P, blk, ALU.is_ge, ADD)
                stt(blk, rank, 3.0 * P, blk, ALU.is_ge, ADD)
                stt(rank, blk, -1.0 * P, rank, MUL, ADD)
                tt(item, blk, tmp[:, 0:1, :].broadcast_to([P, nt, 32]), ADD)
                ts(blk, blk, 0.5, None, ALU.is_gt, None)
                tt(item, item, blk, MUL)
                tt(item, item, items[:, 0:32].unsqueeze(1).broadcast_to([P, nt, 32]), ADD)
                for y, (mask, share) in enumerate(((k1, den), (k2, m2))):
                    for val, to in ((rank, slot_of), (item, item_of)):
                        tt(tmp, val, mask[:, t0:, :], MUL)
                        step(V.tensor_reduce(to[:, y * 4 + t0:y * 4 + 4], tmp, AX.X, ADD))
                    for t in range(t0, NT):
                        n = y * NT + t
                        ts(slot_hot[:, n, :], iota, slot_of[:, n:n + 1], None, ALU.is_equal, None)
                        for v, value in enumerate((share[:, t:t + 1], pair_no[:, t:t + 1], pair_no[:, n:n + 1])):
                            ts(item_hot[:, n, v, :], items, item_of[:, n:n + 1], value, ALU.is_equal, MUL,
                               *([("one-hot", l, n)] if v == 2 else []))
                each = room(MORE_ITEMS * 32).rearrange("p (j e) -> p j e", j=MORE_ITEMS)
                also = room(MORE_ITEMS * 32).rearrange("p (j e) -> p j e", j=MORE_ITEMS)
                numbers = iota[:, 0:MORE_ITEMS].unsqueeze(2).broadcast_to([P, MORE_ITEMS, 32])

                def over(a):
                    return a.unsqueeze(1).broadcast_to([P, MORE_ITEMS, 32])
                tt(each, numbers, over(first_of), ALU.is_ge)
                tt(also, numbers, over(upto), ALU.is_lt)
                tt(each, each, also, MUL)
                tt(each, each, over(items[:, 0:32]), MUL)
                step(V.tensor_reduce(slot_of, each, AX.X, ADD))
                copy(more_expert, slot_of)
                copy(more_flag, upto[:, 31:32])
                dve.wait_ge(*due(("made", ("tables", l))))
                b = bank(("tables", l))
                step(V.memset(weight_of, 0.0))
                copy(weight_of[:, 0:ITEMS], b[:, 0:ITEMS])
                which = room(44)
                for v, table in ((1, token_of), (2, pair_of)):
                    step(V.memset(which, NOWHERE))
                    ts(which[:, 0:ITEMS], b[:, v * ITEMS:(v + 1) * ITEMS], 0.5, NOWHERE, ALU.is_lt, MUL)
                    stt(which[:, 0:ITEMS], b[:, v * ITEMS:(v + 1) * ITEMS], -1.0, which[:, 0:ITEMS], ADD, ADD)
                    copy(table, which, ("item tables", l), *([("read", ("tables", l))] if v == 2 else []))
                gate_diagonals(1)
                stage_end(l, "router")
                tag = ("moe", l)
                before = dict(tally.count)
                with dve.Fori(0, BODIES) as i:
                    tally.turn = (tag, i)
                    for n, (what, j, *half) in enumerate(TURN):
                        name = ("turn", l, n)
                        if half == [1]:
                            continue
                        if what == "gathered":
                            if j >= 2:
                                dve.wait_ge(*due(("made", ("turn", l, TURN.index(("gate up", j - 2))))))
                            else:
                                dve.wait_ge(*due(("made", ("turn", l, TURN.index(("gate up", j + 2)))), 1))
                            dve.wait_ge(*due(("made", name)))
                            copy(rowsT_v[:, j % 2, 0:4, :], bank(name)[:, :].rearrange("p (k n) -> p k n", k=4),
                                 ("read", name), ("rowsT", l, j, 0))
                        elif what == "gate up":
                            if j >= 2:
                                dve.wait_ge(*due(("made", ("turn", l, TURN.index(("hidden", j - 2))))))
                            else:
                                dve.wait_ge(*due(("made", ("turn", l, TURN.index(("hidden", j + 2)))), 1))
                            dve.wait_ge(*due(("made", name)))
                            dve.wait_ge(*due(("sg", l, j)))
                            tt(hid_v[:, j % 2, :], sg_v[:, j % 2, :], bank(name)[:, EH:2 * EH], MUL,
                               ("read", name), ("hid", l, j))
                        elif what == "hidden":
                            if j >= 2:
                                dve.wait_ge(*due(("made", ("turn", l, TURN.index(("down", j - 2, 1))))))
                            else:
                                dve.wait_ge(*due(("made", ("turn", l, TURN.index(("down", j + 2, 1)))), 1))
                            dve.wait_ge(*due(("made", name)))
                            copy(hidT_v[:, j % 2, :], bank(name)[:, 0:EH], ("read", name), ("hidT", l, j))
                        else:
                            if j >= 2:
                                dve.wait_ge(*due(("scattered", l, j - 2)))
                            else:
                                dve.wait_ge(*due(("scattered", l, j + 2), 1))
                            dve.wait_ge(*due(("made", name)))
                            ts(res_v[:, j % 2, 0:512], bank(name)[:, :], weight_of[:, bass.ds(i * PER_BODY + j, 1)],
                               None, MUL, None, ("read", name), ("result", l, j, "dve"))
                tally.looped(tag, before, BODIES)
                stage_end(l, "moe")
                with dve.If(dve.value_load(more_flag[0:1, :], min_val=0, max_val=MORE_ITEMS) != 0):
                    with dve.Fori(0, MORE_ITEMS) as i:
                        dve.wait_ge(more_pe[l], i * MORE_PRODUCTS + 2)
                        V.tensor_copy(rowsT_v[:, 0, 0:4, :], banks[0][:, :].rearrange("p (k n) -> p k n", k=4)).then_inc(more_dve[l], 1)
                        V.tensor_copy(rowsT_v[:, 0, 4:8, :], banks[1][:, :].rearrange("p (k n) -> p k n", k=4)).then_inc(more_dve[l], 1)
                        dve.wait_ge(more_act[l], i + 1)
                        V.tensor_tensor(hid_v[:, 0, :], sg_v[:, 0, :], banks[2][:, EH:2 * EH], MUL).then_inc(more_dve[l], 1)
                        dve.wait_ge(more_pe[l], i * MORE_PRODUCTS + 4)
                        V.tensor_copy(hidT_v[:, 0, :], banks[3][:, 0:EH]).then_inc(more_dve[l], 1)
                        dve.wait_ge(more_pe[l], i * MORE_PRODUCTS + 5)
                        for half in range(2):
                            V.tensor_scalar(res_v[:, 0, 512 * half:512 * half + 512], banks[4 + half][:, :],
                                            weight_of[:, bass.ds(i + EXPERTS, 1)], None, MUL).then_inc(more_dve[l], 1)
                    dve.wait_ge(more_dve[l], MORE_ITEMS * MORE_DVE)
                for t in range(t0, NT):
                    two = two_v[t - t0]
                    dve.wait_ge(*due(("pairs", l, t)))
                    tt(two[:, 0, :], two[:, 0, :], two[:, 1, :], ADD)
                    tt(two[:, 0, :], two[:, 0, :], grow_v[:, t // 2, :], MUL)
                    tt(x_v[:, t, :], x_v[:, t, :], two[:, 0, :], ADD, ("x done", l), ("x updated", l, t))
            for t in range(2, NT):
                dve.wait_ge(*due(("ss", "f", t)))
            rms(("rinv", "f"), None, None, D, None)
            dve.wait_ge(*due(("rstd", "f")))
            dve.wait_ge(*due(("norm_in",)))
            for t in range(2):
                stt(xn_v[:, t, :], x_v[:, 2 + t, :], small[:, 6 + t:7 + t], grow[:, 0:D], MUL, MUL, ("result", t))


def constants():
    f4 = np.float32
    p, t = np.arange(P), np.arange(L)
    s_gt_l = p[:, None] > p[None, :]
    mask = np.stack([np.where(s_gt_l, NEG, 0.0), np.where(s_gt_l.T, NEG, 0.0)], 1)
    sel = np.zeros((P, 2, 3, P), f4)
    for r in range(P):
        for j in range(2):
            for i in range(3):
                if r % 32 == (3 * j + i if r < 64 else 2 * i + j):
                    sel[r, j, i] = 1.0
    keep = np.ones((P, 4, P), f4)
    keep[(p // 32) % 2 == 0, :, 0] = 0.0
    keep[(p // 32) % 2 == 1, :, P - 1] = 0.0
    ang = 2 * np.pi * ((t[:, None] * t[None, :]) % (2 * L)) / (2 * L)
    cos, sin = np.cos(ang), -np.sin(ang)
    nyq = (-1.0) ** t
    cn, sn = cos.copy(), sin.copy()
    cn[:, 0], sn[:, 0] = nyq, nyq
    tp = lambda m: m.reshape(2, P, -1).transpose(1, 0, 2)
    dftn = np.stack([tp(cn[:, :P]), tp(sn[:, :P])], 1)
    scale = np.where(t == 0, 1.0, 2.0) / (2 * L)
    ic, is_ = cos * scale[:, None], sin * scale[:, None]
    is_[0] = nyq / (2 * L)
    tf = t.astype(f4)
    tu = tf / f4(L - 1)
    bands = np.linspace(1e-4, 15, 16).astype(f4)
    fa = (f4(2 * np.pi / L) * tf[:, None] * bands[None, :]).astype(f4)
    feats = np.concatenate([tu[:, None], np.cos(fa), -np.sin(fa)], -1).T
    tcol = np.zeros((P, 4), f4)
    tcol[:, 0], tcol[:, 1] = -tu[:P], -tu[P:]
    tcol[:, 2] = p != 0
    tcol[:, 3] = np.where(p < 64, 1.0, -1.0)
    c = dict(ident=np.eye(P), mask=mask, sel=sel, keep=keep, dftc=tp(cos), dfts=tp(sin), dftn=dftn,
             invc=tp(ic), invs=tp(is_), feats=feats, tcol=tcol,
             tri=p[:, None] < p[None, :], iota=np.tile(p, (P, 1)), items=np.tile(np.arange(ITEMS), (P, 1)),
             pair_no=p[:, None] + 1 + P * np.arange(2 * NT)[None, :], iom=np.tile(np.arange(EXPERTS) - 99.0, (P, 1)))
    c = {k: np.ascontiguousarray(a.reshape(a.shape[0], -1).astype(f4)) for k, a in c.items()}
    return c


_INS = ['x', 'c', 'ctx', 'c_ctx', 'w_mod', 'b_mod', 'norm1_w', 'norm2_w', 'w_in', 'w_out', 'ssd_conv_w',
        'ssd_conv_b', 'ssd_dt_bias', 'ssd_a_log', 'ssd_d', 'ssd_norm_w', 'hy_conv_w', 'hy_conv_b', 'hy_pos_w1',
        'hy_pos_b1', 'hy_pos_w2', 'hy_pos_b2', 'hy_pos_w3', 'hy_freq', 'hy_decay', 'hy_skip', 'ml_conv_w',
        'ml_conv_b', 'ml_gate_b', 'ml_norm_w', 'grp_router_w', 'grp_router_b', 'exp_router_w', 'exp_router_b',
        'moe_w_gate', 'moe_w_up', 'moe_w_down', 'final_norm_w']


def kernel(**inputs):
    import concourse.bacc as _bacc
    from concourse.bass_utils import run_bass_kernel_spmd as _run

    arrays = {n: np.ascontiguousarray(inputs[n]) for n in _INS}
    arrays.update({"const_" + k: a for k, a in constants().items()})
    at = {}
    for first in (True, False):
        nc = _bacc.Bacc("TRN2", target_bir_lowering=False, num_devices=1)
        args = {n: nc.dram_tensor(f"in_{n}", a.shape, mybir.dt.from_np(a.dtype), kind="ExternalInput").ap()
                for n, a in arrays.items()}
        res = nc.dram_tensor("out_0", (1, L, D), F32, kind="ExternalOutput").ap()
        build(nc, args, res, at, first)
    r = _run(nc, [{f"in_{n}": a for n, a in arrays.items()}], core_ids=[0])
    return r.results[0]["out_0"]
```
